# Optimizing a Trainium2 kernel written in Bass

```python
import math
import jax, jax.numpy as jnp
from jax import lax
import numpy as np

D_MODEL = 1024
BATCH = 1
SEQ = 256
DEPTH = 2

CHUNK = 64
HEAD_DIM = 64
N_MIX_HEADS = D_MODEL // HEAD_DIM
MEM_HEADS = 4
SELF_HEADS = N_MIX_HEADS - MEM_HEADS
SWA_KV_HEADS = 3
SWA_GROUP = SELF_HEADS // SWA_KV_HEADS
WINDOW = 128
WINDOW_CHUNKS = WINDOW // CHUNK
ROT_DIM = HEAD_DIM // 4
ROT_HALF = ROT_DIM // 2
ROPE_THETA = 500000.0
FOX_BLOCK = 128
MEM_LEN = 256
D_FF = ((8 * D_MODEL // 3 + 127) // 128) * 128
N_EXPERTS = 8
TOP_K = 2
EXPERT_BLOCK = 128
LN_EPS = 1e-5
NEG = -1e30
ATTN_SCALE = HEAD_DIM ** -0.5
DN_ALPHA = (2.0 * DEPTH) ** 0.25
DN_BETA = (8.0 * DEPTH) ** -0.25
N_SWA_LAYERS = (DEPTH + 1) // 2
N_FOX_LAYERS = DEPTH // 2
SWA_IN = (SELF_HEADS + 2 * SWA_KV_HEADS + MEM_HEADS) * HEAD_DIM
FOX_IN = (3 * SELF_HEADS + MEM_HEADS) * HEAD_DIM + SELF_HEADS


def layer_norm(x, g, b):
    xf = x.astype(jnp.float32)
    mu = jnp.mean(xf, axis=-1, keepdims=True)
    var = jnp.mean(jnp.square(xf - mu), axis=-1, keepdims=True)
    return ((xf - mu) * lax.rsqrt(var + LN_EPS) * g + b).astype(x.dtype)

def rope_tables(positions):
    inv_freq = ROPE_THETA ** (-jnp.arange(0, ROT_DIM, 2, dtype=jnp.float32) / ROT_DIM)
    ang = positions.astype(jnp.float32)[..., None] * inv_freq
    return jnp.cos(ang)[:, :, None, :], jnp.sin(ang)[:, :, None, :]

def partial_rope(t, cos, sin):
    r = t[..., :ROT_DIM].astype(jnp.float32)
    r1, r2 = r[..., :ROT_HALF], r[..., ROT_HALF:]
    rot = jnp.concatenate([r1 * cos - r2 * sin, r2 * cos + r1 * sin], axis=-1)
    return jnp.concatenate([rot.astype(t.dtype), t[..., ROT_DIM:]], axis=-1)

def swa_sink_attention(q, k, v, sinks):
    B, S = q.shape[0], q.shape[1]
    n_c = S // CHUNK
    pad = WINDOW_CHUNKS * CHUNK
    n_keys = (WINDOW_CHUNKS + 1) * CHUNK
    qb = q.reshape(B, n_c, CHUNK, SWA_KV_HEADS, SWA_GROUP, HEAD_DIM)

    def band(t):
        tp = jnp.pad(t, ((0, 0), (pad, 0), (0, 0), (0, 0)))
        tp = tp.reshape(B, n_c + WINDOW_CHUNKS, CHUNK, SWA_KV_HEADS, HEAD_DIM)
        return jnp.concatenate([tp[:, m:m + n_c] for m in range(WINDOW_CHUNKS + 1)], axis=2)

    kb, vb = band(k), band(v)
    s = jnp.einsum('bnqhgd,bnkhd->bnhgqk', qb, kb).astype(jnp.float32) * ATTN_SCALE
    key_chunk = jnp.arange(n_c)[:, None] - WINDOW_CHUNKS + (jnp.arange(n_keys) // CHUNK)[None, :]
    valid = key_chunk >= 0
    s = jnp.where(valid[None, :, None, None, None, :], s, NEG)
    sk = sinks.astype(jnp.float32).reshape(SWA_KV_HEADS, SWA_GROUP)[None, None, :, :, None]
    m = jnp.maximum(jnp.max(s, axis=-1), sk)
    p = jnp.exp(s - m[..., None])
    den = jnp.sum(p, axis=-1) + jnp.exp(sk - m)
    probs = (p / den[..., None]).astype(v.dtype)
    o = jnp.einsum('bnhgqk,bnkhd->bnqhgd', probs, vb)
    return o.reshape(B, S, SELF_HEADS * HEAD_DIM)

def forgetting_attention(q, k, v, log_f):
    B, S = q.shape[0], q.shape[1]
    cum = jnp.cumsum(log_f, axis=1).transpose(0, 2, 1)
    outs = []
    for i in range(S // FOX_BLOCK):
        lo, hi = i * FOX_BLOCK, (i + 1) * FOX_BLOCK
        s = jnp.einsum('bqhd,bkhd->bhqk', q[:, lo:hi], k[:, :hi]).astype(jnp.float32) * ATTN_SCALE
        bias = cum[:, :, lo:hi, None] - cum[:, :, None, :hi]
        causal = jnp.arange(lo, hi)[:, None] >= jnp.arange(hi)[None, :]
        s = jnp.where(causal, s + bias, NEG)
        p = jax.nn.softmax(s, axis=-1).astype(v.dtype)
        outs.append(jnp.einsum('bhqk,bkhd->bqhd', p, v[:, :hi]))
    return jnp.concatenate(outs, axis=1).reshape(B, S, SELF_HEADS * HEAD_DIM)

def memory_attention(qc, km, vm):
    B, S = qc.shape[0], qc.shape[1]
    s = jnp.einsum('bshd,bmhd->bhsm', qc, km).astype(jnp.float32) * ATTN_SCALE
    p = jax.nn.softmax(s, axis=-1).astype(vm.dtype)
    return jnp.einsum('bhsm,bmhd->bshd', p, vm).reshape(B, S, MEM_HEADS * HEAD_DIM)

def swiglu(x, w_in, w_out):
    h = x @ w_in
    a, b = h[..., :D_FF], h[..., D_FF:]
    return (jax.nn.silu(a) * b) @ w_out

def moe_swiglu(x, w_router, b_router, w_in, w_out):
    shp = x.shape
    x2 = x.reshape(-1, shp[-1])
    n_tok = x2.shape[0]
    logits = (x2 @ w_router).astype(jnp.float32) + b_router.astype(jnp.float32)
    top_vals, top_idx = lax.top_k(logits, TOP_K)
    gates = jax.nn.softmax(top_vals, axis=-1)
    n_asg = n_tok * TOP_K
    e_flat = top_idx.reshape(-1)
    t_flat = jnp.repeat(jnp.arange(n_tok, dtype=jnp.int32), TOP_K)
    g_flat = gates.reshape(-1)
    order = jnp.argsort(e_flat)
    se, st, sg = e_flat[order], t_flat[order], g_flat[order]
    counts = jnp.bincount(e_flat, length=N_EXPERTS)
    starts = jnp.cumsum(counts) - counts
    pcounts = (counts + EXPERT_BLOCK - 1) // EXPERT_BLOCK * EXPERT_BLOCK
    pends = jnp.cumsum(pcounts)
    pstarts = pends - pcounts
    dest = pstarts[se] + (jnp.arange(n_asg) - starts[se])
    n_blocks = -(-n_asg // EXPERT_BLOCK) + N_EXPERTS
    n_slots = n_blocks * EXPERT_BLOCK
    slot_tok = jnp.zeros((n_slots,), jnp.int32).at[dest].set(st)
    slot_gate = jnp.zeros((n_slots,), x2.dtype).at[dest].set(sg.astype(x2.dtype))
    block_exp = jnp.minimum(
        jnp.searchsorted(pends, jnp.arange(n_blocks) * EXPERT_BLOCK, side='right'), N_EXPERTS - 1)
    xs = x2[slot_tok].reshape(n_blocks, EXPERT_BLOCK, shp[-1])

    def expert_block(args):
        xb, e = args
        h = xb @ w_in[e]
        return (jax.nn.silu(h[:, :D_FF]) * h[:, D_FF:]) @ w_out[e]

    ys = lax.map(expert_block, (xs, block_exp)).reshape(n_slots, shp[-1])
    y = jnp.zeros_like(x2).at[slot_tok].add((ys * slot_gate[:, None]).astype(x2.dtype))
    return y.reshape(shp)

def first_inputs(seed: int = 0) -> dict:
    key = jax.random.key(seed)
    ks = jax.random.split(key, 20)
    nrm = jax.random.normal
    f32 = jnp.float32
    x = nrm(ks[0], (BATCH, SEQ, D_MODEL), f32)
    mem = nrm(ks[1], (BATCH, MEM_LEN, D_MODEL), f32)
    offset = jax.random.randint(ks[2], (BATCH, 1), 0, 1 << 16, dtype=jnp.int32)
    positions = offset + jnp.arange(SEQ, dtype=jnp.int32)[None, :]
    sd = D_MODEL ** -0.5
    sf = D_FF ** -0.5
    return {
        "x": x,
        "mem": mem,
        "positions": positions,
        "w_in_swa": nrm(ks[3], (N_SWA_LAYERS, D_MODEL, SWA_IN), f32) * sd,
        "attn_sinks": nrm(ks[4], (N_SWA_LAYERS, SELF_HEADS), f32) * 0.5,
        "w_in_fox": nrm(ks[5], (N_FOX_LAYERS, D_MODEL, FOX_IN), f32) * sd,
        "b_forget": jax.random.uniform(ks[6], (N_FOX_LAYERS, SELF_HEADS), f32, 1.0, 4.0),
        "w_mem_kv": nrm(ks[7], (DEPTH, D_MODEL, 2 * MEM_HEADS * HEAD_DIM), f32) * sd,
        "w_out": nrm(ks[8], (DEPTH, D_MODEL, D_MODEL), f32) * sd * DN_BETA,
        "ln_attn_g": 1.0 + 0.02 * nrm(ks[9], (DEPTH, D_MODEL), f32),
        "ln_attn_b": 0.02 * nrm(ks[10], (DEPTH, D_MODEL), f32),
        "w_ffn_in": nrm(ks[11], (N_SWA_LAYERS, D_MODEL, 2 * D_FF), f32) * sd,
        "w_ffn_out": nrm(ks[12], (N_SWA_LAYERS, D_FF, D_MODEL), f32) * sf * DN_BETA,
        "w_router": nrm(ks[13], (N_FOX_LAYERS, D_MODEL, N_EXPERTS), f32) * sd,
        "b_router": 0.01 * nrm(ks[14], (N_FOX_LAYERS, N_EXPERTS), f32),
        "w_exp_in": nrm(ks[15], (N_FOX_LAYERS, N_EXPERTS, D_MODEL, 2 * D_FF), f32) * sd,
        "w_exp_out": nrm(ks[16], (N_FOX_LAYERS, N_EXPERTS, D_FF, D_MODEL), f32) * sf * DN_BETA,
        "ln_ffn_g": 1.0 + 0.02 * nrm(ks[17], (DEPTH, D_MODEL), f32),
        "ln_ffn_b": 0.02 * nrm(ks[18], (DEPTH, D_MODEL), f32),
    }

def first_block(x, mem, positions, w_in_swa, attn_sinks, w_in_fox, b_forget, w_mem_kv, w_out,
              ln_attn_g, ln_attn_b, w_ffn_in, w_ffn_out, w_router, b_router, w_exp_in,
              w_exp_out, ln_ffn_g, ln_ffn_b):
    B, S = x.shape[0], x.shape[1]
    cos, sin = rope_tables(positions)
    hq = SELF_HEADS * HEAD_DIM
    hkv = SWA_KV_HEADS * HEAD_DIM
    hm = MEM_HEADS * HEAD_DIM
    for i in range(DEPTH):
        j = i // 2
        kvm = mem @ w_mem_kv[i]
        km = kvm[..., :hm].reshape(B, MEM_LEN, MEM_HEADS, HEAD_DIM)
        vm = kvm[..., hm:].reshape(B, MEM_LEN, MEM_HEADS, HEAD_DIM)
        if i % 2 == 0:
            proj = x @ w_in_swa[j]
            q = proj[..., :hq].reshape(B, S, SELF_HEADS, HEAD_DIM)
            k = proj[..., hq:hq + hkv].reshape(B, S, SWA_KV_HEADS, HEAD_DIM)
            v = proj[..., hq + hkv:hq + 2 * hkv].reshape(B, S, SWA_KV_HEADS, HEAD_DIM)
            qc = proj[..., hq + 2 * hkv:].reshape(B, S, MEM_HEADS, HEAD_DIM)
            q, k = partial_rope(q, cos, sin), partial_rope(k, cos, sin)
            self_out = swa_sink_attention(q, k, v, attn_sinks[j])
        else:
            proj = x @ w_in_fox[j]
            q = proj[..., :hq].reshape(B, S, SELF_HEADS, HEAD_DIM)
            k = proj[..., hq:2 * hq].reshape(B, S, SELF_HEADS, HEAD_DIM)
            v = proj[..., 2 * hq:3 * hq].reshape(B, S, SELF_HEADS, HEAD_DIM)
            qc = proj[..., 3 * hq:3 * hq + hm].reshape(B, S, MEM_HEADS, HEAD_DIM)
            f_logit = proj[..., 3 * hq + hm:].astype(jnp.float32) + b_forget[j].astype(jnp.float32)
            log_f = jax.nn.log_sigmoid(f_logit)
            self_out = forgetting_attention(q, k, v, log_f)
        cross_out = memory_attention(qc, km, vm)
        mix = jnp.concatenate([self_out, cross_out], axis=-1) @ w_out[i]
        x = layer_norm(DN_ALPHA * x + mix, ln_attn_g[i], ln_attn_b[i])
        if i % 2 == 0:
            ffn = swiglu(x, w_ffn_in[j], w_ffn_out[j])
        else:
            ffn = moe_swiglu(x, w_router[j], b_router[j], w_exp_in[j], w_exp_out[j])
        x = layer_norm(DN_ALPHA * x + ffn, ln_ffn_g[i], ln_ffn_b[i])
    return x


N_META = 16
ROPE_THETA_2 = 10000.0
EPS = 1e-6
A_HEADS = 4
A_DK = 128
A_DV = 128
A_CONV = 4
B_HEADS = 4
B_DH = 128
IDX_HEADS = 8
IDX_DIM = 64
TOPK_MAX = 256
TOPK_DIV = 4
Q_BLOCK = 64
D_FF_2 = 2816
FFN_CONV = 3

A_WIDTH = A_HEADS * A_DV
B_WIDTH = B_HEADS * B_DH
IN_SPLITS = (A_HEADS * A_DK, A_HEADS * A_DK, A_WIDTH, A_WIDTH, A_HEADS, A_HEADS,
             B_WIDTH, B_DH, B_DH, IDX_HEADS * IDX_DIM, IDX_DIM, IDX_HEADS)
IN_COLS = sum(IN_SPLITS)
SPLIT_POINTS = tuple(int(c) for c in np.cumsum(IN_SPLITS)[:-1])


def rms_norm(x, g):
    xf = x.astype(jnp.float32)
    y = xf * lax.rsqrt(jnp.mean(xf * xf, axis=-1, keepdims=True) + EPS)
    return (y * g.astype(jnp.float32)).astype(x.dtype)

def l2_norm(x):
    xf = x.astype(jnp.float32)
    return xf * lax.rsqrt(jnp.sum(xf * xf, axis=-1, keepdims=True) + EPS)

def rope_tables_2(T, dim):
    inv_freq = 1.0 / (ROPE_THETA_2 ** (jnp.arange(0, dim, 2, dtype=jnp.float32) / dim))
    ang = jnp.arange(T, dtype=jnp.float32)[:, None] * inv_freq[None, :]
    return jnp.cos(ang), jnp.sin(ang)

def apply_rope(x, cos, sin):
    xf = x.astype(jnp.float32)
    x1, x2 = jnp.split(xf, 2, axis=-1)
    c, s = cos[:, None, :], sin[:, None, :]
    return jnp.concatenate([x1 * c - x2 * s, x2 * c + x1 * s], axis=-1).astype(x.dtype)

def causal_dwconv(x, w):
    width = w.shape[0]
    T = x.shape[1]
    xp = jnp.pad(x, ((0, 0), (width - 1, 0), (0, 0)))
    out = xp[:, 0:T] * w[0]
    for i in range(1, width):
        out = out + xp[:, i:i + T] * w[i]
    return out

def gated_deltanet(q, k, v, z, a, b, conv_w, a_log, dt_bias, norm_g):
    f32 = jnp.float32
    Bsz, T, _ = q.shape
    qkv = jax.nn.silu(causal_dwconv(jnp.concatenate([q, k, v], axis=-1), conv_w))
    q, k, v = jnp.split(qkv, [A_HEADS * A_DK, 2 * A_HEADS * A_DK], axis=-1)
    q = l2_norm(q.reshape(Bsz, T, A_HEADS, A_DK)) * (A_DK ** -0.5)
    k = l2_norm(k.reshape(Bsz, T, A_HEADS, A_DK))
    v = v.reshape(Bsz, T, A_HEADS, A_DV).astype(f32)
    g = -jnp.exp(a_log.astype(f32)) * jax.nn.softplus(a.astype(f32) + dt_bias.astype(f32))
    beta = jax.nn.sigmoid(b.astype(f32))
    pad = (-T) % CHUNK
    Tp = T + pad
    N = Tp // CHUNK

    def chunks(t):
        t = jnp.pad(t, ((0, 0), (pad, 0)) + ((0, 0),) * (t.ndim - 2))
        t = t.reshape((Bsz, N, CHUNK) + t.shape[2:])
        return jnp.moveaxis(t, 3, 1)

    qc, kc, vc, gch, bc = chunks(q), chunks(k), chunks(v), chunks(g), chunks(beta)
    gcum = jnp.cumsum(gch, axis=-1)
    pos = jnp.arange(CHUNK)
    incl = pos[:, None] >= pos[None, :]
    strict = pos[:, None] > pos[None, :]
    decay = jnp.exp(jnp.where(incl, gcum[..., :, None] - gcum[..., None, :], -jnp.inf))
    kk = jnp.einsum('bhncd,bhnsd->bhncs', kc, kc)
    m = jnp.where(strict, bc[..., None] * kk * decay, 0.0)
    lhs = m + jnp.eye(CHUNK, dtype=f32)
    rhs = jnp.concatenate([vc * bc[..., None], kc * (bc * jnp.exp(gcum))[..., None]], axis=-1)
    sol = lax.linalg.triangular_solve(lhs, rhs, left_side=True, lower=True, unit_diagonal=True)
    u, w = sol[..., :A_DV], sol[..., A_DV:]
    qk = jnp.einsum('bhncd,bhnsd->bhncs', qc, kc) * decay

    def step(S, inp):
        q_c, k_c, u_c, w_c, g_c, qk_c = inp
        v_new = u_c - jnp.einsum('bhcd,bhde->bhce', w_c, S)
        o = (jnp.einsum('bhcd,bhde->bhce', q_c * jnp.exp(g_c)[..., None], S)
             + jnp.einsum('bhcs,bhse->bhce', qk_c, v_new))
        g_last = g_c[..., -1]
        S = (S * jnp.exp(g_last)[..., None, None]
             + jnp.einsum('bhcd,bhce->bhde', k_c * jnp.exp(g_last[..., None] - g_c)[..., None], v_new))
        return S, o

    xs = tuple(jnp.moveaxis(t, 2, 0) for t in (qc, kc, u, w, gcum, qk))
    S0 = jnp.zeros((Bsz, A_HEADS, A_DK, A_DV), f32)
    _, o = lax.scan(step, S0, xs)
    o = jnp.transpose(o, (1, 0, 3, 2, 4)).reshape(Bsz, Tp, A_HEADS, A_DV)[:, pad:]
    o = rms_norm(o, norm_g) * jax.nn.silu(z.reshape(Bsz, T, A_HEADS, A_DV).astype(f32))
    return o.reshape(Bsz, T, A_WIDTH).astype(z.dtype)

def dsa_attention(q, k, v, iq, ik, iw, q_norm, k_norm, kidx_norm, cos_a, sin_a, cos_i, sin_i):
    f32 = jnp.float32
    Bsz, T, _ = q.shape
    S = T - N_META
    topk = min(TOPK_MAX, S // TOPK_DIV)
    q = apply_rope(rms_norm(q.reshape(Bsz, T, B_HEADS, B_DH), q_norm), cos_a, sin_a)
    k = apply_rope(rms_norm(k.reshape(Bsz, T, 1, B_DH), k_norm), cos_a, sin_a)[:, :, 0]
    iq = apply_rope(iq.reshape(Bsz, T, IDX_HEADS, IDX_DIM), cos_i, sin_i)
    ik = apply_rope(rms_norm(ik.reshape(Bsz, T, 1, IDX_DIM), kidx_norm), cos_i, sin_i)[:, :, 0]
    iw = iw * (IDX_HEADS ** -0.5 * IDX_DIM ** -0.5)
    scale = B_DH ** -0.5

    q_m, k_m, v_m = q[:, :N_META], k[:, :N_META], v[:, :N_META]
    s_mm = jnp.einsum('bqhd,bkd->bhqk', q_m, k_m).astype(f32) * scale
    o_meta = jnp.einsum('bhqk,bkd->bqhd', jax.nn.softmax(s_mm, axis=-1).astype(v.dtype), v_m)

    nb = S // Q_BLOCK
    q_r = q[:, N_META:].reshape(Bsz, nb, Q_BLOCK, B_HEADS, B_DH).swapaxes(0, 1)
    iq_r = iq[:, N_META:].reshape(Bsz, nb, Q_BLOCK, IDX_HEADS, IDX_DIM).swapaxes(0, 1)
    iw_r = iw[:, N_META:].reshape(Bsz, nb, Q_BLOCK, IDX_HEADS).swapaxes(0, 1)
    ik_r = ik[:, N_META:]
    kv_r = jnp.concatenate([k[:, N_META:], v[:, N_META:]], axis=-1)
    key_pos = jnp.arange(S)

    def one_block(args):
        j, qb, iqb, iwb = args
        q_pos = j * Q_BLOCK + jnp.arange(Q_BLOCK)
        limit = (q_pos // CHUNK + 1) * CHUNK
        valid = key_pos[None, :] < limit[:, None]
        logit_i = jnp.einsum('bqhd,bsd->bhqs', iqb, ik_r)
        score = jnp.einsum('bhqs,bqh->bqs', jax.nn.relu(logit_i), iwb).astype(f32)
        score = jnp.where(valid[None], score, -jnp.inf)
        _, sel = lax.top_k(score, topk)
        sel_valid = sel < limit[None, :, None]
        kv_sel = jax.vmap(lambda arr, ix: arr[ix])(kv_r, sel)
        k_sel, v_sel = kv_sel[..., :B_DH], kv_sel[..., B_DH:]
        s_meta = jnp.einsum('bqhd,bmd->bhqm', qb, k_m).astype(f32)
        s_sel = jnp.einsum('bqhd,bqkd->bhqk', qb, k_sel).astype(f32)
        s_sel = jnp.where(sel_valid[:, None], s_sel, -jnp.inf)
        p = jax.nn.softmax(jnp.concatenate([s_meta, s_sel], axis=-1) * scale, axis=-1).astype(v.dtype)
        return (jnp.einsum('bhqm,bmd->bqhd', p[..., :N_META], v_m)
                + jnp.einsum('bhqk,bqkd->bqhd', p[..., N_META:], v_sel))

    o_r = lax.map(one_block, (jnp.arange(nb), q_r, iq_r, iw_r))
    o_r = o_r.swapaxes(0, 1).reshape(Bsz, S, B_HEADS, B_DH)
    return jnp.concatenate([o_meta, o_r], axis=1).reshape(Bsz, T, B_WIDTH)

def hybrid_mixer(n, w_in, conv_a, a_log, dt_bias, a_out_norm, q_norm, k_norm, kidx_norm,
                 w_branch_a, w_branch_b, w_gate, b_gate, w_out, cos_a, sin_a, cos_i, sin_i):
    Bsz, T, D = n.shape
    proj = n @ w_in
    aq, ak, av, az, aa, ab, bq, bk, bv, iq, ik, iw = jnp.split(proj, SPLIT_POINTS, axis=-1)
    o_a = gated_deltanet(aq, ak, av, az, aa, ab, conv_a, a_log, dt_bias, a_out_norm)
    o_b = dsa_attention(bq, bk, bv, iq, ik, iw, q_norm, k_norm, kidx_norm, cos_a, sin_a, cos_i, sin_i)
    gates = jax.nn.sigmoid(n @ w_gate + b_gate).reshape(Bsz, T, 2, D)
    y = gates[:, :, 0] * (o_a @ w_branch_a) + gates[:, :, 1] * (o_b @ w_branch_b)
    return y @ w_out

def conv_gated_mlp(n, w_up, conv_w, w_down):
    gate, up = jnp.split(n @ w_up, 2, axis=-1)
    gate = causal_dwconv(gate, conv_w)
    return (jax.nn.silu(gate) * up) @ w_down

def second_inputs(seed: int = 0) -> dict:
    key = jax.random.key(seed)
    ks = jax.random.split(key, 24)
    L, D = DEPTH, D_MODEL
    f32 = jnp.float32

    def nrm(k, shape, scale):
        return jax.random.normal(k, shape, f32) * scale

    def gain(k, shape):
        return 1.0 + nrm(k, shape, 0.02)

    a_init = jax.random.uniform(ks[5], (L, A_HEADS), f32, 1.0, 16.0)
    dt = jnp.exp(jax.random.uniform(ks[6], (L, A_HEADS), f32, math.log(1e-3), math.log(1e-1)))
    return {
        "x": nrm(ks[0], (BATCH, SEQ, D), 1.0),
        "meta_tokens": nrm(ks[1], (N_META, D), 0.5),
        "norm_mix": gain(ks[2], (L, D)),
        "w_in": nrm(ks[3], (L, D, IN_COLS), D ** -0.5),
        "conv_a": nrm(ks[4], (L, A_CONV, 2 * A_HEADS * A_DK + A_WIDTH), 0.5),
        "a_log": jnp.log(a_init),
        "dt_bias": dt + jnp.log(-jnp.expm1(-dt)),
        "a_out_norm": gain(ks[7], (L, A_DV)),
        "q_norm": gain(ks[8], (L, B_DH)),
        "k_norm": gain(ks[9], (L, B_DH)),
        "kidx_norm": gain(ks[10], (L, IDX_DIM)),
        "w_branch_a": nrm(ks[11], (L, A_WIDTH, D), A_WIDTH ** -0.5),
        "w_branch_b": nrm(ks[12], (L, B_WIDTH, D), B_WIDTH ** -0.5),
        "w_gate": nrm(ks[13], (L, D, 2 * D), D ** -0.5),
        "b_gate": nrm(ks[14], (L, 2 * D), 0.1),
        "w_out": nrm(ks[15], (L, D, D), D ** -0.5),
        "norm_ffn": gain(ks[16], (L, D)),
        "w_up": nrm(ks[17], (L, D, 2 * D_FF_2), D ** -0.5),
        "conv_ffn": nrm(ks[18], (L, FFN_CONV, D_FF_2), 0.5),
        "w_down": nrm(ks[19], (L, D_FF_2, D), D_FF_2 ** -0.5),
    }

def second_block(x, meta_tokens, norm_mix, w_in, conv_a, a_log, dt_bias, a_out_norm, q_norm, k_norm,
              kidx_norm, w_branch_a, w_branch_b, w_gate, b_gate, w_out, norm_ffn, w_up, conv_ffn,
              w_down) -> jnp.ndarray:
    Bsz = x.shape[0]
    T = N_META + x.shape[1]
    cos_a, sin_a = rope_tables_2(T, B_DH)
    cos_i, sin_i = rope_tables_2(T, IDX_DIM)
    meta = jnp.broadcast_to(meta_tokens.astype(x.dtype)[None], (Bsz, N_META, x.shape[2]))
    h = jnp.concatenate([meta, x], axis=1)
    for l in range(DEPTH):
        n = rms_norm(h, norm_mix[l])
        h = h + hybrid_mixer(n, w_in[l], conv_a[l], a_log[l], dt_bias[l], a_out_norm[l], q_norm[l],
                             k_norm[l], kidx_norm[l], w_branch_a[l], w_branch_b[l], w_gate[l], b_gate[l],
                             w_out[l], cos_a, sin_a, cos_i, sin_i).astype(h.dtype)
        n = rms_norm(h, norm_ffn[l])
        h = h + conv_gated_mlp(n, w_up[l], conv_ffn[l], w_down[l]).astype(h.dtype)
    return h[:, N_META:]


def setup_inputs(seed=0):
    out = dict(first_inputs(seed))
    for name, value in second_inputs(seed + 1).items():
        if name != "x":
            out[name + "_2"] = value
    return out


def reference(
    x, mem, positions, w_in_swa, attn_sinks, w_in_fox, b_forget, w_mem_kv, w_out, ln_attn_g,
    ln_attn_b, w_ffn_in, w_ffn_out, w_router, b_router, w_exp_in, w_exp_out, ln_ffn_g, ln_ffn_b,
    meta_tokens_2, norm_mix_2, w_in_2, conv_a_2, a_log_2, dt_bias_2, a_out_norm_2, q_norm_2,
    k_norm_2, kidx_norm_2, w_branch_a_2, w_branch_b_2, w_gate_2, b_gate_2, w_out_2, norm_ffn_2,
    w_up_2, conv_ffn_2, w_down_2,
):
    x = first_block(
        x, mem, positions, w_in_swa, attn_sinks, w_in_fox, b_forget, w_mem_kv, w_out, ln_attn_g,
        ln_attn_b, w_ffn_in, w_ffn_out, w_router, b_router, w_exp_in, w_exp_out, ln_ffn_g,
        ln_ffn_b,
    )
    return second_block(
        x, meta_tokens_2, norm_mix_2, w_in_2, conv_a_2, a_log_2, dt_bias_2, a_out_norm_2,
        q_norm_2, k_norm_2, kidx_norm_2, w_branch_a_2, w_branch_b_2, w_gate_2, b_gate_2,
        w_out_2, norm_ffn_2, w_up_2, conv_ffn_2, w_down_2,
    )


_drawn_inputs = setup_inputs


def setup_inputs(seed=0):
    import zlib

    import numpy as np

    out = dict(_drawn_inputs(seed))
    spreads = {}
    factors = {'attn_sinks': 8.0,
     'a_out_norm_2': 5.472,
     'q_norm_2': 8.0,
     'k_norm_2': 8.0,
     'kidx_norm_2': 4.041,
     'norm_ffn_2': 2.687}
    for name, (base, spread) in spreads.items():
        noise = np.random.default_rng([zlib.crc32(name.encode()), seed]).standard_normal(out[name].shape)
        drawn = base * np.exp(spread * noise) if base else spread * noise
        out[name] = __import__('jax').numpy.asarray(drawn.astype(out[name].dtype))
    for name, factor in factors.items():
        out[name] = (out[name] * factor).astype(out[name].dtype)
    return out
```

```python
from contextlib import ExitStack

import numpy as np
import concourse.bass as bass
from concourse import mybir

F32 = mybir.dt.float32
I32 = mybir.dt.int32
ALU = mybir.AluOpType
ACT = mybir.ActivationFunctionType
AX = mybir.AxisListType

D = 1024
KT = 8
S = 256
NM = 16
T2 = S + NM
FF = 2816
FT = FF // 128
NE = 8
DEPTH = 2
ALPHA = float((2.0 * DEPTH) ** 0.25)
SCALE = 0.125
BSCALE = float(128 ** -0.5)
BIG = 1e30
INV1 = [float.fromhex(x) for x in (
    '0x1.0000000000000p+0', '0x1.8d275e0000000p-3', '0x1.3411900000000p-5', '0x1.ddee9c0000000p-8',
    '0x1.72ba440000000p-10', '0x1.1f91f00000000p-12', '0x1.be21880000000p-15', '0x1.5a0f4e0000000p-17')]
TWO_PI_1 = 6.28125
TWO_PI_2 = float(np.float32(int((2 * np.pi - TWO_PI_1) * 2 ** 20) / 2 ** 20))
TWO_PI_3 = float(np.float32(2 * np.pi - TWO_PI_1 - TWO_PI_2))
MAGIC = 12582912.0

FIELDS = [
    ("ident", 128), ("ones", 128), ("mean", 128), ("mean128", 128), ("mean64", 128), ("upper", 128),
    ("swa", 512), ("causal", 512), ("valid", 512), ("rot1", 128), ("rota", 128), ("roti", 128),
    ("cosa", T2), ("sina", T2), ("cosi", T2), ("sini", T2), ("um", 128), ("umt", 128),
    ("lm", 896), ("lmt", 896), ("colsel", 15), ("inv1", 1), ("eps5", 1), ("eps6", 1),
    ("ln_attn_g", 16), ("ln_attn_b", 16), ("ln_ffn_g", 16), ("ln_ffn_b", 16),
    ("norm_mix", 16), ("norm_ffn", 16), ("sinks", 12), ("b_forget", 12), ("b_router", 8),
    ("a_log", 8), ("dt_bias", 8), ("conv_a", 96), ("conv_ffn", 132), ("a_out_norm", 2),
    ("q_norm", 2), ("k_norm", 2), ("kidx", 2), ("b_gate", 32),
]
AT = {}
_n = 0
for _name, _w in FIELDS:
    AT[_name] = _n
    _n += _w
NPACK = _n

FOX_CHUNKS = [(0, 512), (512, 1024), (1024, 1536), (1536, 2048), (2048, 2572)]


class Token:

    def __init__(self, sem, value=None):
        self.sem, self.value, self.used = sem, value, value is not None


class Queue:

    def __init__(self, sem, serial):
        self.sem, self.serial, self.ops, self.last = sem, serial, [], None

    def __call__(self, fn, *after, free=False):
        token = Token(self.sem)
        waits = flat(after)
        if self.serial and not free and self.last is not None:
            waits.append(self.last)
        self.ops.append((fn, waits, token, 1))
        self.last = token
        return token

    def emit(self, eng):
        seen = {}
        for fn, waits, token, by in self.ops:
            need = {}
            for w in waits:
                if w.value > need.get(w.sem, 0):
                    need[w.sem] = w.value
            for sem, value in need.items():
                if seen.get(sem, 0) < value:
                    eng.wait_ge(sem, value)
                    seen[sem] = value
            if fn is None:
                continue
            ins = fn(eng)
            if token.used:
                ins.then_inc(token.sem, by)


def flat(xs):
    out = []
    for x in xs:
        if x is None:
            continue
        if isinstance(x, (list, tuple)):
            out += flat(x)
        else:
            out.append(x)
    return out


def number(queues):
    for q in queues:
        for _, waits, _, _ in q.ops:
            for w in waits:
                w.used = True
    for q in queues:
        n = 0
        for _, _, token, by in q.ops:
            if by == 1 and token.used:
                n += 1
                token.value = n


class Slots:

    def __init__(self, views):
        self.rows = [[v, []] for v in views]

    def take(self):
        row = self.rows.pop(0)
        return row[0], row[1]

    def give(self, view, *tokens):
        self.rows.append([view, flat(tokens)])


def build(nc, a):
    ctx = ExitStack()
    with ctx:
        def sb(name, shape, dt=F32):
            return ctx.enter_context(nc.sbuf_tensor(name, shape, dt))

        def sem(name):
            return ctx.enter_context(nc.semaphore(name))

        pk = sb("pk", [128, NPACK])
        NR = 4
        RING = 524 * 8
        ring = [sb(f"ring{i}", [128, RING]) for i in range(NR)]
        hX = sb("hX", [128, KT, T2])
        nX = sb("nX", [128, KT, T2])
        rX = sb("rX", [128, KT * T2])
        sq = sb("sq", [128, KT * T2])
        mX = sb("mX", [128, KT, T2])
        W1 = sb("W1", [128, FT * T2])
        W2 = sb("W2", [128, 7700])
        TM = sb("TM", [128, 8, T2])
        sm = sb("sm", [128, 512])
        banks = [ctx.enter_context(nc.psum_tensor(f"pb{i}", [128, 512], F32)) for i in range(8)]

        P = Queue(sem("s_pe"), False)
        V = Queue(sem("s_dve"), True)
        A = Queue(sem("s_act"), True)
        G = Queue(sem("s_pool"), True)
        Y = Queue(sem("s_sp"), False)
        PB = Slots(banks)
        ring_sems = [sem(f"s_ring{i}") for i in range(NR)]
        ring_count = [0] * NR
        RS = Slots(list(range(NR)))
        s_in = sem("s_in")
        s_out = sem("s_out")

        def C(name, i=0, w=None, p=128):
            o = AT[name] + i
            return pk[0:p, o:o + (w if w is not None else dict(FIELDS)[name])]

        def dma(queue, out, src, s, total, *after):
            token = Token(s, total)
            queue.ops.append((lambda e: e.dma_start(out, src), flat(after), token, 16))
            return token

        class Load:

            def __init__(self, parts):
                self.i, free = RS.take()
                self.buf = ring[self.i]
                for f, src in parts:
                    ring_count[self.i] += 16
                    self.ready = dma(Y, f(self.buf), src, ring_sems[self.i], ring_count[self.i], free)
                    free = []

            def done(self, *tokens):
                RS.give(self.i, *tokens)

        def cols(w, c0, c1):
            n, kt = c1 - c0, w.shape[0] // 128
            view = lambda b: b[:, 0:kt * n].rearrange("p (k n) -> p k n", k=kt)
            ld = Load([(view, w.rearrange("(k p) n -> p k n", p=128)[:, :, c0:c1])])
            ld.w = view(ld.buf)
            return ld

        def whole(w):
            _, kt, n = w.shape
            view = lambda b: b[:, 0:kt * n].rearrange("p (k n) -> p k n", k=kt)
            ld = Load([(view, w)])
            ld.w = view(ld.buf)
            return ld

        def mm(out, lhsT, rhs, start, stop, *after, **kw):
            return P(lambda e: e.matmul(out, lhsT, rhs, start=start, stop=stop, **kw), *after)

        def tr(out, in_, n, *after):
            return P(lambda e: e.transpose(out, in_, C("ident", 0, n, n)), *after)

        def vtt(out, x, y, op, *after, q=None, free=False):
            return (q or V)(lambda e: e.tensor_tensor(out, x, y, op), *after, free=free)

        def vts(out, x, s1, s2, o1, o2=None, *after, free=False, q=None):
            if o2 is None:
                return (q or V)(lambda e: e.tensor_scalar(out, x, s1, None, o1), *after, free=free)
            return (q or V)(lambda e: e.tensor_scalar(out, x, s1, s2, o1, o2), *after, free=free)

        def stt(out, x, s, y, o1, o2, *after, free=False):
            return V(lambda e: e.scalar_tensor_tensor(out=out, in0=x, scalar=s, in1=y, op0=o1, op1=o2),
                     *after, free=free)

        def act(out, x, f, *after, free=False, **kw):
            return A(lambda e: e.activation(out, x, f, **kw), *after, free=free)

        def vcopy(out, x, *after, free=False):
            return V(lambda e: e.tensor_copy(out, x), *after, free=free)

        def recip(out, x, *after):
            return V(lambda e: e.reciprocal(out, x), *after)

        M_, A_, B_ = (0, NM), (NM, NM + 128), (NM + 128, T2)

        def group(bank, m, t0, t1, w, c0, rhs, kt, after):
            n = t1 - t0
            for k in range(kt):
                tok = mm(bank[0:m, 0:n], w[:, k, c0:c0 + m], rhs(k)[:, t0:t1], k == 0, k == kt - 1,
                         after if k == 0 else None)
            return tok

        def product(ld, groups, rhs, kt, t0, t1, after, evac):
            for c0, m, key in groups:
                bank, free = PB.take()
                tok = group(bank, m, t0, t1, ld.w, c0, rhs, kt, [free, ld.ready, after])
                PB.give(bank, evac(key, bank[0:m, 0:t1 - t0], tok))
            ld.done(tok)

        def rows(ld, c0, n, lhs, kt, tiles, after, evac):
            for i, (t0, t1) in enumerate(tiles):
                bank, free = PB.take()
                for k in range(kt):
                    tok = mm(bank[0:t1 - t0, 0:n], lhs(k)[:, t0:t1], ld.w[:, k, c0:c0 + n], k == 0,
                             k == kt - 1, [free, ld.ready, after] if k == 0 else None)
                PB.give(bank, evac(i, bank[0:t1 - t0, 0:n], tok))
            return tok

        in_tot = 0

        def load_in(out, src):
            nonlocal in_tot
            in_tot += 16
            return dma(Y, out, src, s_in, in_tot)

        load_in(pk[:, :], a["pack"])
        pos_i = TM[:, 0, 0:S].bitcast(I32)
        load_in(pos_i, a["pos"])
        load_in(hX[:, :, NM:T2], a["xT"])
        inputs = load_in(hX[:, :, 0:NM], a["metaT"])
        memT = whole(a["memT"])
        for q in (P, V, A, G):
            q.ops.append((None, [inputs], Token(None, 0), 0))

        cos1, sin1 = TM[:, 6, 0:S], TM[:, 7, 0:S]
        posf, ang, kk, r1 = TM[:, 1, 0:S], TM[:, 2, 0:S], TM[:, 3, 0:S], TM[:, 4, 0:S]
        vcopy(posf, pos_i)
        vts(ang, posf, C("inv1"), None, ALU.mult)
        vts(kk, ang, float(1 / (2 * np.pi)), MAGIC, ALU.mult, ALU.add)
        vts(kk, kk, MAGIC, None, ALU.subtract)
        stt(r1, kk, -TWO_PI_1, ang, ALU.mult, ALU.add)
        stt(r1, kk, -TWO_PI_2, r1, ALU.mult, ALU.add)
        stt(r1, kk, -TWO_PI_3, r1, ALU.mult, ALU.add)
        t = vts(r1, r1, 3.1415925, -3.1415925, ALU.min, ALU.max)
        act(sin1, r1, ACT.Sin, t)
        t = act(kk, r1, ACT.Sin, scale=0.5)
        vtt(kk, kk, kk, ALU.mult, t)
        rope1 = vts(cos1, kk, -2.0, 1.0, ALU.mult, ALU.add)
        rope1 = [rope1, A.last]

        tmp = Slots([TM[:, i, :] for i in range(4)])
        for i in range(4):
            v_, _ = tmp.take()
            tmp.give(v_, V.last, A.last)
        tmp2 = Slots([TM[:, i, :] for i in range(4, 6)])
        v_, _ = tmp2.take()
        tmp2.give(v_, V.last, A.last)

        r3 = rX[:, :].rearrange("p (k t) -> p k t", k=KT)
        q3 = sq[:, :].rearrange("p (k t) -> p k t", k=KT)

        def layer_norm(g, b, li, out, r_ready):
            bank, free = PB.take()
            mu = bank[:, 0:S]
            for k in range(KT):
                t = mm(mu, C("mean"), r3[:, k, NM:T2], k == 0, k == KT - 1, free if k == 0 else None,
                       r_ready[k])
            bank2, free2 = PB.take()
            var = bank2[:, 0:S]
            for k in range(KT):
                d = vtt(r3[:, k, NM:T2], r3[:, k, NM:T2], mu, ALU.subtract, t, free=k > 0)
                s = act(q3[:, k, NM:T2], r3[:, k, NM:T2], ACT.Square, d, free=k > 0)
                t2 = mm(var, C("mean"), q3[:, k, NM:T2], k == 0, k == KT - 1, free2 if k == 0 else None, s)
            PB.give(bank, d)
            sd, tf = tmp.take()
            s = act(sd[:, 0:S], var, ACT.Sqrt, t2, tf, bias=C("eps5"))
            PB.give(bank2, s)
            rs = recip(sd[:, 0:S], sd[:, 0:S], s)
            out_ready = []
            for k in range(KT):
                v = vtt(r3[:, k, NM:T2], r3[:, k, NM:T2], sd[:, 0:S], ALU.mult, rs, free=k > 0)
                i = li * 8 + k
                out_ready.append(act(out[:, k, NM:T2], r3[:, k, NM:T2], ACT.Identity, v, P.last,
                                     free=k > 0, scale=C(g, i, 1), bias=C(b, i, 1)))
            tmp.give(sd, v)
            return out_ready

        def rms_norm(g, li, h, out, h_ready):
            bank, free = PB.take()
            ms = bank[:, 0:T2]
            for k in range(KT):
                s = act(q3[:, k, :], h[:, k, :], ACT.Square, h_ready[k], P.last if k == 0 else None, free=k > 0)
                t = mm(ms, C("mean"), q3[:, k, :], k == 0, k == KT - 1, free if k == 0 else None, s)
            sd, tf = tmp.take()
            s = act(sd, ms, ACT.Sqrt, t, tf, bias=C("eps6"))
            PB.give(bank, s)
            rs = recip(sd, sd, s)
            ready = []
            for k in range(KT):
                ready.append(stt(out[:, k, :], h[:, k, :], C(g, li * 8 + k, 1), sd, ALU.mult, ALU.mult,
                                 rs, P.last, free=k > 0))
            tmp.give(sd, ready[-1])
            return ready

        sc_slots = Slots([rX[:, 512 * i:512 * i + 512] for i in range(3)])
        pt_slots = Slots([sq[:, 512 * i:512 * i + 512] for i in range(3)])
        st_slots = Slots([sm[:, 8 * i:8 * i + 8] for i in range(6)])

        def attend(heads, ready):
            n = len(heads)
            st = {}
            for i in range(n + 2):
                if i < n:
                    h = heads[i]
                    bank, free = PB.take()
                    for t in range(2):
                        tok = mm(bank[:, 256 * t:256 * t + 256], h["q"][:, 128 * t:128 * t + 128], h["k"],
                                 t == 0, t == 1, [free, ready] if t == 0 else None, skip_group_check=True)
                    sc, f = sc_slots.take()
                    s2, f2 = st_slots.take()
                    v = h["add"](sc, bank, [tok, f])
                    PB.give(bank, v)
                    nm, den = s2[:, 0:2], s2[:, 2:4]
                    sc3 = sc.rearrange("p (t k) -> p t k", t=2)
                    v = V(lambda e, nm=nm, sc3=sc3: e.tensor_reduce(nm, sc3, AX.X, ALU.max, negate=True), f2)
                    if h.get("sink") is not None:
                        v = vts(nm, nm, h["sink_neg"], None, ALU.min)
                    for t in range(2):
                        c = act(sc[:, 256 * t:256 * t + 256], sc[:, 256 * t:256 * t + 256], ACT.Exp, v,
                                bias=nm[:, t:t + 1], accum_out=den[:, t:t + 1])
                    if h.get("sink") is not None:
                        c = act(s2[:, 4:6], nm, ACT.Exp, bias=h["sink"])
                        vtt(den, den, s2[:, 4:6], ALU.add, c)
                    recip(den, den, c)
                    for t in range(2):
                        v = vts(sc[:, 256 * t:256 * t + 256], sc[:, 256 * t:256 * t + 256], den[:, t:t + 1],
                                None, ALU.mult)
                    st_slots.give(s2, v)
                    st[i] = (sc, v)
                if 1 <= i <= n:
                    sc, v = st[i - 1]
                    bank, free = PB.take()
                    for kt in range(2):
                        for t in range(2):
                            tok = tr(bank[:, 256 * kt + 128 * t:256 * kt + 128 * t + 128],
                                     sc[:, 256 * t + 128 * kt:256 * t + 128 * kt + 128], 128,
                                     [free, v] if kt + t == 0 else None)
                    sc_slots.give(sc, tok)
                    pt, f = pt_slots.take()
                    c = act(pt, bank[:, :], ACT.Copy, tok, f)
                    PB.give(bank, c)
                    st[i - 1] = (pt, c)
                if i >= 2:
                    j = i - 2
                    h = heads[j]
                    pt, c = st[j]
                    if j % 2 == 0:
                        obank, ofree = PB.take()
                    p0 = 64 * (j % 2)
                    for kt in range(2):
                        tok = mm(obank[p0:p0 + 64, 0:S], h["v"][kt], pt[:, 256 * kt:256 * kt + 256], kt == 0,
                                 kt == 1, [c, ofree] if kt == 0 else None)
                    pt_slots.give(pt, tok)
                    if j % 2 == 1:
                        v = vcopy(mX[:, h["tile"], NM:T2], obank[:, 0:S], tok)
                        PB.give(obank, v)
            return V.last

        def ffn_in(w_in, xr, x_ready, t0, t1, on_pair):
            wr = w_in.rearrange("(k p) n -> p k n", p=128)
            n = t1 - t0
            for u in range(FT // 2):
                view = lambda b, z: b[:, 2048 * z:2048 * z + 2048].rearrange("p (k n) -> p k n", k=KT)
                ld = Load([(lambda b: view(b, 0), wr[:, :, 256 * u:256 * u + 256]),
                           (lambda b: view(b, 1), wr[:, :, FF + 256 * u:FF + 256 * u + 256])])
                for g in range(2):
                    bk = []
                    for z in range(2):
                        bank, free = PB.take()
                        w = view(ld.buf, z)
                        for k in range(KT):
                            tok = mm(bank[:, 0:n], w[:, k, 128 * g:128 * g + 128], xr[:, k, t0:t1], k == 0,
                                     k == KT - 1, [free, ld.ready] if k == 0 else None, x_ready[k])
                        bk.append((bank, tok))
                    on_pair(2 * u + g, bk[0][0], bk[0][1], bk[1][0], bk[1][1])
                ld.done(tok)

        hT = W1[:, :].rearrange("p (k t) -> p k t", k=FT)

        def ffn_out(w_out, h_ready, t0, t1, evac):
            n = t1 - t0
            for g in range(KT):
                ld = whole(w_out[g])
                bank, free = PB.take()
                for k in range(FT):
                    tok = mm(bank[:, 0:n], ld.w[:, k, :], hT[:, k, t0:t1], k == 0, k == FT - 1,
                             [free, ld.ready] if k == 0 else None, h_ready[k])
                ld.done(tok)
                PB.give(bank, evac(g, bank[:, 0:n], tok))

        x_ready = [inputs] * KT
        xs = lambda k: hX[:, k, :]
        ms_ = lambda k: memT.w[:, k, :]
        for layer in range(2):
            o = 0

            def area(n):
                nonlocal o
                if o < FT * T2 and o + n > FT * T2:
                    o = FT * T2
                r = W1[:, o:o + n] if o < FT * T2 else W2[:, o - FT * T2:o - FT * T2 + n]
                o += n
                return r

            qn = area(8 * S).rearrange("p (k t) -> p k t", k=8)
            kn = area((3 if layer == 0 else 6) * S).rearrange("p (k t) -> p k t", t=S)
            vn = area(2 * (192 if layer == 0 else 768)).rearrange("p (t n) -> p t n", t=2)
            km = area(2 * S).rearrange("p (k t) -> p k t", t=S)
            vm = area(2 * 256).rearrange("p (t n) -> p t n", t=2)
            free_w = P.last

            wk = cols(a["w_mem_kv"][layer], 0, 512)
            product_tok = None
            for g in range(2):
                bank, free = PB.take()
                tok = group(bank, 128, 0, S, wk.w, 128 * g, ms_, KT, [free, wk.ready, memT.ready])
                PB.give(bank, act(km[:, g, :], bank[:, 0:S], ACT.Copy, tok, free_w))
            tok = rows(wk, 256, 256, ms_, KT, [(0, 128), (128, 256)], None,
                       lambda i, ps, tk: vcopy(vm[:, i, :], ps, tk, free_w))
            wk.done(tok)
            if layer == 1:
                memT.done(tok)

            def plain(dst):
                return lambda key, ps, tk: act(dst[:, key, :], ps, ACT.Copy, tk, free_w, free=True)

            if layer == 0:
                def roped(key, ps, tk):
                    dst = qn[:, key, :] if key < 8 else kn[:, key - 8, :]
                    raw, tf = tmp.take()
                    c = act(raw[:, 0:S], ps, ACT.Copy, tk, tf)
                    bank, free = PB.take()
                    m = mm(bank[:, 0:S], C("rot1"), raw[:, 0:S], True, True, c, free)
                    t2, tf2 = tmp2.take()
                    v = vtt(t2[:, 0:S], bank[:, 0:S], sin1, ALU.mult, m, tf2, rope1)
                    PB.give(bank, v)
                    vtt(dst, raw[:, 0:S], cos1, ALU.mult, c, free_w)
                    v = vtt(dst, dst, t2[:, 0:S], ALU.add)
                    tmp.give(raw, v)
                    tmp2.give(t2, v)
                    return c

                w = a["w_swa"]
                product(cols(w, 0, 512), [(128 * i, 128, i) for i in range(4)], xs, KT, NM, T2, x_ready, roped)
                product(cols(w, 512, 1024), [(0, 128, 4), (128, 128, 5), (256, 128, 8), (384, 128, 9)], xs,
                        KT, NM, T2, None, roped)
                product(cols(w, 1024, 1152), [(0, 128, 10)], xs, KT, NM, T2, None, roped)
                product(cols(w, 1152, 1408), [(0, 128, 6), (128, 128, 7)], xs, KT, NM, T2, None, plain(qn))
                ld = cols(w, 1408, 1600)
                ld.done(rows(ld, 0, 192, xs, KT, [A_, B_], None,
                             lambda i, ps, tk: vcopy(vn[:, i, :], ps, tk, free_w)))
                vts(sm[:, 64:76], C("sinks"), -1.0, None, ALU.mult)
                mask = C("swa")

                def add(sc, bank, after):
                    return stt(sc, bank[:, :], SCALE, mask, ALU.mult, ALU.add, after)

                heads = [dict(q=qn[64 * (i % 2):64 * (i % 2) + 64, i // 2, :],
                              k=kn[64 * (i % 2):64 * (i % 2) + 64, i // 4, :],
                              v=[vn[:, t, 64 * (i // 4):64 * (i // 4) + 64] for t in range(2)], add=add,
                              sink=C("sinks", i, 1), sink_neg=sm[:, 64 + i:65 + i], tile=i // 2)
                         for i in range(12)]
            else:
                w = a["w_fox"]
                cq = area(24).rearrange("p (t n) -> p t n", t=2)
                R = area(12 * S).rearrange("p (h t) -> p h t", t=S)
                ck = area(2 * S)
                dests = [(qn, i) for i in range(6)] + [(kn, i) for i in range(6)]

                def to(key, ps, tk):
                    d, i = dests[key]
                    return act(d[:, i, :], ps, ACT.Copy, tk, free_w, free=True)

                for c in range(3):
                    product(cols(w, 512 * c, 512 * c + 512), [(128 * i, 128, 4 * c + i) for i in range(4)], xs,
                            KT, NM, T2, x_ready if c == 0 else None, to)
                ld = cols(w, 1536, 2048)
                ld.done(rows(ld, 0, 512, xs, KT, [A_, B_], None,
                             lambda i, ps, tk: vcopy(vn[:, i, 0:512], ps, tk, free_w)))
                ld = cols(w, 2048, 2572)
                rows(ld, 0, 256, xs, KT, [A_, B_], None,
                     lambda i, ps, tk: vcopy(vn[:, i, 512:768], ps, tk, free_w))
                lf = sm[:, 128:152].rearrange("p (t n) -> p t n", t=2)
                lg = sm[:, 152:176].rearrange("p (t n) -> p t n", t=2)
                ls = sm[:, 176:200].rearrange("p (t n) -> p t n", t=2)
                rows(ld, 512, 12, xs, KT, [A_, B_], None,
                     lambda i, ps, tk: vtt(lf[:, i, :], ps, C("b_forget"), ALU.add, tk))
                product(ld, [(256, 128, 6), (384, 128, 7)], xs, KT, NM, T2, None, plain(qn))
                c = act(lg, lf, ACT.Abs, V.last)
                c = act(lg, lg, ACT.Exp, scale=-1.0)
                c = act(lg, lg, ACT.Ln, bias=1.0)
                lft = stt(ls, lf, 0.0, lg, ALU.min, ALU.subtract, c)
                bank, free = PB.take()
                mm(bank[:, 0:12], C("upper"), ls[:, 0, :], True, False, free, lft, skip_group_check=True)
                mm(bank[:, 16:28], C("upper"), ls[:, 1, :], False, False, skip_group_check=True)
                tok = mm(bank[:, 16:28], C("ones"), ls[:, 0, :], False, True, skip_group_check=True)
                v = vcopy(cq[:, 0, :], bank[:, 0:12], tok)
                v = vcopy(cq[:, 1, :], bank[:, 16:28], tok)
                PB.give(bank, v)
                bank, free = PB.take()
                for t in range(2):
                    tok = tr(bank[0:12, 128 * t:128 * t + 128], cq[:, t, :], 128, v, free)
                v = vcopy(ck[0:12, 0:S], bank[0:12, 0:S], tok)
                PB.give(bank, v)
                for h in range(12):
                    bank, free = PB.take()
                    tok = mm(bank[:, 0:S], C("ident", h, 1, 12).to_broadcast([12, 128]), ck[0:12, 0:S], True,
                             True, v, free)
                    c = act(R[:, h, :], bank[:, 0:S], ACT.Copy, tok, free=True)
                    PB.give(bank, c)
                tb = [tmp.take() for _ in range(2)]
                bias_buf = [x[0] for x in tb]
                bias_free = [x[1] for x in tb]

                def adder(h):
                    def add(sc, bank, after):
                        for t in range(2):
                            b = bias_buf[t][:, 0:S]
                            stt(b, R[:, h, :], cq[:, t, h:h + 1], C("causal", 256 * t, 256), ALU.subtract,
                                ALU.subtract, c, bias_free)
                            v = stt(sc[:, 256 * t:256 * t + 256], bank[:, 256 * t:256 * t + 256], SCALE, b,
                                    ALU.mult, ALU.subtract, after)
                        return v
                    return add

                heads = [dict(q=qn[64 * (i % 2):64 * (i % 2) + 64, i // 2, :],
                              k=kn[64 * (i % 2):64 * (i % 2) + 64, i // 2, :],
                              v=[vn[:, t, 64 * i:64 * i + 64] for t in range(2)], add=adder(i), tile=i // 2)
                         for i in range(12)]

            def add_mem(sc, bank, after):
                return vts(sc, bank[:, :], SCALE, None, ALU.mult, None, after)

            heads += [dict(q=qn[64 * (i % 2):64 * (i % 2) + 64, 6 + i // 2, :],
                           k=km[64 * (i % 2):64 * (i % 2) + 64, i // 2, :],
                           v=[vm[:, t, 64 * i:64 * i + 64] for t in range(2)], add=add_mem, tile=6 + i // 2)
                      for i in range(4)]
            mixed = attend(heads, [V.last, A.last])
            if layer == 1:
                for b in bias_buf:
                    tmp.give(b, V.last)

            r_ready = {}

            def res(key, ps, tk):
                r_ready[key] = stt(r3[:, key, NM:T2], hX[:, key, NM:T2], ALPHA, ps, ALU.mult, ALU.add, tk,
                                   P.last, A.last, free=True)
                return r_ready[key]

            for c in range(2):
                product(cols(a["w_out"][layer], 512 * c, 512 * c + 512),
                        [(128 * i, 128, 4 * c + i) for i in range(4)], lambda k: mX[:, k, :], KT, NM, T2,
                        mixed, res)
            x_ready = layer_norm("ln_attn_g", "ln_attn_b", layer, nX, r_ready)

            if layer == 0:
                h_ready = {}

                def pair(j, ba, ta, bb, tb_):
                    s_, tf = tmp.take()
                    c = act(s_[:, 0:S], ba[:, 0:S], ACT.Silu, ta, tf, free=True)
                    PB.give(ba, c)
                    v = vtt(hT[:, j, NM:T2], s_[:, 0:S], bb[:, 0:S], ALU.mult, c, tb_, free_ff, free=True)
                    PB.give(bb, v)
                    tmp.give(s_, v)
                    h_ready[j] = v

                free_ff = P.last
                ffn_in(a["w_ffn_in"], nX, x_ready, NM, T2, pair)

                def down(g, ps, tk):
                    r_ready[g] = stt(r3[:, g, NM:T2], nX[:, g, NM:T2], ALPHA, ps, ALU.mult, ALU.add, tk,
                                     free=True)
                    return r_ready[g]

                ffn_out(a["w_ffn_out"], h_ready, NM, T2, down)
                x_ready = layer_norm("ln_ffn_g", "ln_ffn_b", layer, hX, r_ready)
            else:
                ld = whole(a["w_router"])
                lo = sm[:, 200:216].rearrange("p (t n) -> p t n", t=2)
                ld.done(rows(ld, 0, 8, lambda k: nX[:, k, :], KT, [A_, B_], x_ready,
                             lambda i, ps, tk: vtt(lo[:, i, :], ps, C("b_router"), ALU.add, tk)))
                gt_ = sm[:, 216:232].rearrange("p (t n) -> p t n", t=2)
                eq = sm[:, 232:248].rearrange("p (t n) -> p t n", t=2)
                cu = sm[:, 248:264].rearrange("p (t n) -> p t n", t=2)
                cv = sm[:, 264:280].rearrange("p (t n) -> p t n", t=2)
                ex = sm[:, 280:296].rearrange("p (t n) -> p t n", t=2)
                mx = sm[:, 296:312].rearrange("p (t n) -> p t n", t=2)
                s1 = sm[:, 312:314]
                for t in range(2):
                    V(lambda e, t=t: e.max(mx[:, t, :], lo[:, t, :]))
                    vts(gt_[:, t, :], lo[:, t, :], mx[:, t, 1:2], None, ALU.is_gt)
                    vts(eq[:, t, :], lo[:, t, :], mx[:, t, 1:2], None, ALU.is_equal)
                    v = vts(ex[:, t, :], lo[:, t, :], mx[:, t, 0:1], None, ALU.subtract)
                c = act(ex, ex, ACT.Exp, v)
                src, dst = eq, cu
                for sft in (1, 2, 4):
                    vcopy(dst[:, :, 0:sft], src[:, :, 0:sft])
                    vtt(dst[:, :, sft:8], src[:, :, sft:8], src[:, :, 0:8 - sft], ALU.add)
                    src, dst = dst, (cv if dst is cu else cu)
                V(lambda e: e.tensor_reduce(s1, gt_, AX.X, ALU.add))
                for t in range(2):
                    vts(src[:, t, :], src[:, t, :], s1[:, t:t + 1], 2.0, ALU.add, ALU.is_le)
                vtt(eq, eq, src, ALU.mult)
                vtt(eq, eq, gt_, ALU.add)
                vtt(ex, ex, eq, ALU.mult, c)
                V(lambda e: e.tensor_reduce(s1, ex, AX.X, ALU.add))
                recip(s1, s1)
                for t in range(2):
                    v = vts(ex[:, t, :], ex[:, t, :], s1[:, t:t + 1], None, ALU.mult)
                bank, free = PB.take()
                for t in range(2):
                    tok = tr(bank[0:8, 128 * t:128 * t + 128], ex[:, t, :], 128, v, free)
                gT = sq[0:8, 0:S]
                v = vcopy(gT, bank[0:8, 0:S], tok, P.last)
                PB.give(bank, v)
                gates = W2[:, 0:8 * S].rearrange("p (h t) -> p h t", t=S)
                for h in range(NE):
                    bank, free = PB.take()
                    tok = mm(bank[:, 0:S], C("ident", h, 1, 8).to_broadcast([8, 128]), gT, True, True, v, free)
                    gt_ready = act(gates[:, h, :], bank[:, 0:S], ACT.Copy, tok, free=True)
                    PB.give(bank, gt_ready)
                for ex_i in range(NE):
                    h_ready = {}
                    free_ff = P.last

                    def pair(j, ba, ta, bb, tb_):
                        s_, tf = tmp.take()
                        c = act(s_[:, 0:S], ba[:, 0:S], ACT.Silu, ta, tf, free=True)
                        PB.give(ba, c)
                        v = vtt(s_[:, 0:S], s_[:, 0:S], bb[:, 0:S], ALU.mult, c, tb_, free=True)
                        PB.give(bb, v)
                        v = vtt(hT[:, j, NM:T2], s_[:, 0:S], gates[:, ex_i, :], ALU.mult, free_ff, gt_ready)
                        tmp.give(s_, v)
                        h_ready[j] = v

                    ffn_in(a["w_exp_in"][ex_i], nX, x_ready, NM, T2, pair)

                    def down(g, ps, tk):
                        if ex_i == 0:
                            r_ready[g] = stt(r3[:, g, NM:T2], nX[:, g, NM:T2], ALPHA, ps, ALU.mult, ALU.add,
                                             tk, free=True)
                        else:
                            r_ready[g] = vtt(r3[:, g, NM:T2], r3[:, g, NM:T2], ps, ALU.add, tk, r_ready[g],
                                             free=True)
                        return r_ready[g]

                    ffn_out(a["w_exp_out"][ex_i], h_ready, NM, T2, down)
                x_ready = layer_norm("ln_ffn_g", "ln_ffn_b", layer, hX, r_ready)

        h_rdy = [list(flat([x_ready[k], inputs])) for k in range(KT)]
        tiles = [M_, A_, B_]
        for layer in range(2):
            n_ready = rms_norm("norm_mix", layer, hX, nX, h_rdy)
            ns = lambda k: nX[:, k, :]
            w = a["w_in_2"][layer]
            free_w = [P.last, V.last, A.last]
            o = 0

            def area(n):
                nonlocal o
                if o < FT * T2 and o + n > FT * T2:
                    o = FT * T2
                r = W1[:, o:o + n] if o < FT * T2 else W2[:, o - FT * T2:o - FT * T2 + n]
                o += n
                return r

            qkv = area(12 * T2).rearrange("p (k t) -> p k t", t=T2)
            zz = area(4 * T2).rearrange("p (k t) -> p k t", t=T2)
            ktok = area(3 * 512).rearrange("p (t h n) -> p t h n", t=3, h=4)
            vtok = area(3 * 512).rearrange("p (t h n) -> p t h n", t=3, h=4)

            def conv(key, ps, tk):
                dst = qkv[:, key, :]
                cw = lambda i: C("conv_a", (layer * 12 + key) * 4 + i, 1)
                v = vts(dst, ps, cw(3), None, ALU.mult, None, tk, free_w)
                for i in (2, 1, 0):
                    d = 3 - i
                    v = stt(dst[:, d:T2], ps[:, 0:T2 - d], cw(i), dst[:, d:T2], ALU.mult, ALU.add)
                act(dst, dst, ACT.Silu, v, free=True)
                return v

            for c in range(3):
                product(cols(w, 512 * c, 512 * c + 512), [(128 * i, 128, 4 * c + i) for i in range(4)], ns, KT,
                        0, T2, n_ready if c == 0 else None, conv)
            product(cols(w, 1536, 2048), [(128 * i, 128, i) for i in range(4)], ns, KT, 0, T2, None,
                    lambda key, ps, tk: act(zz[:, key, :], ps, ACT.Silu, tk, free_w, free=True))
            silu_done = A.last
            lds = cols(w, 2560, 2560 + 400)
            sml = sm[:, 320:368].rearrange("p (t n) -> p t n", t=3)
            rows(lds, 384, 16, ns, KT, tiles, None,
                 lambda i, ps, tk: vcopy(sml[0:ps.shape[0], i, :], ps, tk, free_w))
            gb = sm[:, 368:380].rearrange("p (t n) -> p t n", t=3)
            be = sm[:, 380:392].rearrange("p (t n) -> p t n", t=3)
            sa = sm[:, 392:404].rearrange("p (t n) -> p t n", t=3)
            gc = sm[:, 404:416].rearrange("p (t n) -> p t n", t=3)
            ge = sm[:, 416:428].rearrange("p (t n) -> p t n", t=3)
            gl = sm[:, 428:440].rearrange("p (t n) -> p t n", t=3)
            gk = sm[:, 440:452].rearrange("p (t n) -> p t n", t=3)
            ea = sm[:, 452:456]
            c = act(ea, C("a_log", 4 * layer, 4), ACT.Exp, V.last)
            for t, (t0, t1) in enumerate(tiles):
                n = t1 - t0
                v = vtt(gb[0:n, t, :], sml[0:n, t, 0:4], C("dt_bias", 4 * layer, 4)[0:n, :], ALU.add)
                c = act(sa[0:n, t, :], gb[0:n, t, :], ACT.Abs, v)
                c = act(sa[0:n, t, :], sa[0:n, t, :], ACT.Exp, scale=-1.0)
                c = act(sa[0:n, t, :], sa[0:n, t, :], ACT.Ln, bias=1.0)
                v = stt(gb[0:n, t, :], gb[0:n, t, :], 0.0, sa[0:n, t, :], ALU.max, ALU.add, c)
                v = stt(gb[0:n, t, :], gb[0:n, t, :], -1.0, ea[0:n, :], ALU.mult, ALU.mult)
                c = act(be[0:n, t, :], sml[0:n, t, 4:8], ACT.Exp, scale=-1.0)
                vts(be[0:n, t, :], be[0:n, t, :], 1.0, None, ALU.add, None, c)
                v = recip(be[0:n, t, :], be[0:n, t, :])
                bank, free = PB.take()
                mm(bank[0:n, 0:4], C("upper", 0, n, n), gb[0:n, t, :], True, False, v, free,
                   skip_group_check=True)
                tok = mm(bank[:, 16:20], C("ones", 0, 128, n), gb[0:n, t, :], False, True,
                         skip_group_check=True)
                v = vcopy(gc[0:n, t, :], bank[0:n, 0:4], tok)
                v = vtt(gk[0:n, t, :], bank[0:n, 16:20], gc[0:n, t, :], ALU.subtract)
                c = act(gl[:, t, :], bank[:, 16:20], ACT.Exp, v)
                PB.give(bank, v, c)
                act(gk[0:n, t, :], gk[0:n, t, :], ACT.Exp)
                c = act(ge[0:n, t, :], gc[0:n, t, :], ACT.Exp)
                v = vtt(ge[0:n, t, :], ge[0:n, t, :], be[0:n, t, :], ALU.mult, c)

            def col_stats(src, n, scale, eps, after):
                bank, free = PB.take()
                for i in range(n):
                    s_, tf = tmp.take()
                    c = act(s_, src(i), ACT.Square, tf, after)
                    m = mm(bank[0:n, 0:T2], C("colsel", 7 - i, n), s_, i == 0, i == n - 1, c,
                           free if i == 0 else None)
                    tmp.give(s_, m)
                rt, rf = tmp2.take()
                c = act(rt[0:n, :], bank[0:n, 0:T2], ACT.Sqrt, m, rf, scale=scale, bias=eps[0:n, :])
                PB.give(bank, c)
                v = recip(rt[0:n, :], rt[0:n, :], c)
                return rt, v

            def spread(rt, n, i, after):
                bank, free = PB.take()
                m = mm(bank[:, 0:T2], C("ident", i, 1, n).to_broadcast([n, 128]), rt[0:n, :], True, True, after,
                       free)
                return bank, m

            rt, v = col_stats(lambda i: qkv[:, i, :], 8, 1.0, C("eps6"), silu_done)
            for i in range(8):
                bank, m = spread(rt, 8, i, v)
                s = BSCALE if i < 4 else 1.0
                v2 = stt(qkv[:, i, :], qkv[:, i, :], s, bank[:, 0:T2], ALU.mult, ALU.mult, m)
                PB.give(bank, v2)
            tmp2.give(rt, P.last)
            for t, (t0, t1) in enumerate(tiles):
                n = t1 - t0
                for which, dst in ((4, ktok), (8, vtok)):
                    bank, free = PB.take()
                    for h in range(4):
                        tok = tr(bank[0:n, 128 * h:128 * h + 128], qkv[:, which + h, t0:t1], 128, free, v2,
                                 silu_done)
                    v = vcopy(dst[0:n, t, :, :], bank[0:n, :].rearrange("p (h n) -> p h n", h=4), tok)
                    PB.give(bank, v)

            oA = mX[:, 0:4, :]
            o_base = o
            W = [W2[:, 7700 - 512 * (i + 1):7700 - 512 * i] for i in range(9)] + \
                [rX[:, 512 * i:512 * i + 512] for i in range(4)] + [sq[:, 512 * i:512 * i + 512] for i in range(4)]
            assert o - FT * T2 <= 7700 - 9 * 512
            hs = [x.rearrange("p (h n) -> p h n", h=4) for x in W]
            Mm, DT, MT, X, XT, Yb, CT, EG, kb, vb, kd, wT, u, QK, St, Gd, qe = hs
            smask = C("lm")
            tiles_free = [P.last]
            for t, (t0, t1) in enumerate(tiles):
                n = t1 - t0
                for h in range(4):
                    v = vts(Gd[0:n, h, 0:n], C("upper", 0, n, n), gb[0:n, t, h:h + 1], None, ALU.mult, None,
                            P.last if h == 0 else None)
                bank, free = PB.take()
                g3 = bank[:, :].rearrange("p (h n) -> p h n", h=4)
                for h in range(4):
                    tok = mm(g3[:, h, 0:n], C("ones", 0, 128, n), Gd[0:n, h, 0:n], h == 0, h == 3, v, free,
                             skip_group_check=True)
                for h in range(4):
                    stt(Mm[0:n, h, 0:n], g3[0:n, h, 0:n], gc[0:n, t, h:h + 1], C("um", 0, n, n), ALU.subtract,
                        ALU.add, tok)
                    v = stt(DT[0:n, h, 0:n], g3[0:n, h, 0:n], gc[0:n, t, h:h + 1], C("umt", 0, n, n),
                            ALU.subtract, ALU.add)
                c1 = act(EG[:, :, 0:n], g3[:, :, 0:n], ACT.Exp, v, P.last)
                PB.give(bank, c1)
                act(Mm[0:n, :, 0:n], Mm[0:n, :, 0:n], ACT.Exp, scale=-1.0)
                c = act(DT[0:n, :, 0:n], DT[0:n, :, 0:n], ACT.Exp)
                bank, free = PB.take()
                k3 = bank[:, :].rearrange("p (h n) -> p h n", h=4)
                for h in range(4):
                    tok = mm(k3[0:n, h, 0:n], qkv[:, 4 + h, t0:t1], qkv[:, 4 + h, t0:t1], h == 0, h == 3, free,
                             skip_group_check=True)
                for h in range(4):
                    v = stt(Mm[0:n, h, 0:n], k3[0:n, h, 0:n], be[0:n, t, h:h + 1], Mm[0:n, h, 0:n], ALU.mult,
                            ALU.mult, tok, c)
                PB.give(bank, v)
                bank, free = PB.take()
                m3 = bank[:, :].rearrange("p (h n) -> p h n", h=4)
                for h in range(4):
                    tok = tr(m3[0:n, h, 0:n], Mm[0:n, h, 0:n], n, v, free)
                c = act(MT[0:n, :, 0:n], m3[0:n, :, 0:n], ACT.Copy, tok)
                PB.give(bank, c)
                lb = lambda nm, l: C(nm, 128 * l, n, n).unsqueeze(1).to_broadcast([n, 4, n])
                ib = C("ident", 0, n, n).unsqueeze(1).to_broadcast([n, 4, n])
                vtt(X[0:n, :, 0:n], Mm[0:n, :, 0:n], lb("lm", 0), ALU.mult, P.last)
                vtt(X[0:n, :, 0:n], ib, X[0:n, :, 0:n], ALU.subtract)
                vtt(XT[0:n, :, 0:n], MT[0:n, :, 0:n], lb("lmt", 0), ALU.mult, c)
                x_tok = vtt(XT[0:n, :, 0:n], ib, XT[0:n, :, 0:n], ALU.subtract)
                levels = 7 if n == 128 else 4
                for l in range(1, levels):
                    gct = vtt(CT[0:n, :, 0:n], MT[0:n, :, 0:n], lb("lmt", l), ALU.mult, c, P.last, q=G)
                    bank, free = PB.take()
                    b3 = bank[:, :].rearrange("p (h n) -> p h n", h=4)
                    for h in range(4):
                        tok = mm(b3[0:n, h, 0:n], CT[0:n, h, 0:n], X[0:n, h, 0:n], h == 0, h == 3, gct, x_tok,
                                 free, skip_group_check=True)
                    cy = act(Yb[0:n, :, 0:n], b3[0:n, :, 0:n], ACT.Copy, tok)
                    PB.give(bank, cy)
                    bank2, free2 = PB.take()
                    b4 = bank2[:, :].rearrange("p (h n) -> p h n", h=4)
                    for h in range(4):
                        tok2 = mm(b4[0:n, h, 0:n], Yb[0:n, h, 0:n], XT[0:n, h, 0:n], h == 0, h == 3, cy, free2,
                                  skip_group_check=True)
                    if l < levels - 1:
                        bank, free = PB.take()
                        b5 = bank[:, :].rearrange("p (h n) -> p h n", h=4)
                        for h in range(4):
                            tok = mm(b5[0:n, h, 0:n], XT[0:n, h, 0:n], Yb[0:n, h, 0:n], h == 0, h == 3, cy,
                                     free, skip_group_check=True)
                        v = vtt(X[0:n, :, 0:n], X[0:n, :, 0:n], b5[0:n, :, 0:n], ALU.subtract, tok)
                        PB.give(bank, v)
                        tok2 = [tok2, tok]
                    x_tok = vtt(XT[0:n, :, 0:n], XT[0:n, :, 0:n], b4[0:n, :, 0:n], ALU.subtract, tok2)
                    PB.give(bank2, x_tok)
                for h in range(4):
                    vts(vb[0:n, h, :], vtok[0:n, t, h, :], be[0:n, t, h:h + 1], None, ALU.mult, free=h > 0)
                    vts(kb[0:n, h, :], ktok[0:n, t, h, :], ge[0:n, t, h:h + 1], None, ALU.mult, free=True)
                    v = vts(kd[0:n, h, :], ktok[0:n, t, h, :], gk[0:n, t, h:h + 1], None, ALU.mult, None, A.last,
                            free=True)
                v = vtt(qe[:, :, 0:n], qkv[:, 0:4, t0:t1], EG[:, :, 0:n], ALU.mult, c1, free=True)
                bank, free = PB.take()
                u3 = bank[:, :].rearrange("p (h n) -> p h n", h=4)
                for h in range(4):
                    tok = mm(u3[0:n, h, :], XT[0:n, h, 0:n], vb[0:n, h, :], h == 0, h == 3, v, free,
                             skip_group_check=True)
                c = act(u[0:n, :, :], u3[0:n, :, :], ACT.Copy, tok)
                PB.give(bank, c)
                if t > 0:
                    bank, free = PB.take()
                    w3 = bank[:, :].rearrange("p (h n) -> p h n", h=4)
                    for h in range(4):
                        tok = mm(w3[:, h, 0:n], kb[0:n, h, :], XT[0:n, h, 0:n], h == 0, h == 3, free,
                                 skip_group_check=True)
                    c = act(wT[:, :, 0:n], w3[:, :, 0:n], ACT.Copy, tok)
                    PB.give(bank, c)
                bank, free = PB.take()
                q3_ = bank[:, :].rearrange("p (h n) -> p h n", h=4)
                for h in range(4):
                    tok = mm(q3_[0:n, h, 0:n], qkv[:, 4 + h, t0:t1], qkv[:, h, t0:t1], h == 0, h == 3, free,
                             skip_group_check=True)
                v = vtt(QK[0:n, :, 0:n], q3_[0:n, :, 0:n], DT[0:n, :, 0:n], ALU.mult, tok)
                PB.give(bank, v)
                if t > 0:
                    bank, free = PB.take()
                    s3 = bank[:, :].rearrange("p (h n) -> p h n", h=4)
                    for h in range(4):
                        tok = mm(s3[0:n, h, :], wT[:, h, 0:n], St[:, h, :], h == 0, h == 3, free, c, v,
                                 skip_group_check=True)
                    v = vtt(u[0:n, :, :], u[0:n, :, :], s3[0:n, :, :], ALU.subtract, tok)
                    PB.give(bank, v)
                bank, free = PB.take()
                o3 = bank[:, :].rearrange("p (h n) -> p h n", h=4)
                for h in range(4):
                    if t > 0:
                        mm(o3[:, h, 0:n], St[:, h, :], qe[:, h, 0:n], h == 0, False, free, v,
                           skip_group_check=True)
                    tok = mm(o3[:, h, 0:n], u[0:n, h, :], QK[0:n, h, 0:n], t == 0 and h == 0, h == 3, free, v,
                             c, skip_group_check=True)
                v2 = vcopy(oA[:, :, t0:t1], o3[:, :, 0:n], tok)
                PB.give(bank, v2)
                if t < 2:
                    bank, free = PB.take()
                    d3 = bank[:, :].rearrange("p (h n) -> p h n", h=4)
                    for h in range(4):
                        tok = mm(d3[:, h, :], kd[0:n, h, :], u[0:n, h, :], h == 0, h == 3, free, v,
                                 skip_group_check=True)
                    for h in range(4):
                        if t == 0:
                            v = vcopy(St[:, h, :], d3[:, h, :], tok)
                        else:
                            v = stt(St[:, h, :], St[:, h, :], gl[:, t, h:h + 1], d3[:, h, :], ALU.mult,
                                    ALU.add, tok)
                    PB.give(bank, v)
            rt, v = col_stats(lambda i: oA[:, i, :], 4, 1.0 / 128, C("eps6"), V.last)
            for i in range(4):
                bank, m = spread(rt, 4, i, v)
                v2 = stt(oA[:, i, :], oA[:, i, :], C("a_out_norm", layer, 1), bank[:, 0:T2], ALU.mult,
                         ALU.mult, m)
                PB.give(bank, v2)
                v2 = vtt(oA[:, i, :], oA[:, i, :], zz[:, i, :], ALU.mult, silu_done)
            tmp2.give(rt, P.last)
            oa_ready = v2

            free_w = [P.last, V.last, A.last, G.last]
            o = 0
            qb = area(4 * T2).rearrange("p (k t) -> p k t", t=T2)
            kb_ = area(T2)
            iq = area(4 * T2).rearrange("p (k t) -> p k t", t=T2)
            ik = area(T2)
            vv = area(3 * 128).rearrange("p (t n) -> p t n", t=3)
            score = area(S)
            work = area(2 * S).rearrange("p (a n) -> p a n", a=2)
            smk = area(2 * T2).rearrange("p (a n) -> p a n", a=2)

            def rope2(src, rot, cos, sin, after):
                bank, free = PB.take()
                m = mm(bank[:, 0:T2], C(rot), src, True, True, after, free)
                t2, tf = tmp.take()
                v = vtt(t2, bank[:, 0:T2], C(sin), ALU.mult, m, tf)
                PB.give(bank, v)
                vtt(src, src, C(cos), ALU.mult, m)
                v = vtt(src, src, t2, ALU.add)
                tmp.give(t2, v)
                return v

            def raw(dst):
                return lambda key, ps, tk: act(dst if key is None else dst[:, key, :], ps, ACT.Copy, tk, free_w,
                                               free=True)

            product(cols(w, 2048, 2560), [(128 * i, 128, i) for i in range(4)], ns, KT, 0, T2, None, raw(qb))
            product(cols(w, 2960, 3472), [(128 * i, 128, i) for i in range(4)], ns, KT, 0, T2, None, raw(iq))
            rows(lds, 256, 128, ns, KT, tiles, None,
                 lambda i, ps, tk: vcopy(vv[0:ps.shape[0], i, :], ps, tk, free_w))
            for c0, d_ in ((0, kb_), (128, ik)):
                bank, free = PB.take()
                tok = group(bank, 128, 0, T2, lds.w, c0, ns, KT, [free, lds.ready])
                PB.give(bank, act(d_, bank[:, 0:T2], ACT.Copy, tok, free_w, free=True))
            lds.done(tok)
            raws = A.last
            rt, v = col_stats(lambda i: qb[:, i, :] if i < 4 else kb_, 5, 1.0 / 128, C("eps6"), raws)
            for i in range(5):
                dst = qb[:, i, :] if i < 4 else kb_
                bank, m = spread(rt, 5, i, v)
                v2 = stt(dst, dst, C("q_norm" if i < 4 else "k_norm", layer, 1), bank[:, 0:T2], ALU.mult,
                         ALU.mult, m)
                PB.give(bank, v2)
            tmp2.give(rt, P.last)
            s_, tf = tmp.take()
            c = act(s_, ik, ACT.Square, tf, raws)
            bank, free = PB.take()
            m = mm(bank[:, 0:T2], C("mean64"), s_, True, True, c, free)
            c = act(s_, bank[:, 0:T2], ACT.Sqrt, m, bias=C("eps6"))
            PB.give(bank, c)
            v = recip(s_, s_, c)
            v = stt(ik, ik, C("kidx", layer, 1), s_, ALU.mult, ALU.mult)
            tmp.give(s_, v)
            for i in range(4):
                rope2(qb[:, i, :], "rota", "cosa", "sina", v)
            rope2(kb_, "rota", "cosa", "sina", v)
            for i in range(4):
                rope2(iq[:, i, :], "roti", "cosi", "sini", v)
            roped2 = rope2(ik, "roti", "cosi", "sini", v)
            IS = float(8 ** -0.5 * 64 ** -0.5)
            iwt = sm[:, 456:472].rearrange("p (t n) -> p t n", t=2)
            iw_tok = vts(iwt, sml[:, 1:3, 8:16], IS, None, ALU.mult)
            for t in (1, 2):
                t0, t1 = tiles[t]
                bks = [PB.take() for _ in range(4)]
                toks = []
                for h in range(8):
                    p0 = 64 * (h % 2)
                    b = 2 * (h // 4) + h % 2
                    bank, free = bks[b]
                    cc = 256 * ((h // 2) % 2)
                    toks.append(mm(bank[:, cc:cc + 256], iq[p0:p0 + 64, h // 2, t0:t1],
                                   ik[p0:p0 + 64, NM:T2], (h // 2) % 2 == 0, (h // 2) % 2 == 1, free, roped2,
                                   skip_group_check=True))
                for h in range(8):
                    b = 2 * (h // 4) + h % 2
                    cc = 256 * ((h // 2) % 2)
                    src = bks[b][0][:, cc:cc + 256]
                    if h == 0:
                        v = vts(score, src, 0.0, iwt[:, t - 1, h:h + 1], ALU.max, ALU.mult, toks, free_w)
                    else:
                        s_, tf = tmp.take()
                        v = vts(s_[:, 0:S], src, 0.0, iwt[:, t - 1, h:h + 1], ALU.max, ALU.mult, tf)
                        v = vtt(score, score, s_[:, 0:S], ALU.add)
                        tmp.give(s_, v)
                for bank, _ in bks:
                    PB.give(bank, v)
                vtt(score, score, C("valid", 256 * (t - 1), 256), ALU.add)
                cur = score
                mx8 = sm[:, 472:480]
                for r in range(8):
                    nxt = work[:, r % 2, :]
                    V(lambda e, cur=cur: e.max(mx8, cur))
                    V(lambda e, cur=cur, nxt=nxt: e.match_replace(nxt, mx8, cur, -3e38))
                    cur = nxt
                V(lambda e, t=t: e.memset(smk[:, t - 1, 0:NM], 0.0))
                vtt(smk[:, t - 1, NM:T2], cur, score, ALU.is_equal)
                sel = vts(smk[:, t - 1, NM:T2], smk[:, t - 1, NM:T2], -BIG, None, ALU.mult)

            units = [(h, t) for t in (1, 2) for h in range(4)] + [(h, 0) for h in range(4)]
            ob = {}
            st = {}
            n_u = len(units)
            for i in range(n_u + 2):
                if i < n_u:
                    h, t = units[i]
                    t0, t1 = tiles[t]
                    n = t1 - t0
                    nk = T2 if t else NM
                    bank, free = PB.take()
                    tok = mm(bank[0:n, 0:nk], qb[:, h, t0:t1], kb_[:, 0:nk], True, True, free, roped2)
                    sc, f = sc_slots.take()
                    s2, f2 = st_slots.take()
                    if t:
                        v = stt(sc[0:n, 0:nk], bank[0:n, 0:nk], BSCALE, smk[0:n, t - 1, :], ALU.mult, ALU.add,
                                tok, f, sel, free_w)
                    else:
                        v = vts(sc[0:n, 0:nk], bank[0:n, 0:nk], BSCALE, None, ALU.mult, None, tok, f, free_w)
                    PB.give(bank, v)
                    v = V(lambda e, a_=s2[0:n, 0:1], b_=sc[0:n, 0:nk]: e.tensor_reduce(a_, b_, AX.X, ALU.max,
                                                                                     negate=True), f2)
                    c = act(sc[0:n, 0:nk], sc[0:n, 0:nk], ACT.Exp, v, bias=s2[0:n, 0:1],
                            accum_out=s2[0:n, 1:2])
                    recip(s2[0:n, 1:2], s2[0:n, 1:2], c)
                    v = vts(sc[0:n, 0:nk], sc[0:n, 0:nk], s2[0:n, 1:2], None, ALU.mult)
                    st_slots.give(s2, v)
                    st[i] = (sc, v)
                if 1 <= i <= n_u:
                    h, t = units[i - 1]
                    t0, t1 = tiles[t]
                    n = t1 - t0
                    sc, v = st[i - 1]
                    bank, free = PB.take()
                    pt, f = pt_slots.take()
                    for j, (k0, k1) in enumerate(tiles if t else tiles[:1]):
                        tok = tr(bank[0:k1 - k0, 128 * j:128 * j + n], sc[0:n, k0:k1], n,
                                 [free, v])
                    sc_slots.give(sc, tok)
                    c = act(pt[0:NM, 0:n], bank[0:NM, 0:n], ACT.Copy, tok, f, free_w)
                    if t:
                        c = act(pt[:, 128:384], bank[:, 128:384], ACT.Copy)
                    PB.give(bank, c)
                    st[i - 1] = (pt, c)
                if i >= 2:
                    h, t = units[i - 2]
                    t0, t1 = tiles[t]
                    n = t1 - t0
                    pt, c = st[i - 2]
                    bank, free = PB.take()
                    kts = tiles if t else tiles[:1]
                    for j, (k0, k1) in enumerate(kts):
                        tok = mm(bank[:, 0:n], vv[0:k1 - k0, j, :], pt[0:k1 - k0, 128 * j:128 * j + n], j == 0,
                                 j == len(kts) - 1, free, c)
                    pt_slots.give(pt, tok)
                    v = vcopy(mX[:, 4 + h, t0:t1], bank[:, 0:n], tok)
                    PB.give(bank, v)
            ob_ready = V.last

            ygate = W2[:, 0:8 * T2].rearrange("p (k t) -> p k t", t=T2)
            wg = a["w_gate"][layer]
            y_ready = {}
            free_y = [P.last, V.last]
            for half in range(2):
                g0 = cols(wg, 512 * half, 512 * half + 512)
                g1 = cols(wg, 1024 + 512 * half, 1024 + 512 * half + 512)
                br = [cols(a["w_branch_a"][layer], 512 * half, 512 * half + 512),
                      cols(a["w_branch_b"][layer], 512 * half, 512 * half + 512)]
                for i in range(4):
                    g = 4 * half + i
                    res2 = []
                    for z, ld in enumerate((g0, g1)):
                        bank, free = PB.take()
                        tok = group(bank, 128, 0, T2, ld.w, 128 * i, ns, KT, [free, ld.ready])
                        s_, tf = tmp.take()
                        c = act(s_, bank[:, 0:T2], ACT.Sigmoid, tok, tf, bias=C("b_gate", 16 * layer + 8 * z + g, 1))
                        PB.give(bank, c)
                        bank, free = PB.take()
                        tok = group(bank, 128, 0, T2, br[z].w, 128 * i, lambda k, z=z: mX[:, 4 * z + k, :], 4,
                                    [free, br[z].ready, oa_ready, ob_ready])
                        v = vtt(s_, s_, bank[:, 0:T2], ALU.mult, c, tok)
                        PB.give(bank, v)
                        res2.append(s_)
                    y_ready[g] = vtt(ygate[:, g, :], res2[0], res2[1], ALU.add, free_y)
                    for s_ in res2:
                        tmp.give(s_, y_ready[g])
                for ld in (g0, g1, *br):
                    ld.done(P.last)
            h_rdy = {}

            def addh(key, ps, tk):
                h_rdy[key] = vtt(hX[:, key, :], hX[:, key, :], ps, ALU.add, tk, free=True)
                return h_rdy[key]

            for c in range(2):
                product(cols(a["w_out_2"][layer], 512 * c, 512 * c + 512),
                        [(128 * i, 128, 4 * c + i) for i in range(4)], lambda k: ygate[:, k, :], KT, 0, T2,
                        [y_ready[g] for g in range(8)], addh)
            n_ready = rms_norm("norm_ffn", layer, hX, nX, h_rdy)
            h_ready = {}
            free_ff = [P.last, V.last, A.last]

            def pair2(j, ba, ta, bb, tb_):
                s_, tf = tmp.take()
                cw = lambda i: C("conv_ffn", (layer * 22 + j) * 3 + i, 1)
                vts(s_, ba[:, 0:T2], cw(2), None, ALU.mult, None, ta, tf)
                stt(s_[:, 1:T2], ba[:, 0:T2 - 1], cw(1), s_[:, 1:T2], ALU.mult, ALU.add)
                v = stt(s_[:, 2:T2], ba[:, 0:T2 - 2], cw(0), s_[:, 2:T2], ALU.mult, ALU.add)
                PB.give(ba, v)
                c = act(s_, s_, ACT.Silu, v, free=True)
                v = vtt(hT[:, j, :], s_, bb[:, 0:T2], ALU.mult, c, tb_, free_ff)
                PB.give(bb, v)
                tmp.give(s_, v)
                h_ready[j] = v

            ffn_in(a["w_up"][layer], nX, n_ready, 0, T2, pair2)
            ffn_out(a["w_down"][layer], h_ready, 0, T2, addh)

        n_out = 0
        for k in range(KT):
            n_out += 16
            last = dma(Y, a["out"][:, k, :], hX[:, k, NM:T2], s_out, n_out, h_rdy[k])
        Y.ops.append((None, [last], Token(None, 0), 0))

        number([P, V, A, G, Y])
        block = ctx.enter_context(nc.Block())

        @block.sync
        def _(eng):
            Y.emit(eng)

        @block.gpsimd
        def _(eng):
            G.emit(eng)

        @block.scalar
        def _(eng):
            A.emit(eng)

        @block.tensor
        def _(eng):
            P.emit(eng)

        @block.vector
        def _(eng):
            V.emit(eng)


def _pack(inp):
    pk = np.zeros((128, NPACK), np.float32)

    def put(name, v):
        v = np.asarray(v)
        v = v.reshape(v.shape[0], -1)
        pk[0:v.shape[0], AT[name]:AT[name] + v.shape[1]] = v

    i, j = np.arange(128)[:, None], np.arange(128)[None, :]
    put("ident", np.eye(128))
    put("ones", np.ones((128, 128)))
    put("mean", np.full((128, 128), 1 / 1024))
    put("mean128", np.full((128, 128), 1 / 128))
    put("mean64", np.where(i // 64 == j // 64, 1 / 64, 0))
    put("upper", i <= j)
    q = np.arange(256).reshape(2, 128).T[:, :, None]
    k = np.arange(256)[None, None, :]
    put("swa", np.where((k // 64 <= q // 64) & (k // 64 >= q // 64 - 2), 0, -BIG))
    put("causal", np.where(k <= q, 0, -BIG))
    put("valid", np.where(k < (q // 64 + 1) * 64, 0, -BIG))
    rot = np.zeros((128, 128))
    for h in range(2):
        for d in range(8):
            rot[64 * h + d + 8, 64 * h + d] = -1
            rot[64 * h + d, 64 * h + d + 8] = 1
    put("rot1", rot)
    rot = np.zeros((128, 128))
    for d in range(64):
        rot[d + 64, d] = -1
        rot[d, d + 64] = 1
    put("rota", rot)
    rot = np.zeros((128, 128))
    for h in range(2):
        for d in range(32):
            rot[64 * h + d + 32, 64 * h + d] = -1
            rot[64 * h + d, 64 * h + d + 32] = 1
    put("roti", rot)
    for nm, dim in (("a", 128), ("i", 64)):
        inv = (1.0 / (np.float32(10000.0) ** (np.arange(0, dim, 2, dtype=np.float32) / np.float32(dim)))).astype(
            np.float32)
        ang = (np.arange(T2, dtype=np.float32)[None, :] * inv[:, None]).astype(np.float32).astype(np.float64)
        ang = np.concatenate([ang] * (256 // dim))
        put("cos" + nm, np.cos(ang))
        put("sin" + nm, np.sin(ang))
    put("um", np.where(j > i, BIG, 0))
    put("umt", np.where(j < i, -BIG, 0))
    lm = np.zeros((128, 7, 128))
    for l in range(7):
        b = 1 << l
        lm[:, l] = (i // (2 * b) == j // (2 * b)) & (i // b % 2 == 1) & (j // b % 2 == 0)
    put("lm", lm)
    put("lmt", lm.transpose(2, 1, 0))
    put("colsel", np.broadcast_to(np.arange(15) == 7, (128, 15)))
    f = np.zeros((128, 1), np.float32)
    for h in range(2):
        for d in range(16):
            f[64 * h + d] = INV1[d % 8]
    put("inv1", f)
    put("eps5", np.full((128, 1), 1e-5))
    put("eps6", np.full((128, 1), 1e-6))

    def feat(x):
        x = np.asarray(x)
        return np.moveaxis(x.reshape(x.shape[:-1] + (-1, 128)), -1, 0)

    for nm in ("ln_attn_g", "ln_attn_b", "ln_ffn_g", "ln_ffn_b"):
        put(nm, feat(inp[nm]))
    put("norm_mix", feat(inp["norm_mix_2"]))
    put("norm_ffn", feat(inp["norm_ffn_2"]))

    def over(x):
        return np.broadcast_to(np.asarray(x).reshape(1, -1), (128, np.asarray(x).size))

    put("sinks", over(inp["attn_sinks"]))
    put("b_forget", over(inp["b_forget"]))
    put("b_router", over(inp["b_router"]))
    put("a_log", over(inp["a_log_2"]))
    put("dt_bias", over(inp["dt_bias_2"]))
    put("conv_a", np.asarray(inp["conv_a_2"]).reshape(2, 4, 12, 128).transpose(3, 0, 2, 1))
    put("conv_ffn", np.asarray(inp["conv_ffn_2"]).reshape(2, 3, 22, 128).transpose(3, 0, 2, 1))
    put("a_out_norm", feat(inp["a_out_norm_2"]))
    put("q_norm", feat(inp["q_norm_2"]))
    put("k_norm", feat(inp["k_norm_2"]))
    kx = np.asarray(inp["kidx_norm_2"]).T
    put("kidx", np.concatenate([kx, kx]))
    put("b_gate", feat(inp["b_gate_2"]))
    return pk


def _arrays(inp):
    c = np.ascontiguousarray
    f = lambda n: np.asarray(inp[n])

    def tokens(x):
        return c(x.reshape(x.shape[0], 8, 128).transpose(2, 1, 0))

    def down(w):
        lead = w.shape[:-2]
        w = w.reshape(lead + (22, 128, 8, 128))
        n = len(lead)
        return c(w.transpose(tuple(range(n)) + (n + 2, n + 1, n, n + 3)))

    w = f("w_in_swa")[0]
    kd = [w[:, 768 + 64 * h:832 + 64 * h] for h in range(3) for _ in range(2)]
    w_swa = np.concatenate([w[:, 0:768]] + kd + [w[:, 1152:1408], w[:, 960:1152]], axis=1)
    w2 = f("w_in_2")
    w_in_2 = np.concatenate([w2[:, :, 0:2048], w2[:, :, 2056:2568], w2[:, :, 2568:2696], w2[:, :, 3336:3400],
                             w2[:, :, 3336:3400], w2[:, :, 2696:2824], w2[:, :, 2048:2056],
                             w2[:, :, 3400:3408], w2[:, :, 2824:3336]], axis=2)
    return {
        "pack": _pack(inp),
        "pos": c(np.broadcast_to(f("positions").reshape(1, S), (128, S))),
        "xT": tokens(f("x")[0]),
        "metaT": tokens(f("meta_tokens_2")),
        "memT": tokens(f("mem")[0]),
        "w_mem_kv": c(f("w_mem_kv")),
        "w_swa": c(w_swa),
        "w_fox": c(f("w_in_fox")[0]),
        "w_out": c(f("w_out")),
        "w_ffn_in": c(f("w_ffn_in")[0]),
        "w_ffn_out": down(f("w_ffn_out")[0]),
        "w_router": c(f("w_router")[0].reshape(8, 128, 8).transpose(1, 0, 2)),
        "w_exp_in": c(f("w_exp_in")[0]),
        "w_exp_out": down(f("w_exp_out")[0]),
        "w_in_2": c(w_in_2),
        "w_branch_a": c(f("w_branch_a_2")),
        "w_branch_b": c(f("w_branch_b_2")),
        "w_gate": c(f("w_gate_2")),
        "w_out_2": c(f("w_out_2")),
        "w_up": c(f("w_up_2")),
        "w_down": down(f("w_down_2")),
    }


def kernel(**inputs):
    import concourse.bacc as bacc
    from concourse.bass_utils import run_bass_kernel_spmd

    nc = bacc.Bacc("TRN2", target_bir_lowering=False, num_devices=1)
    arrays = _arrays(inputs)
    a = {}
    for name, x in arrays.items():
        a[name] = nc.dram_tensor(name, x.shape, mybir.dt.from_np(x.dtype), kind="ExternalInput").ap()
    a["out"] = nc.dram_tensor("out", (128, 8, S), F32, kind="ExternalOutput").ap()
    build(nc, a)
    r = run_bass_kernel_spmd(nc, [arrays], core_ids=[0])
    out = r.results[0]["out"]
    return np.ascontiguousarray(out.transpose(2, 1, 0).reshape(1, S, D))
```

```python
from contextlib import ExitStack

import numpy as np
import concourse.bass as bass
from concourse import mybir

F32 = mybir.dt.float32
F32R = mybir.dt.float32r
I32 = mybir.dt.int32
ALU = mybir.AluOpType
ACT = mybir.ActivationFunctionType
AX = mybir.AxisListType

D = 1024
KT = 8
S = 256
NM = 16
T2 = S + NM
FF = 2816
FT = FF // 128
NE = 8
DEPTH = 2
ALPHA = float((2.0 * DEPTH) ** 0.25)
SCALE = 0.125
BSCALE = float(128 ** -0.5)
BIG = 1e30
INV1 = [float.fromhex(x) for x in (
    '0x1.0000000000000p+0', '0x1.8d275e0000000p-3', '0x1.3411900000000p-5', '0x1.ddee9c0000000p-8',
    '0x1.72ba440000000p-10', '0x1.1f91f00000000p-12', '0x1.be21880000000p-15', '0x1.5a0f4e0000000p-17')]
TWO_PI_1 = 6.28125
TWO_PI_2 = float(np.float32(int((2 * np.pi - TWO_PI_1) * 2 ** 20) / 2 ** 20))
TWO_PI_3 = float(np.float32(2 * np.pi - TWO_PI_1 - TWO_PI_2))
MAGIC = 12582912.0

FIELDS = [
    ("ident", 128), ("ones", 128), ("mean", 128), ("iota", 128), ("slot", 1), ("mean64", 128), ("upper", 128),
    ("swa", 512), ("causal", 512), ("valid", 512), ("rot1", 128), ("rota", 128), ("roti", 128),
    ("cosa", T2), ("sina", T2), ("cosi", T2), ("sini", T2), ("um", 128), ("umt", 128),
    ("lm", 896), ("lmt", 896), ("colsel", 15), ("inv1", 1), ("eps5", 1), ("eps6", 1),
    ("ln_attn_g", 16), ("ln_attn_b", 16), ("ln_ffn_g", 16), ("ln_ffn_b", 16),
    ("norm_mix", 16), ("norm_ffn", 16), ("sinks", 12), ("b_forget", 12), ("b_router", 8),
    ("a_log", 8), ("dt_bias", 8), ("conv_a", 96), ("conv_ffn", 132), ("a_out_norm", 2),
    ("q_norm", 2), ("k_norm", 2), ("kidx", 2), ("b_gate", 32),
]
AT = {}
_n = 0
for _name, _w in FIELDS:
    AT[_name] = _n
    _n += _w
NPACK = _n

class Token:

    def __init__(self, sem, value=None):
        self.sem, self.value, self.used = sem, value, value is not None


class Queue:

    def __init__(self, sem, serial):
        self.sem, self.serial, self.ops, self.last = sem, serial, [], None

    def __call__(self, fn, *after, free=False):
        token = Token(self.sem)
        waits = flat(after)
        if self.serial and not free and self.last is not None:
            waits.append(self.last)
        self.ops.append((fn, waits, token, 1))
        self.last = token
        return token

    def branch(self, flag, after):
        b = Branch(flag, flat(after), Token(self.sem))
        self.ops.append(b)
        return b

    def emit(self, eng, ops=None, seen=None):
        ops, seen = (self.ops, {}) if ops is None else (ops, seen)

        def wait(tokens):
            need = {}
            for w in tokens:
                if w.value > need.get(w.sem, 0):
                    need[w.sem] = w.value
            for sem, value in need.items():
                if seen.get(sem, 0) < value:
                    eng.wait_ge(sem, value)
                    seen[sem] = value

        for op in ops:
            if isinstance(op, Branch):
                wait(op.waits)
                flag = eng.value_load(op.flag, min_val=0, max_val=1)
                entered = dict(seen)
                for guard, body, end in ((lambda: eng.If(flag > 0), op.taken, op.n_taken),
                                         (lambda: eng.Else(), op.other, op.n_other)):
                    with guard():
                        self.emit(eng, body, dict(entered))
                        if end < op.join.value:
                            eng.wait_ge(self.sem, end)
                            eng.sem_inc(self.sem, op.join.value - end)
                seen.clear()
                seen.update(entered)
                continue
            fn, waits, token, by = op
            wait(waits)
            if fn is None:
                continue
            ins = fn(eng)
            if token.used:
                ins.then_inc(token.sem, by)


class Branch:
    def __init__(self, flag, waits, join):
        self.flag, self.waits, self.join = flag, waits, join
        self.taken, self.other = [], []


def flat(xs):
    out = []
    for x in xs:
        if x is None:
            continue
        if isinstance(x, (list, tuple)):
            out += flat(x)
        else:
            out.append(x)
    return out


def number(queues):
    def mark(ops):
        for op in ops:
            if isinstance(op, Branch):
                for w in op.waits:
                    w.used = True
                for body in (op.taken, op.other):
                    mark(body)
                    [x for x in body if x[0] is not None][-1][2].used = True
            else:
                for w in op[1]:
                    w.used = True

    def count(ops, n):
        for op in ops:
            if isinstance(op, Branch):
                op.n_taken, op.n_other = count(op.taken, n), count(op.other, n)
                n = op.join.value = max(op.n_taken, op.n_other)
            elif op[3] == 1 and op[2].used and op[2].value is None:
                n += 1
                op[2].value = n
        return n

    for q in queues:
        mark(q.ops)
    for q in queues:
        count(q.ops, 0)


class Slots:

    def __init__(self, views):
        self.rows = [[v, []] for v in views]

    def take(self):
        row = self.rows.pop(0)
        return row[0], row[1]

    def give(self, view, *tokens):
        self.rows.append([view, flat(tokens)])

    def all_free(self, n):
        assert len(self.rows) == n
        for row in self.rows:
            row[1] = []


def build(nc, a):
    ctx = ExitStack()
    with ctx:
        def sb(name, shape, dt=F32):
            return ctx.enter_context(nc.sbuf_tensor(name, shape, dt))

        def sem(name):
            return ctx.enter_context(nc.semaphore(name))

        pk = sb("pk", [128, NPACK])
        NR = 4
        CH = 2048
        ring = [sb(f"ring{i}", [128, CH]) for i in range(NR)]
        wH = [sb(f"wH{i}", [128, CH], F32R) for i in range(2)]
        wL = [sb(f"wL{i}", [128, CH], F32R) for i in range(2)]
        hX = sb("hX", [128, KT, T2])
        nH = sb("nH", [128, KT, T2], F32R)
        nL = sb("nL", [128, KT, T2], F32R)
        rX = sb("rX", [128, KT * T2])
        sq = sb("sq", [128, KT * T2])
        mX = sb("mX", [128, KT, T2])
        TM = sb("TM", [128, 8, T2])
        sm = sb("sm", [128, 512])
        sb_flag = sb("flag", [128, 1], I32)
        sb_small = sb("small_w", [128, 96])
        base = (nc.sbuf_base + 31) // 32 * 32

        def at(name, shape, dt, off):
            return nc.alloc_sbuf_tensor_at(name, shape, dt, offset=base + 4 * off)

        NW2 = 7696
        W1 = at("W1", [128, FT * T2], F32, 0)
        W2 = at("W2", [128, NW2], F32, FT * T2)
        kv1 = at("kv1", [128, 1024], F32, FT * T2 + NW2)
        mH = at("mH", [128, KT, T2], F32R, FT * T2 + NW2 - 2 * KT * T2)
        mL = at("mL", [128, KT, T2], F32R, FT * T2 + NW2 - KT * T2)
        yH = at("yH", [128, KT, T2], F32R, 0)
        yL = at("yL", [128, KT, T2], F32R, KT * T2)
        hH = at("hH", [128, FT, T2], F32R, 0)
        hL = at("hL", [128, FT, T2], F32R, FT * T2)
        gts = at("gts", [128, NE, S], F32, 2 * FT * T2)
        xgH = at("xgH", [128, KT, 128], F32R, 0)
        xgL = at("xgL", [128, KT, 128], F32R, 1024)
        hgH = at("hgH", [128, FT, 128], F32R, 2048)
        hgL = at("hgL", [128, FT, 128], F32R, 2048 + FT * 128)
        Pg = at("Pg", [128, 2, 2, 128], F32, 2048 + 2 * FT * 128)
        Pt = at("Pt", [128, 2, 256], F32, 2560 + 2 * FT * 128)
        banks = [ctx.enter_context(nc.psum_tensor(f"pb{i}", [128, 512], F32)) for i in range(8)]

        P = Queue(sem("s_pe"), False)
        V = Queue(sem("s_dve"), True)
        A = Queue(sem("s_act"), True)
        G = Queue(sem("s_pool"), True)
        Y = Queue(sem("s_sp"), False)
        PB = Slots(banks)
        ring_sems = [sem(f"s_ring{i}") for i in range(NR)]
        s_raw = sem("s_raw")
        s_in = sem("s_in")
        s_out = sem("s_out")

        def C(name, i=0, w=None, p=128):
            o = AT[name] + i
            return pk[0:p, o:o + (w if w is not None else dict(FIELDS)[name])]

        def dma(queue, out, src, s, total, *after):
            token = Token(s, total)
            queue.ops.append((lambda e: e.dma_start(out, src), flat(after), token, 16))
            return token

        plan = []

        def cols(w, c0, c1):
            plan.append((w.rearrange("(k p) n -> p k n", p=128)[:, :, c0:c1], w.shape[0] // 128, c1 - c0, True))

        def laid(w, split=True):
            plan.append((w, w.shape[1], w.shape[2], split))

        def plan_down(w):
            for g in range(KT):
                for z in range(2):
                    laid(w[g, z])

        def plan_up(w):
            for u in range(FT // 2):
                for z in range(2):
                    laid(w[u, z])

        for layer in range(2):
            for c in range(2):
                cols(a["w_mem_kv"][layer], 256 * c, 256 * c + 256)
        for layer in range(2):
            if layer == 0:
                for c in range(0, 1280, 256):
                    cols(a["w_swa"], c, c + 256)
                cols(a["w_swa"], 1280, 1408)
                cols(a["w_swa"], 1408, 1600)
            else:
                for c in range(0, 2560, 256):
                    cols(a["w_fox"], c, c + 256)
                laid(a["w_forget"], False)
            for c in range(4):
                cols(a["w_out"][layer], 256 * c, 256 * c + 256)
            if layer == 0:
                plan_up(a["w_ffn_in"])
                plan_down(a["w_ffn_out"])
            else:
                laid(a["w_router"], False)
                moe_at = len(plan)
                for e_ in range(NE):
                    plan_up(a["w_exp_in"][e_])
                    w = a["w_exp_out"][e_].rearrange("(k p) n -> p k n", p=128)
                    for c in range(FT // 2):
                        plan.append((w[:, 2 * c:2 * c + 2, :], 2, 1024, True))
                moe_end = len(plan)
        for layer in range(2):
            for c in range(14):
                cols(a["w_in_2"][layer], 256 * c, 256 * c + 256)
            for c in range(4):
                cols(a["w_gate"][layer], 256 * c, 256 * c + 256)
                cols(a["w_gate"][layer], 1024 + 256 * c, 1024 + 256 * c + 256)
                cols(a["w_branch"][layer], 256 * c, 256 * c + 256)
            for c in range(4):
                cols(a["w_out_2"][layer], 256 * c, 256 * c + 256)
            plan_up(a["w_up"][layer])
            plan_down(a["w_down"][layer])

        def queue_stream():
            for c, (src, kt, n, _) in enumerate(plan):
                i = c % NR
                dst = ring[i][:, 0:kt * n].rearrange("p (k n) -> p k n", k=kt)
                dma(Y, dst, src, ring_sems[i], 16 * (c // NR + 1), Token(s_raw, c - NR + 1) if c >= NR else None)

        class Stream:

            def __init__(self):
                self.c = self.ahead = 0
                self.limit = moe_at
                self.free = [[], []]

            def split(self):
                c = self.ahead
                self.ahead += 1
                _, kt, n, parts = plan[c]
                raw = ring[c % NR][:, 0:kt * n]
                landed = Token(ring_sems[c % NR], 16 * (c // NR + 1))
                if parts:
                    h, l = wH[c % 2][:, 0:kt * n], wL[c % 2][:, 0:kt * n]
                    t = act(h, raw, ACT.Copy, landed, self.free[c % 2], free=True)
                    fn = lambda e: e.tensor_tensor(l, raw, h.bitcast(F32), ALU.subtract)
                else:
                    t = self.free[c % 2]
                    fn = lambda e: e.tensor_copy(small_w[:, 0:kt * n], raw)
                token = Token(s_raw, c + 1)
                V.ops.append((fn, flat([t, landed]), token, 1))
                V.last = token

            def take(self, kt, n):
                c = self.c
                self.c += 1
                assert plan[c][1:3] == (kt, n), (c, plan[c][1:3], kt, n)
                while self.ahead <= min(c + 1, self.limit - 1):
                    self.split()
                v = lambda b: b[:, 0:kt * n].rearrange("p (k n) -> p k n", k=kt)
                if not plan[c][3]:
                    return Chunk(self, c, v(small_w), None)
                return Chunk(self, c, v(wH[c % 2]), v(wL[c % 2]))

        class Chunk:
            def __init__(self, stream, c, h, l):
                self.stream, self.i, self.h, self.l = stream, c % 2, h, l
                self.ready = Token(s_raw, c + 1)

            def done(self, *tokens):
                self.stream.free[self.i] = flat(tokens)

        small_w = sb_small
        def mm(out, lhsT, rhs, start, stop, *after, **kw):
            return P(lambda e: e.matmul(out, lhsT, rhs, start=start, stop=stop, **kw), *after)

        def tr(out, in_, n, *after):
            return P(lambda e: e.transpose(out, in_, C("ident", 0, n, n)), *after)

        def vtt(out, x, y, op, *after, q=None, free=False):
            return (q or V)(lambda e: e.tensor_tensor(out, x, y, op), *after, free=free)

        def vts(out, x, s1, s2, o1, o2=None, *after, free=False, q=None):
            if o2 is None:
                return (q or V)(lambda e: e.tensor_scalar(out, x, s1, None, o1), *after, free=free)
            return (q or V)(lambda e: e.tensor_scalar(out, x, s1, s2, o1, o2), *after, free=free)

        def stt(out, x, s, y, o1, o2, *after, free=False):
            return V(lambda e: e.scalar_tensor_tensor(out=out, in0=x, scalar=s, in1=y, op0=o1, op1=o2),
                     *after, free=free)

        def act(out, x, f, *after, free=False, **kw):
            return A(lambda e: e.activation(out, x, f, **kw), *after, free=free)

        def vcopy(out, x, *after, free=False):
            return V(lambda e: e.tensor_copy(out, x), *after, free=free)

        def recip(out, x, *after):
            return V(lambda e: e.reciprocal(out, x), *after)

        M_, A_, B_ = (0, NM), (NM, NM + 128), (NM + 128, T2)

        def mm3(out, lh, ll, rh, rl, start, stop, *after, **kw):
            mm(out, lh, rh, start, False, *after, **kw)
            mm(out, lh, rl, False, False, **kw)
            return mm(out, ll, rh, False, stop, **kw)

        def group(out, t0, t1, ch, c0, k0, kt, x, first, last, after, kw={}):
            for k in range(kt):
                tok = mm3(out, ch.h[:, k, c0:c0 + 128], ch.l[:, k, c0:c0 + 128], x[0][:, k0 + k, t0:t1],
                          x[1][:, k0 + k, t0:t1], first and k == 0, last and k == kt - 1,
                          after if k == 0 else None, **kw)
            return tok

        def product(keys, x, t0, t1, after, evac):
            ch = S_.take(KT, 128 * len(keys))
            for i, key in enumerate(keys):
                bank, free = PB.take()
                tok = group(bank[:, 0:t1 - t0], t0, t1, ch, 128 * i, 0, KT, x, True, True,
                            [free, ch.ready, after])
                PB.give(bank, evac(key, bank[:, 0:t1 - t0], tok))
            ch.done(tok)

        def rows(n, x, tiles, after, evac):
            ch = S_.take(KT, n)
            for i, (t0, t1) in enumerate(tiles):
                bank, free = PB.take()
                for k in range(KT):
                    tok = mm3(bank[:, 0:n], x[0][:, k, t0:t0 + 128], x[1][:, k, t0:t0 + 128], ch.h[:, k, :],
                              ch.l[:, k, :], k == 0, k == KT - 1, [free, ch.ready, after] if k == 0 else None)
                PB.give(bank, evac(i, bank[0:t1 - t0, 0:n], tok))
            ch.done(tok)

        def few_rows(n, x, tiles, after, evac):
            ch = S_.take(KT, n)
            for i, (t0, t1) in enumerate(tiles):
                bank, free = PB.take()
                for k in range(KT):
                    tok = mm(bank[:, 0:n], x[:, k, t0:t1], ch.h[:, k, :], k == 0, k == KT - 1,
                             [free, ch.ready, after] if k == 0 else None)
                PB.give(bank, evac(i, bank[0:t1 - t0, 0:n], tok))
            ch.done(tok)

        def parts(h, l, x, *after):
            c = act(h, x, ACT.Copy, *after, free=True)
            return [c, vtt(l, x, h.bitcast(F32), ALU.subtract, c, *after, free=True)]

        S_ = Stream()

        in_tot = 0

        def load_in(out, src):
            nonlocal in_tot
            in_tot += 16
            return dma(Y, out, src, s_in, in_tot)

        load_in(pk[:, :], a["pack"])
        pos_i = TM[:, 0, 0:S].bitcast(I32)
        load_in(pos_i, a["pos"])
        load_in(hX[:, :, NM:T2], a["xT"])
        load_in(hX[:, :, 0:NM], a["metaT"])
        sq_mem = sq[:, 0:KT * S].rearrange("p (k t) -> p k t", k=KT)
        inputs = load_in(sq_mem, a["memT"])
        queue_stream()
        for q in (P, V, A, G):
            q.ops.append((None, [inputs], Token(None, 0), 0))

        cos1, sin1 = TM[:, 6, 0:S], TM[:, 7, 0:S]
        posf, ang, kk, r1 = TM[:, 1, 0:S], TM[:, 2, 0:S], TM[:, 3, 0:S], TM[:, 4, 0:S]
        vcopy(posf, pos_i)
        vts(ang, posf, C("inv1"), None, ALU.mult)
        vts(kk, ang, float(1 / (2 * np.pi)), MAGIC, ALU.mult, ALU.add)
        vts(kk, kk, MAGIC, None, ALU.subtract)
        stt(r1, kk, -TWO_PI_1, ang, ALU.mult, ALU.add)
        stt(r1, kk, -TWO_PI_2, r1, ALU.mult, ALU.add)
        stt(r1, kk, -TWO_PI_3, r1, ALU.mult, ALU.add)
        t = vts(r1, r1, 3.1415925, -3.1415925, ALU.min, ALU.max)
        act(sin1, r1, ACT.Sin, t)
        t = act(kk, r1, ACT.Sin, scale=0.5)
        vtt(kk, kk, kk, ALU.mult, t)
        rope1 = vts(cos1, kk, -2.0, 1.0, ALU.mult, ALU.add)
        rope1 = [rope1, A.last]

        tmp = Slots([TM[:, i, :] for i in range(4)])
        for i in range(4):
            v_, _ = tmp.take()
            tmp.give(v_, V.last, A.last)
        tmp2 = Slots([TM[:, i, :] for i in range(4, 6)])
        v_, _ = tmp2.take()
        tmp2.give(v_, V.last, A.last)

        r3 = rX[:, :].rearrange("p (k t) -> p k t", k=KT)
        q3 = sq[:, :].rearrange("p (k t) -> p k t", k=KT)

        def layer_norm(g, b, li, r_ready, split=True):
            bank, free = PB.take()
            mu = bank[:, 0:S]
            for k in range(KT):
                t = mm(mu, C("mean"), r3[:, k, NM:T2], k == 0, k == KT - 1, free if k == 0 else None,
                       r_ready[k])
            bank2, free2 = PB.take()
            var = bank2[:, 0:S]
            for k in range(KT):
                d = vtt(r3[:, k, NM:T2], r3[:, k, NM:T2], mu, ALU.subtract, t, free=k > 0)
                s = act(q3[:, k, NM:T2], r3[:, k, NM:T2], ACT.Square, d, free=k > 0)
                t2 = mm(var, C("mean"), q3[:, k, NM:T2], k == 0, k == KT - 1, free2 if k == 0 else None, s)
            PB.give(bank, d)
            sd, tf = tmp.take()
            s = act(sd[:, 0:S], var, ACT.Sqrt, t2, tf, bias=C("eps5"))
            PB.give(bank2, s)
            rs = recip(sd[:, 0:S], sd[:, 0:S], s)
            readers = [P.last, V.last]
            out_ready = []
            for k in range(KT):
                v = vtt(r3[:, k, NM:T2], r3[:, k, NM:T2], sd[:, 0:S], ALU.mult, rs, free=k > 0)
                i = li * 8 + k
                aff = dict(scale=C(g, i, 1), bias=C(b, i, 1))
                c = act(hX[:, k, NM:T2], r3[:, k, NM:T2], ACT.Identity, v, readers, free=k > 0, **aff)
                if split:
                    h = nH[:, k, NM:T2]
                    c = act(h, r3[:, k, NM:T2], ACT.Identity, v, readers, free=True, **aff)
                    c = [c, vtt(nL[:, k, NM:T2], hX[:, k, NM:T2], h.bitcast(F32), ALU.subtract, c, free=True)]
                out_ready.append(c)
            tmp.give(sd, v)
            return out_ready

        def rms_norm(g, li, h_ready):
            h = hX
            bank, free = PB.take()
            ms = bank[:, 0:T2]
            for k in range(KT):
                s = act(q3[:, k, :], h[:, k, :], ACT.Square, h_ready[k], P.last if k == 0 else None, free=k > 0)
                t = mm(ms, C("mean"), q3[:, k, :], k == 0, k == KT - 1, free if k == 0 else None, s)
            sd, tf = tmp.take()
            s = act(sd, ms, ACT.Sqrt, t, tf, bias=C("eps6"))
            PB.give(bank, s)
            rs = recip(sd, sd, s)
            ready = []
            readers = P.last
            for k in range(KT):
                v = stt(r3[:, k, :], h[:, k, :], C(g, li * 8 + k, 1), sd, ALU.mult, ALU.mult, rs, free=k > 0)
                c = act(nH[:, k, :], r3[:, k, :], ACT.Copy, v, readers, free=True)
                ready.append(vtt(nL[:, k, :], r3[:, k, :], nH[:, k, :].bitcast(F32), ALU.subtract, c, v,
                                 free=True))
            tmp.give(sd, ready[-1])
            return ready

        sc_slots = Slots([rX[:, 512 * i:512 * i + 512] for i in range(3)])
        pt_slots = Slots([sq[:, 512 * i:512 * i + 512] for i in range(3)])
        st_slots = Slots([sm[:, 8 * i:8 * i + 8] for i in range(6)])

        def attend(heads, ready):
            n = len(heads)
            st = {}
            for i in range(n + 2):
                if i < n:
                    h = heads[i]
                    bank, free = PB.take()
                    for t in range(2):
                        tok = mm(bank[:, 256 * t:256 * t + 256], h["q"][:, 128 * t:128 * t + 128], h["k"],
                                 t == 0, t == 1, [free, ready] if t == 0 else None, skip_group_check=True)
                    sc, f = sc_slots.take()
                    s2, f2 = st_slots.take()
                    v = h["add"](sc, bank, [tok, f])
                    PB.give(bank, v)
                    nm, den = s2[:, 0:2], s2[:, 2:4]
                    sc3 = sc.rearrange("p (t k) -> p t k", t=2)
                    v = V(lambda e, nm=nm, sc3=sc3: e.tensor_reduce(nm, sc3, AX.X, ALU.max, negate=True), f2)
                    if h.get("sink") is not None:
                        v = vts(nm, nm, h["sink_neg"], None, ALU.min)
                    for t in range(2):
                        c = act(sc[:, 256 * t:256 * t + 256], sc[:, 256 * t:256 * t + 256], ACT.Exp, v,
                                bias=nm[:, t:t + 1], accum_out=den[:, t:t + 1])
                    if h.get("sink") is not None:
                        c = act(s2[:, 4:6], nm, ACT.Exp, bias=h["sink"])
                        vtt(den, den, s2[:, 4:6], ALU.add, c)
                    recip(den, den, c)
                    for t in range(2):
                        v = vts(sc[:, 256 * t:256 * t + 256], sc[:, 256 * t:256 * t + 256], den[:, t:t + 1],
                                None, ALU.mult)
                    st_slots.give(s2, v)
                    st[i] = (sc, v)
                if 1 <= i <= n:
                    sc, v = st[i - 1]
                    bank, free = PB.take()
                    for kt in range(2):
                        for t in range(2):
                            tok = tr(bank[:, 256 * kt + 128 * t:256 * kt + 128 * t + 128],
                                     sc[:, 256 * t + 128 * kt:256 * t + 128 * kt + 128], 128,
                                     [free, v] if kt + t == 0 else None)
                    sc_slots.give(sc, tok)
                    pt, f = pt_slots.take()
                    c = act(pt, bank[:, :], ACT.Copy, tok, f)
                    PB.give(bank, c)
                    st[i - 1] = (pt, c)
                if i >= 2:
                    j = i - 2
                    h = heads[j]
                    pt, c = st[j]
                    if j % 2 == 0:
                        obank, ofree = PB.take()
                    p0 = 64 * (j % 2)
                    for kt in range(2):
                        tok = mm(obank[p0:p0 + 64, 0:S], h["v"][kt], pt[:, 256 * kt:256 * kt + 256], kt == 0,
                                 kt == 1, [c, ofree] if kt == 0 else None)
                    pt_slots.give(pt, tok)
                    if j % 2 == 1:
                        v = vcopy(mX[:, h["tile"], NM:T2], obank[:, 0:S], tok)
                        PB.give(obank, v)
            return V.last

        n_ = (nH, nL)
        m_ = (mH, mL)
        hp = (hH, hL)

        def ffn_in(x_ready, t0, t1, on_pair):
            n = t1 - t0
            for u in range(FT // 2):
                bk = [PB.take() for _ in range(4)]
                for z in range(2):
                    ch = S_.take(4, 512)
                    toks = []
                    for i, (bank, free) in enumerate(bk):
                        toks.append(group(bank[:, 0:n], t0, t1, ch, 128 * i, 4 * z, 4, n_, z == 0, z == 1,
                                          [free, ch.ready, x_ready]))
                    ch.done(toks[-1])
                for g in range(2):
                    on_pair(2 * u + g, bk[g][0], toks[g], bk[2 + g][0], toks[2 + g])

        def ffn_out(h_ready, t0, t1, evac):
            n = t1 - t0
            for g in range(KT):
                bank, free = PB.take()
                for z in range(2):
                    ch = S_.take(FT // 2, 128)
                    tok = group(bank[:, 0:n], t0, t1, ch, 0, 11 * z, 11, hp, z == 0, z == 1,
                                [free, ch.ready, [h_ready[k] for k in range(11 * z, 11 * z + 11)]])
                    ch.done(tok)
                PB.give(bank, evac(g, bank[:, 0:n], tok))

        v = parts(mH[:, :, 0:S], mL[:, :, 0:S], sq_mem)
        kv1_k = kv1[:, 0:512].rearrange("p (k t) -> p k t", k=2)
        kv1_v = kv1[:, 512:1024].rearrange("p (t n) -> p t n", t=2)
        kv0_k = W1[:, 5984 - 1024:5984 - 512].rearrange("p (k t) -> p k t", k=2)
        kv0_v = W1[:, 5984 - 512:5984].rearrange("p (t n) -> p t n", t=2)
        mem_ready = v
        for kd_, vd_ in ((kv0_k, kv0_v), (kv1_k, kv1_v)):
            product([0, 1], m_, 0, S, mem_ready,
                    lambda key, ps, tk: act(kd_[:, key, :], ps, ACT.Copy, tk, free=True))
            rows(256, m_, [(0, 128), (128, 256)], None, lambda i, ps, tk: vcopy(vd_[:, i, :], ps, tk, free=True))
        x_ready = [parts(nH[:, k, NM:T2], nL[:, k, NM:T2], hX[:, k, NM:T2]) for k in range(KT)]
        for layer in range(2):
            o = 0
            lim = FT * T2 - (1024 if layer == 0 else 0)

            def area(n):
                nonlocal o
                if o < FT * T2 and o + n > lim:
                    o = FT * T2
                r = W1[:, o:o + n] if o < FT * T2 else W2[:, o - FT * T2:o - FT * T2 + n]
                o += n
                assert o <= FT * T2 + NW2
                return r

            qn = area(8 * S).rearrange("p (k t) -> p k t", k=8)
            kn = area((3 if layer == 0 else 6) * S).rearrange("p (k t) -> p k t", t=S)
            vn = area(2 * (192 if layer == 0 else 768)).rearrange("p (t n) -> p t n", t=2)
            km, vm = (kv0_k, kv0_v) if layer == 0 else (kv1_k, kv1_v)
            free_w = P.last

            def plain(dst):
                return lambda key, ps, tk: act(dst[:, key, :], ps, ACT.Copy, tk, free_w, free=True)

            if layer == 0:
                def roped(key, ps, tk):
                    dst = qn[:, key, :] if key < 8 else kn[:, key - 8, :]
                    raw, tf = tmp.take()
                    c = act(raw[:, 0:S], ps, ACT.Copy, tk, tf)
                    bank, free = PB.take()
                    m = mm(bank[:, 0:S], C("rot1"), raw[:, 0:S], True, True, c, free)
                    t2, tf2 = tmp2.take()
                    v = vtt(t2[:, 0:S], bank[:, 0:S], sin1, ALU.mult, m, tf2, rope1)
                    PB.give(bank, v)
                    vtt(dst, raw[:, 0:S], cos1, ALU.mult, c, free_w)
                    v = vtt(dst, dst, t2[:, 0:S], ALU.add)
                    tmp.give(raw, v)
                    tmp2.give(t2, v)
                    return c

                for c in range(3):
                    product([2 * c, 2 * c + 1], n_, NM, T2, x_ready if c == 0 else None, roped)
                product([8, 9], n_, NM, T2, None, roped)
                product([10, 6], n_, NM, T2, None,
                        lambda key, ps, tk: roped(key, ps, tk) if key == 10 else plain(qn)(key, ps, tk))
                product([7], n_, NM, T2, None, plain(qn))
                rows(192, n_, [A_, B_], None, lambda i, ps, tk: vcopy(vn[:, i, :], ps, tk, free_w))
                vts(sm[:, 64:76], C("sinks"), -1.0, None, ALU.mult)
                mask = C("swa")

                def add(sc, bank, after):
                    return stt(sc, bank[:, :], SCALE, mask, ALU.mult, ALU.add, after)

                heads = [dict(q=qn[64 * (i % 2):64 * (i % 2) + 64, i // 2, :],
                              k=kn[64 * (i % 2):64 * (i % 2) + 64, i // 4, :],
                              v=[vn[:, t, 64 * (i // 4):64 * (i // 4) + 64] for t in range(2)], add=add,
                              sink=C("sinks", i, 1), sink_neg=sm[:, 64 + i:65 + i], tile=i // 2)
                         for i in range(12)]
            else:
                cq = area(24).rearrange("p (t n) -> p t n", t=2)
                R = area(12 * S).rearrange("p (h t) -> p h t", t=S)
                ck = area(2 * S)
                dests = [(qn, i) for i in range(6)] + [(kn, i) for i in range(6)]

                def to(key, ps, tk):
                    d, i = dests[key]
                    return act(d[:, i, :], ps, ACT.Copy, tk, free_w, free=True)

                for c in range(6):
                    product([2 * c, 2 * c + 1], n_, NM, T2, x_ready if c == 0 else None, to)
                for c in range(3):
                    rows(256, n_, [A_, B_], None,
                         lambda i, ps, tk: vcopy(vn[:, i, 256 * c:256 * c + 256], ps, tk, free_w))
                product([6, 7], n_, NM, T2, None, plain(qn))
                lf = sm[:, 128:152].rearrange("p (t n) -> p t n", t=2)
                lg = sm[:, 152:176].rearrange("p (t n) -> p t n", t=2)
                ls = sm[:, 176:200].rearrange("p (t n) -> p t n", t=2)
                few_rows(12, hX, [A_, B_], None,
                         lambda i, ps, tk: vtt(lf[:, i, :], ps, C("b_forget"), ALU.add, tk))
                c = act(lg, lf, ACT.Abs, V.last)
                c = act(lg, lg, ACT.Exp, scale=-1.0)
                c = act(lg, lg, ACT.Ln, bias=1.0)
                lft = stt(ls, lf, 0.0, lg, ALU.min, ALU.subtract, c)
                bank, free = PB.take()
                mm(bank[:, 0:12], C("upper"), ls[:, 0, :], True, False, free, lft, skip_group_check=True)
                mm(bank[:, 16:28], C("upper"), ls[:, 1, :], False, False, skip_group_check=True)
                tok = mm(bank[:, 16:28], C("ones"), ls[:, 0, :], False, True, skip_group_check=True)
                v = vcopy(cq[:, 0, :], bank[:, 0:12], tok)
                v = vcopy(cq[:, 1, :], bank[:, 16:28], tok)
                PB.give(bank, v)
                bank, free = PB.take()
                for t in range(2):
                    tok = tr(bank[0:12, 128 * t:128 * t + 128], cq[:, t, :], 128, v, free)
                v = vcopy(ck[0:12, 0:S], bank[0:12, 0:S], tok)
                PB.give(bank, v)
                for h in range(12):
                    bank, free = PB.take()
                    tok = mm(bank[:, 0:S], C("ident", h, 1, 12).to_broadcast([12, 128]), ck[0:12, 0:S], True,
                             True, v, free)
                    c = act(R[:, h, :], bank[:, 0:S], ACT.Copy, tok, free=True)
                    PB.give(bank, c)
                tb = [tmp.take() for _ in range(2)]
                bias_buf = [x[0] for x in tb]
                bias_free = [x[1] for x in tb]

                def adder(h):
                    def add(sc, bank, after):
                        for t in range(2):
                            b = bias_buf[t][:, 0:S]
                            stt(b, R[:, h, :], cq[:, t, h:h + 1], C("causal", 256 * t, 256), ALU.subtract,
                                ALU.subtract, c, bias_free)
                            v = stt(sc[:, 256 * t:256 * t + 256], bank[:, 256 * t:256 * t + 256], SCALE, b,
                                    ALU.mult, ALU.subtract, after)
                        return v
                    return add

                heads = [dict(q=qn[64 * (i % 2):64 * (i % 2) + 64, i // 2, :],
                              k=kn[64 * (i % 2):64 * (i % 2) + 64, i // 2, :],
                              v=[vn[:, t, 64 * i:64 * i + 64] for t in range(2)], add=adder(i), tile=i // 2)
                         for i in range(12)]

            def add_mem(sc, bank, after):
                return vts(sc, bank[:, :], SCALE, None, ALU.mult, None, after)

            heads += [dict(q=qn[64 * (i % 2):64 * (i % 2) + 64, 6 + i // 2, :],
                           k=km[64 * (i % 2):64 * (i % 2) + 64, i // 2, :],
                           v=[vm[:, t, 64 * i:64 * i + 64] for t in range(2)], add=add_mem, tile=6 + i // 2)
                      for i in range(4)]
            mixed = attend(heads, [V.last, A.last])
            if layer == 1:
                for b in bias_buf:
                    tmp.give(b, V.last)

            r_ready = {}

            def res(key, ps, tk):
                r_ready[key] = stt(r3[:, key, NM:T2], hX[:, key, NM:T2], ALPHA, ps, ALU.mult, ALU.add, tk,
                                   P.last, A.last, free=True)
                return r_ready[key]

            v = parts(mH[:, :, NM:T2], mL[:, :, NM:T2], mX[:, :, NM:T2], mixed, P.last)
            for c in range(4):
                product([2 * c, 2 * c + 1], m_, NM, T2, v, res)
            x_ready = layer_norm("ln_attn_g", "ln_attn_b", layer, r_ready)

            if layer == 0:
                h_ready = {}
                free_ff = [P.last, V.last, A.last]

                def pair(j, ba, ta, bb, tb_):
                    s_, tf = tmp.take()
                    c = act(s_[:, 0:S], ba[:, 0:S], ACT.Silu, ta, tf, free=True)
                    PB.give(ba, c)
                    v = vtt(s_[:, 0:S], s_[:, 0:S], bb[:, 0:S], ALU.mult, c, tb_, free=True)
                    PB.give(bb, v)
                    h_ready[j] = parts(hH[:, j, NM:T2], hL[:, j, NM:T2], s_[:, 0:S], v, free_ff)
                    tmp.give(s_, h_ready[j])

                ffn_in(x_ready, NM, T2, pair)

                def down(g, ps, tk):
                    r_ready[g] = stt(r3[:, g, NM:T2], hX[:, g, NM:T2], ALPHA, ps, ALU.mult, ALU.add, tk,
                                     free=True)
                    return r_ready[g]

                ffn_out(h_ready, NM, T2, down)
                x_ready = layer_norm("ln_ffn_g", "ln_ffn_b", layer, r_ready)
            else:
                lo = sm[:, 200:216].rearrange("p (t n) -> p t n", t=2)
                few_rows(8, hX, [A_, B_], x_ready,
                         lambda i, ps, tk: vtt(lo[:, i, :], ps, C("b_router"), ALU.add, tk))
                gt_ = sm[:, 216:232].rearrange("p (t n) -> p t n", t=2)
                eq = sm[:, 232:248].rearrange("p (t n) -> p t n", t=2)
                cu = sm[:, 248:264].rearrange("p (t n) -> p t n", t=2)
                cv = sm[:, 264:280].rearrange("p (t n) -> p t n", t=2)
                ex = sm[:, 280:296].rearrange("p (t n) -> p t n", t=2)
                mx = sm[:, 296:312].rearrange("p (t n) -> p t n", t=2)
                s1 = sm[:, 312:314]
                for t in range(2):
                    V(lambda e, t=t: e.max(mx[:, t, :], lo[:, t, :]))
                    vts(gt_[:, t, :], lo[:, t, :], mx[:, t, 1:2], None, ALU.is_gt)
                    vts(eq[:, t, :], lo[:, t, :], mx[:, t, 1:2], None, ALU.is_equal)
                    v = vts(ex[:, t, :], lo[:, t, :], mx[:, t, 0:1], None, ALU.subtract)
                c = act(ex, ex, ACT.Exp, v)
                src, dst = eq, cu
                for sft in (1, 2, 4):
                    vcopy(dst[:, :, 0:sft], src[:, :, 0:sft])
                    vtt(dst[:, :, sft:8], src[:, :, sft:8], src[:, :, 0:8 - sft], ALU.add)
                    src, dst = dst, (cv if dst is cu else cu)
                V(lambda e: e.tensor_reduce(s1, gt_, AX.X, ALU.add))
                for t in range(2):
                    vts(src[:, t, :], src[:, t, :], s1[:, t:t + 1], 2.0, ALU.add, ALU.is_le)
                vtt(eq, eq, src, ALU.mult)
                vtt(eq, eq, gt_, ALU.add)
                vtt(ex, ex, eq, ALU.mult, c)
                V(lambda e: e.tensor_reduce(s1, ex, AX.X, ALU.add))
                recip(s1, s1)
                for t in range(2):
                    v = vts(ex[:, t, :], ex[:, t, :], s1[:, t:t + 1], None, ALU.mult)
                bank, free = PB.take()
                mm(bank[:, 0:8], C("upper"), eq[:, 0, :], True, False, v, free, skip_group_check=True)
                mm(bank[:, 8:16], C("upper"), eq[:, 1, :], False, False, skip_group_check=True)
                mm(bank[:, 8:16], C("ones"), eq[:, 0, :], False, False, skip_group_check=True)
                mm(bank[:, 16:24], C("ones"), eq[:, 0, :], False, False, skip_group_check=True)
                tok = mm(bank[:, 16:24], C("ones"), eq[:, 1, :], False, True, skip_group_check=True)
                pos = sm[:, 200:216].rearrange("p (t n) -> p t n", t=2)
                vtt(pos, bank[:, 0:16].rearrange("p (t n) -> p t n", t=2), eq, ALU.mult, tok)
                vts(pos, pos, -1.0, None, ALU.add)
                counts = bank[:, 16:24]
                V(lambda e: e.tensor_reduce(s1[:, 0:1], counts, AX.X, ALU.max))
                flag = sb_flag
                flag_ready = vts(flag[:, :], s1[:, 0:1], 128.5, None, ALU.is_gt)
                PB.give(bank, flag_ready)
                for k in range(KT):
                    r_ready[k] = vts(r3[:, k, NM:T2], hX[:, k, NM:T2], ALPHA, None, ALU.mult, None, x_ready[k],
                                     free=True)
                pools = [(PB, 8), (tmp, 4), (tmp2, 2)]

                def meet(tokens):
                    for q in (P, V, A):
                        q.ops.append((None, list(tokens), Token(None, 0), 0))
                    for pool, n in pools:
                        pool.all_free(n)
                    S_.free = [[], []]

                meet([P.last, V.last, A.last, flag_ready])
                top = {q: (q.ops, q.branch(flag[0:1, 0:1], [flag_ready])) for q in (P, V, A)}

                for q, (_, b) in top.items():
                    q.ops, q.last = b.taken, None
                bank, free = PB.take()
                for t in range(2):
                    tok = tr(bank[0:8, 128 * t:128 * t + 128], ex[:, t, :], 128)
                gT = sq[0:8, 0:S]
                v = vcopy(gT, bank[0:8, 0:S], tok)
                PB.give(bank, v)
                for h in range(NE):
                    bank, free = PB.take()
                    tok = mm(bank[:, 0:S], C("ident", h, 1, 8).to_broadcast([8, 128]), gT, True, True, v, free)
                    gt_ready = act(gts[:, h, :], bank[:, 0:S], ACT.Copy, tok, free=True)
                    PB.give(bank, gt_ready)
                S_.limit = moe_end
                for e_ in range(NE):
                    h_ready = {}
                    free_ff = [P.last]

                    def pair(j, ba, ta, bb, tb_):
                        s_, tf = tmp.take()
                        c = act(s_[:, 0:S], ba[:, 0:S], ACT.Silu, ta, tf, free=True)
                        PB.give(ba, c)
                        v = vtt(s_[:, 0:S], s_[:, 0:S], bb[:, 0:S], ALU.mult, c, tb_, free=True)
                        PB.give(bb, v)
                        v = vtt(s_[:, 0:S], s_[:, 0:S], gts[:, e_, :], ALU.mult, gt_ready)
                        h_ready[j] = parts(hH[:, j, NM:T2], hL[:, j, NM:T2], s_[:, 0:S], v, free_ff)
                        tmp.give(s_, h_ready[j])

                    ffn_in([], NM, T2, pair)
                    bk = [PB.take() for _ in range(4)]
                    for c in range(FT // 2):
                        ch = S_.take(2, 1024)
                        for g in range(KT):
                            bank, free = bk[g // 2]
                            tok = group(bank[:, 256 * (g % 2):256 * (g % 2) + 256], NM, T2, ch, 128 * g, 2 * c, 2,
                                        hp, c == 0 and g % 2 == 0, c == FT // 2 - 1,
                                        [free, ch.ready, h_ready[2 * c], h_ready[2 * c + 1]],
                                        dict(skip_group_check=True))
                        ch.done(tok)
                    for g in range(KT):
                        v = vtt(r3[:, g, NM:T2], r3[:, g, NM:T2],
                                bk[g // 2][0][:, 256 * (g % 2):256 * (g % 2) + 256], ALU.add, tok)
                        if g % 2:
                            PB.give(bk[g // 2][0], v)
                dense_end = [P.last, V.last, A.last]
                meet([])
                for q, (ops, b) in top.items():
                    q.ops, q.last = b.other, None
                S_.c = S_.ahead = moe_at

                xt3 = sq[:, 0:2048].rearrange("p (t n) -> p t n", t=2)
                for t, (t0, t1) in enumerate([A_, B_]):
                    for half in range(2):
                        bank, free = PB.take()
                        for i in range(4):
                            tok = tr(bank[:, 128 * i:128 * i + 128], hX[:, 4 * half + i, t0:t1], 128, free)
                        xt_ready = act(xt3[:, t, 512 * half:512 * half + 512], bank[:, :], ACT.Copy, tok)
                        PB.give(bank, xt_ready)
                ym = mX[:, :, :].rearrange("p k t -> p (k t)")
                gs = sm[:, 312:320]
                st = {}

                def gather(e_):
                    Pe = Pg[:, e_ % 2, :, :]
                    for t in range(2):
                        v = vts(Pe[:, t, :], C("iota"), pos[:, t, e_:e_ + 1], None, ALU.is_equal, None, P.last)
                    bks = [PB.take() for _ in range(2)]
                    for g in range(KT):
                        bank, free = bks[g // 4]
                        for t in range(2):
                            tok = mm(bank[:, 128 * (g % 4):128 * (g % 4) + 128], xt3[:, t, 128 * g:128 * g + 128],
                                     Pe[:, t, :], g % 4 == 0 and t == 0, t == 1, v, free, xt_ready,
                                     skip_group_check=True)
                        if g % 4 == 3:
                            x = bank[:, :].rearrange("p (k n) -> p k n", k=4)
                            w = [slice(g - 3, g + 1)]
                            r = parts(xgH[:, g - 3:g + 1, :], xgL[:, g - 3:g + 1, :], x, tok, st.get("in_done"))
                            PB.give(bank, r)
                            st["xg", g // 4] = r
                    bank, free = PB.take()
                    for t in range(2):
                        tok = tr(bank[:, 128 * t:128 * t + 128], Pe[:, t, :], 128, free)
                    for t in range(2):
                        tok = mm(bank[:, 256:257], Pe[:, t, :], ex[:, t, e_:e_ + 1], t == 0, t == 1,
                                 skip_group_check=True)
                    st["pt", e_] = act(Pt[:, e_ % 2, :], bank[:, 0:256], ACT.Copy, tok)
                    c = act(gs[:, e_ % 2:e_ % 2 + 1], bank[:, 256:257], ACT.Copy)
                    st["gs", e_] = c
                    PB.give(bank, c)

                def up_unit(u):
                    bank, free = PB.take()
                    for z in range(2):
                        ch = S_.take(4, 512)
                        for k in range(4):
                            kk_ = 4 * z + k
                            lh, ll = xgH[:, kk_, :], xgL[:, kk_, :]
                            w = [free, ch.ready, st["xg", z]] if k == 0 else None
                            mm(bank[:, :], lh, ch.h[:, k, :], kk_ == 0, False, w)
                            mm(bank[:, :], lh, ch.l[:, k, :], False, False)
                            tok = mm(bank[:, :], ll, ch.h[:, k, :], False, kk_ == KT - 1)
                        ch.done(tok)
                    s_, tf = tmp.take()
                    c = act(s_[:, 0:256], bank[:, 0:256], ACT.Silu, tok, tf, free=True)
                    v = vtt(s_[:, 0:256], s_[:, 0:256], bank[:, 256:512], ALU.mult, c, free=True)
                    PB.give(bank, v)
                    st["s", u] = (s_, v)
                    return tok

                def turn(u):
                    s_, v = st["s", u]
                    bank, free = PB.take()
                    for i in range(2):
                        tok = tr(bank[:, 128 * i:128 * i + 128], s_[:, 128 * i:128 * i + 128], 128, free, v)
                    tmp.give(s_, tok)
                    x = bank[:, 0:256].rearrange("p (k n) -> p k n", k=2)
                    st["h", u] = parts(hgH[:, 2 * u:2 * u + 2, :], hgL[:, 2 * u:2 * u + 2, :], x, tok,
                                       st.get("down_done"))
                    PB.give(bank, st["h", u])

                def down_all(e_):
                    bks = [PB.take() for _ in range(2)]
                    for c in range(FT // 2):
                        ch = S_.take(2, 1024)
                        for k in range(2):
                            kk_ = 2 * c + k
                            for p_, (lh, ws) in enumerate(((hgH, (ch.h, ch.l)), (hgL, (ch.h,)))):
                                for w in ws:
                                    for half in range(2):
                                        bank, free = bks[half]
                                        tok = mm(bank[:, :], lh[:, kk_, :], w[:, k, 512 * half:512 * half + 512],
                                                 kk_ == 0 and p_ == 0 and w is ch.h,
                                                 kk_ == FT - 1 and p_ == 1, [free, ch.ready, st["h", c]])
                        ch.done(tok)
                        if c == 1 and e_ + 1 < NE:
                            gather(e_ + 1)
                    st["down_done"] = tok
                    for half in range(2):
                        v = act(ym[:, 512 * half:512 * half + 512], bks[half][0][:, :], ACT.Copy, tok,
                                st["gs", e_], st.get("spread_done"), free=True,
                                scale=gs[:, e_ % 2:e_ % 2 + 1])
                        PB.give(bks[half][0], v)
                        st["y", half] = v

                def spread_all(e_):
                    for g in range(KT):
                        bank, free = PB.take()
                        tok = mm(bank[:, 0:S], ym[:, 128 * g:128 * g + 128], Pt[:, e_ % 2, :], True, True,
                                 free, st["y", g // 4], st["pt", e_])
                        v = vtt(r3[:, g, NM:T2], r3[:, g, NM:T2], bank[:, 0:S], ALU.add, tok, free=g > 0)
                        PB.give(bank, v)
                    st["spread_done"] = tok

                gather(0)
                for e_ in range(NE):
                    for u in range(FT // 2):
                        st["in_done"] = up_unit(u)
                        if u >= 1:
                            turn(u - 1)
                        if u == 1 and e_ > 0:
                            spread_all(e_ - 1)
                    turn(FT // 2 - 1)
                    down_all(e_)
                spread_all(NE - 1)

                meet([])
                for q, (ops, b) in top.items():
                    q.ops, q.last = ops, b.join
                meet([b.join for _, b in top.values()] + [Token(s_raw, moe_end)])
                S_.limit = len(plan)
                r_ready = [[]] * KT
                x_ready = layer_norm("ln_ffn_g", "ln_ffn_b", layer, r_ready, split=False)

        h_rdy = [list(flat([x_ready[k], inputs])) for k in range(KT)]
        tiles = [M_, A_, B_]
        for layer in range(2):
            n_ready = rms_norm("norm_mix", layer, h_rdy)
            free_w = [P.last, V.last, A.last]
            o = 0

            def area(n):
                nonlocal o
                if o < FT * T2 and o + n > FT * T2:
                    o = FT * T2
                r = W1[:, o:o + n] if o < FT * T2 else W2[:, o - FT * T2:o - FT * T2 + n]
                o += n
                return r

            qkv = area(12 * T2).rearrange("p (k t) -> p k t", t=T2)
            zz = area(4 * T2).rearrange("p (k t) -> p k t", t=T2)
            qb = area(4 * T2).rearrange("p (k t) -> p k t", t=T2)
            kik = area(2 * T2).rearrange("p (k t) -> p k t", t=T2)
            kb_, ik = kik[:, 0, :], kik[:, 1, :]
            iq = mX[:, 4:8, :]
            vv = TM[:, 6:8, :].rearrange("p a t -> p (a t)")[:, 0:384].rearrange("p (t n) -> p t n", t=3)
            ktok = area(3 * 512).rearrange("p (t h n) -> p t h n", t=3, h=4)
            vtok = area(3 * 512).rearrange("p (t h n) -> p t h n", t=3, h=4)

            def conv(key, ps, tk):
                dst = qkv[:, key, :]
                cw = lambda i: C("conv_a", (layer * 12 + key) * 4 + i, 1)
                v = vts(dst, ps, cw(3), None, ALU.mult, None, tk, free_w)
                for i in (2, 1, 0):
                    d = 3 - i
                    v = stt(dst[:, d:T2], ps[:, 0:T2 - d], cw(i), dst[:, d:T2], ALU.mult, ALU.add)
                act(dst, dst, ACT.Silu, v, free=True)
                return v

            for c in range(6):
                product([2 * c, 2 * c + 1], n_, 0, T2, n_ready if c == 0 else None, conv)
            for c in range(2):
                product([2 * c, 2 * c + 1], n_, 0, T2, None,
                        lambda key, ps, tk: act(zz[:, key, :], ps, ACT.Silu, tk, free_w, free=True))
            silu_done = A.last
            sml = sm[:, 320:368].rearrange("p (t n) -> p t n", t=3)

            def raw(dst):
                return lambda key, ps, tk: act(dst[:, key, :], ps, ACT.Copy, tk, free_w, free=True)

            def bv(i, ps, tk):
                vcopy(sml[0:ps.shape[0], i, :], ps[:, 128:144], tk, free_w)
                return vcopy(vv[0:ps.shape[0], i, :], ps[:, 0:128], tk, free_w)

            rows(256, n_, tiles, None, bv)
            for c in range(2):
                product([2 * c, 2 * c + 1], n_, 0, T2, None, raw(qb))
            for c in range(2):
                product([2 * c, 2 * c + 1], n_, 0, T2, None, raw(iq))
            product([0, 1], n_, 0, T2, None, raw(kik))
            raws = A.last
            gb = sm[:, 368:380].rearrange("p (t n) -> p t n", t=3)
            be = sm[:, 380:392].rearrange("p (t n) -> p t n", t=3)
            sa = sm[:, 392:404].rearrange("p (t n) -> p t n", t=3)
            gc = sm[:, 404:416].rearrange("p (t n) -> p t n", t=3)
            ge = sm[:, 416:428].rearrange("p (t n) -> p t n", t=3)
            gl = sm[:, 428:440].rearrange("p (t n) -> p t n", t=3)
            gk = sm[:, 440:452].rearrange("p (t n) -> p t n", t=3)
            ea = sm[:, 452:456]
            c = act(ea, C("a_log", 4 * layer, 4), ACT.Exp, V.last)
            for t, (t0, t1) in enumerate(tiles):
                n = t1 - t0
                v = vtt(gb[0:n, t, :], sml[0:n, t, 0:4], C("dt_bias", 4 * layer, 4)[0:n, :], ALU.add)
                c = act(sa[0:n, t, :], gb[0:n, t, :], ACT.Abs, v)
                c = act(sa[0:n, t, :], sa[0:n, t, :], ACT.Exp, scale=-1.0)
                c = act(sa[0:n, t, :], sa[0:n, t, :], ACT.Ln, bias=1.0)
                v = stt(gb[0:n, t, :], gb[0:n, t, :], 0.0, sa[0:n, t, :], ALU.max, ALU.add, c)
                v = stt(gb[0:n, t, :], gb[0:n, t, :], -1.0, ea[0:n, :], ALU.mult, ALU.mult)
                c = act(be[0:n, t, :], sml[0:n, t, 4:8], ACT.Exp, scale=-1.0)
                vts(be[0:n, t, :], be[0:n, t, :], 1.0, None, ALU.add, None, c)
                v = recip(be[0:n, t, :], be[0:n, t, :])
                bank, free = PB.take()
                mm(bank[0:n, 0:4], C("upper", 0, n, n), gb[0:n, t, :], True, False, v, free,
                   skip_group_check=True)
                tok = mm(bank[:, 16:20], C("ones", 0, 128, n), gb[0:n, t, :], False, True,
                         skip_group_check=True)
                v = vcopy(gc[0:n, t, :], bank[0:n, 0:4], tok)
                v = vtt(gk[0:n, t, :], bank[0:n, 16:20], gc[0:n, t, :], ALU.subtract)
                c = act(gl[:, t, :], bank[:, 16:20], ACT.Exp, v)
                PB.give(bank, v, c)
                act(gk[0:n, t, :], gk[0:n, t, :], ACT.Exp)
                c = act(ge[0:n, t, :], gc[0:n, t, :], ACT.Exp)
                v = vtt(ge[0:n, t, :], ge[0:n, t, :], be[0:n, t, :], ALU.mult, c)

            def col_stats(src, n, scale, eps, after):
                bank, free = PB.take()
                for i in range(n):
                    s_, tf = tmp.take()
                    c = act(s_, src(i), ACT.Square, tf, after)
                    m = mm(bank[0:n, 0:T2], C("colsel", 7 - i, n), s_, i == 0, i == n - 1, c,
                           free if i == 0 else None)
                    tmp.give(s_, m)
                rt, rf = tmp2.take()
                c = act(rt[0:n, :], bank[0:n, 0:T2], ACT.Sqrt, m, rf, scale=scale, bias=eps[0:n, :])
                PB.give(bank, c)
                v = recip(rt[0:n, :], rt[0:n, :], c)
                return rt, v

            def spread(rt, n, i, after):
                bank, free = PB.take()
                m = mm(bank[:, 0:T2], C("ident", i, 1, n).to_broadcast([n, 128]), rt[0:n, :], True, True, after,
                       free)
                return bank, m

            rt, v = col_stats(lambda i: qkv[:, i, :], 8, 1.0, C("eps6"), silu_done)
            for i in range(8):
                bank, m = spread(rt, 8, i, v)
                s = BSCALE if i < 4 else 1.0
                v2 = stt(qkv[:, i, :], qkv[:, i, :], s, bank[:, 0:T2], ALU.mult, ALU.mult, m)
                PB.give(bank, v2)
            tmp2.give(rt, P.last)
            for t, (t0, t1) in enumerate(tiles):
                n = t1 - t0
                for which, dst in ((4, ktok), (8, vtok)):
                    bank, free = PB.take()
                    for h in range(4):
                        tok = tr(bank[0:n, 128 * h:128 * h + 128], qkv[:, which + h, t0:t1], 128, free, v2,
                                 silu_done)
                    v = vcopy(dst[0:n, t, :, :], bank[0:n, :].rearrange("p (h n) -> p h n", h=4), tok)
                    PB.give(bank, v)

            oA = mX[:, 0:4, :]
            o_base = o
            W = [W2[:, NW2 - 512 * (i + 1):NW2 - 512 * i] for i in range(9)] + \
                [rX[:, 512 * i:512 * i + 512] for i in range(4)] + [sq[:, 512 * i:512 * i + 512] for i in range(4)]
            assert o - FT * T2 <= NW2 - 9 * 512
            hs = [x.rearrange("p (h n) -> p h n", h=4) for x in W]
            Mm, DT, MT, X, XT, Yb, CT, EG, kb, vb, kd, wT, u, QK, St, Gd, qe = hs
            smask = C("lm")
            tiles_free = [P.last]
            for t, (t0, t1) in enumerate(tiles):
                n = t1 - t0
                for h in range(4):
                    v = vts(Gd[0:n, h, 0:n], C("upper", 0, n, n), gb[0:n, t, h:h + 1], None, ALU.mult, None,
                            P.last if h == 0 else None)
                bank, free = PB.take()
                g3 = bank[:, :].rearrange("p (h n) -> p h n", h=4)
                for h in range(4):
                    tok = mm(g3[:, h, 0:n], C("ones", 0, 128, n), Gd[0:n, h, 0:n], h == 0, h == 3, v, free,
                             skip_group_check=True)
                for h in range(4):
                    stt(Mm[0:n, h, 0:n], g3[0:n, h, 0:n], gc[0:n, t, h:h + 1], C("um", 0, n, n), ALU.subtract,
                        ALU.add, tok)
                    v = stt(DT[0:n, h, 0:n], g3[0:n, h, 0:n], gc[0:n, t, h:h + 1], C("umt", 0, n, n),
                            ALU.subtract, ALU.add)
                c1 = act(EG[:, :, 0:n], g3[:, :, 0:n], ACT.Exp, v, P.last)
                PB.give(bank, c1)
                act(Mm[0:n, :, 0:n], Mm[0:n, :, 0:n], ACT.Exp, scale=-1.0)
                c = act(DT[0:n, :, 0:n], DT[0:n, :, 0:n], ACT.Exp)
                bank, free = PB.take()
                k3 = bank[:, :].rearrange("p (h n) -> p h n", h=4)
                for h in range(4):
                    tok = mm(k3[0:n, h, 0:n], qkv[:, 4 + h, t0:t1], qkv[:, 4 + h, t0:t1], h == 0, h == 3, free,
                             skip_group_check=True)
                for h in range(4):
                    v = stt(Mm[0:n, h, 0:n], k3[0:n, h, 0:n], be[0:n, t, h:h + 1], Mm[0:n, h, 0:n], ALU.mult,
                            ALU.mult, tok, c)
                PB.give(bank, v)
                bank, free = PB.take()
                m3 = bank[:, :].rearrange("p (h n) -> p h n", h=4)
                for h in range(4):
                    tok = tr(m3[0:n, h, 0:n], Mm[0:n, h, 0:n], n, v, free)
                c = act(MT[0:n, :, 0:n], m3[0:n, :, 0:n], ACT.Copy, tok)
                PB.give(bank, c)
                lb = lambda nm, l: C(nm, 128 * l, n, n).unsqueeze(1).to_broadcast([n, 4, n])
                ib = C("ident", 0, n, n).unsqueeze(1).to_broadcast([n, 4, n])
                vtt(X[0:n, :, 0:n], Mm[0:n, :, 0:n], lb("lm", 0), ALU.mult, P.last)
                vtt(X[0:n, :, 0:n], ib, X[0:n, :, 0:n], ALU.subtract)
                vtt(XT[0:n, :, 0:n], MT[0:n, :, 0:n], lb("lmt", 0), ALU.mult, c)
                x_tok = vtt(XT[0:n, :, 0:n], ib, XT[0:n, :, 0:n], ALU.subtract)
                levels = 7 if n == 128 else 4
                for l in range(1, levels):
                    gct = vtt(CT[0:n, :, 0:n], MT[0:n, :, 0:n], lb("lmt", l), ALU.mult, c, P.last, q=G)
                    bank, free = PB.take()
                    b3 = bank[:, :].rearrange("p (h n) -> p h n", h=4)
                    for h in range(4):
                        tok = mm(b3[0:n, h, 0:n], CT[0:n, h, 0:n], X[0:n, h, 0:n], h == 0, h == 3, gct, x_tok,
                                 free, skip_group_check=True)
                    cy = act(Yb[0:n, :, 0:n], b3[0:n, :, 0:n], ACT.Copy, tok)
                    PB.give(bank, cy)
                    bank2, free2 = PB.take()
                    b4 = bank2[:, :].rearrange("p (h n) -> p h n", h=4)
                    for h in range(4):
                        tok2 = mm(b4[0:n, h, 0:n], Yb[0:n, h, 0:n], XT[0:n, h, 0:n], h == 0, h == 3, cy, free2,
                                  skip_group_check=True)
                    if l < levels - 1:
                        bank, free = PB.take()
                        b5 = bank[:, :].rearrange("p (h n) -> p h n", h=4)
                        for h in range(4):
                            tok = mm(b5[0:n, h, 0:n], XT[0:n, h, 0:n], Yb[0:n, h, 0:n], h == 0, h == 3, cy,
                                     free, skip_group_check=True)
                        v = vtt(X[0:n, :, 0:n], X[0:n, :, 0:n], b5[0:n, :, 0:n], ALU.subtract, tok)
                        PB.give(bank, v)
                        tok2 = [tok2, tok]
                    x_tok = vtt(XT[0:n, :, 0:n], XT[0:n, :, 0:n], b4[0:n, :, 0:n], ALU.subtract, tok2)
                    PB.give(bank2, x_tok)
                for h in range(4):
                    vts(vb[0:n, h, :], vtok[0:n, t, h, :], be[0:n, t, h:h + 1], None, ALU.mult, free=h > 0)
                    vts(kb[0:n, h, :], ktok[0:n, t, h, :], ge[0:n, t, h:h + 1], None, ALU.mult, free=True)
                    v = vts(kd[0:n, h, :], ktok[0:n, t, h, :], gk[0:n, t, h:h + 1], None, ALU.mult, None, A.last,
                            free=True)
                v = vtt(qe[:, :, 0:n], qkv[:, 0:4, t0:t1], EG[:, :, 0:n], ALU.mult, c1, free=True)
                bank, free = PB.take()
                u3 = bank[:, :].rearrange("p (h n) -> p h n", h=4)
                for h in range(4):
                    tok = mm(u3[0:n, h, :], XT[0:n, h, 0:n], vb[0:n, h, :], h == 0, h == 3, v, free,
                             skip_group_check=True)
                c = act(u[0:n, :, :], u3[0:n, :, :], ACT.Copy, tok)
                PB.give(bank, c)
                if t > 0:
                    bank, free = PB.take()
                    w3 = bank[:, :].rearrange("p (h n) -> p h n", h=4)
                    for h in range(4):
                        tok = mm(w3[:, h, 0:n], kb[0:n, h, :], XT[0:n, h, 0:n], h == 0, h == 3, free,
                                 skip_group_check=True)
                    c = act(wT[:, :, 0:n], w3[:, :, 0:n], ACT.Copy, tok)
                    PB.give(bank, c)
                bank, free = PB.take()
                q3_ = bank[:, :].rearrange("p (h n) -> p h n", h=4)
                for h in range(4):
                    tok = mm(q3_[0:n, h, 0:n], qkv[:, 4 + h, t0:t1], qkv[:, h, t0:t1], h == 0, h == 3, free,
                             skip_group_check=True)
                v = vtt(QK[0:n, :, 0:n], q3_[0:n, :, 0:n], DT[0:n, :, 0:n], ALU.mult, tok)
                PB.give(bank, v)
                if t > 0:
                    bank, free = PB.take()
                    s3 = bank[:, :].rearrange("p (h n) -> p h n", h=4)
                    for h in range(4):
                        tok = mm(s3[0:n, h, :], wT[:, h, 0:n], St[:, h, :], h == 0, h == 3, free, c, v,
                                 skip_group_check=True)
                    v = vtt(u[0:n, :, :], u[0:n, :, :], s3[0:n, :, :], ALU.subtract, tok)
                    PB.give(bank, v)
                bank, free = PB.take()
                o3 = bank[:, :].rearrange("p (h n) -> p h n", h=4)
                for h in range(4):
                    if t > 0:
                        mm(o3[:, h, 0:n], St[:, h, :], qe[:, h, 0:n], h == 0, False, free, v,
                           skip_group_check=True)
                    tok = mm(o3[:, h, 0:n], u[0:n, h, :], QK[0:n, h, 0:n], t == 0 and h == 0, h == 3, free, v,
                             c, skip_group_check=True)
                v2 = vcopy(oA[:, :, t0:t1], o3[:, :, 0:n], tok)
                PB.give(bank, v2)
                if t < 2:
                    bank, free = PB.take()
                    d3 = bank[:, :].rearrange("p (h n) -> p h n", h=4)
                    for h in range(4):
                        tok = mm(d3[:, h, :], kd[0:n, h, :], u[0:n, h, :], h == 0, h == 3, free, v,
                                 skip_group_check=True)
                    for h in range(4):
                        if t == 0:
                            v = vcopy(St[:, h, :], d3[:, h, :], tok)
                        else:
                            v = stt(St[:, h, :], St[:, h, :], gl[:, t, h:h + 1], d3[:, h, :], ALU.mult,
                                    ALU.add, tok)
                    PB.give(bank, v)
            rt, v = col_stats(lambda i: oA[:, i, :], 4, 1.0 / 128, C("eps6"), V.last)
            for i in range(4):
                bank, m = spread(rt, 4, i, v)
                v2 = stt(oA[:, i, :], oA[:, i, :], C("a_out_norm", layer, 1), bank[:, 0:T2], ALU.mult,
                         ALU.mult, m)
                PB.give(bank, v2)
                v2 = vtt(oA[:, i, :], oA[:, i, :], zz[:, i, :], ALU.mult, silu_done)
            tmp2.give(rt, P.last)
            oa_ready = v2

            free_w = [P.last, V.last, A.last, G.last]
            o = FT * T2 + 3072
            score = area(S)
            work = area(2 * S).rearrange("p (a n) -> p a n", a=2)
            smk = area(2 * T2).rearrange("p (a n) -> p a n", a=2)

            def rope2(src, rot, cos, sin, after):
                bank, free = PB.take()
                m = mm(bank[:, 0:T2], C(rot), src, True, True, after, free)
                t2, tf = tmp.take()
                v = vtt(t2, bank[:, 0:T2], C(sin), ALU.mult, m, tf)
                PB.give(bank, v)
                vtt(src, src, C(cos), ALU.mult, m)
                v = vtt(src, src, t2, ALU.add)
                tmp.give(t2, v)
                return v

            rt, v = col_stats(lambda i: qb[:, i, :] if i < 4 else kb_, 5, 1.0 / 128, C("eps6"), raws)
            for i in range(5):
                dst = qb[:, i, :] if i < 4 else kb_
                bank, m = spread(rt, 5, i, v)
                v2 = stt(dst, dst, C("q_norm" if i < 4 else "k_norm", layer, 1), bank[:, 0:T2], ALU.mult,
                         ALU.mult, m)
                PB.give(bank, v2)
            tmp2.give(rt, P.last)
            s_, tf = tmp.take()
            c = act(s_, ik, ACT.Square, tf, raws)
            bank, free = PB.take()
            m = mm(bank[:, 0:T2], C("mean64"), s_, True, True, c, free)
            c = act(s_, bank[:, 0:T2], ACT.Sqrt, m, bias=C("eps6"))
            PB.give(bank, c)
            v = recip(s_, s_, c)
            v = stt(ik, ik, C("kidx", layer, 1), s_, ALU.mult, ALU.mult)
            tmp.give(s_, v)
            for i in range(4):
                rope2(qb[:, i, :], "rota", "cosa", "sina", v)
            rope2(kb_, "rota", "cosa", "sina", v)
            for i in range(4):
                rope2(iq[:, i, :], "roti", "cosi", "sini", v)
            roped2 = rope2(ik, "roti", "cosi", "sini", v)
            IS = float(8 ** -0.5 * 64 ** -0.5)
            iwt = sm[:, 456:472].rearrange("p (t n) -> p t n", t=2)
            iw_tok = vts(iwt, sml[:, 1:3, 8:16], IS, None, ALU.mult)
            for t in (1, 2):
                t0, t1 = tiles[t]
                bks = [PB.take() for _ in range(4)]
                toks = []
                for h in range(8):
                    p0 = 64 * (h % 2)
                    b = 2 * (h // 4) + h % 2
                    bank, free = bks[b]
                    cc = 256 * ((h // 2) % 2)
                    toks.append(mm(bank[:, cc:cc + 256], iq[p0:p0 + 64, h // 2, t0:t1],
                                   ik[p0:p0 + 64, NM:T2], (h // 2) % 2 == 0, (h // 2) % 2 == 1, free, roped2,
                                   skip_group_check=True))
                for h in range(8):
                    b = 2 * (h // 4) + h % 2
                    cc = 256 * ((h // 2) % 2)
                    src = bks[b][0][:, cc:cc + 256]
                    if h == 0:
                        v = vts(score, src, 0.0, iwt[:, t - 1, h:h + 1], ALU.max, ALU.mult, toks, free_w)
                    else:
                        s_, tf = tmp.take()
                        v = vts(s_[:, 0:S], src, 0.0, iwt[:, t - 1, h:h + 1], ALU.max, ALU.mult, tf)
                        v = vtt(score, score, s_[:, 0:S], ALU.add)
                        tmp.give(s_, v)
                for bank, _ in bks:
                    PB.give(bank, v)
                vtt(score, score, C("valid", 256 * (t - 1), 256), ALU.add)
                cur = score
                mx8 = sm[:, 472:480]
                for r in range(8):
                    nxt = work[:, r % 2, :]
                    V(lambda e, cur=cur: e.max(mx8, cur))
                    V(lambda e, cur=cur, nxt=nxt: e.match_replace(nxt, mx8, cur, -3e38))
                    cur = nxt
                V(lambda e, t=t: e.memset(smk[:, t - 1, 0:NM], 0.0))
                vtt(smk[:, t - 1, NM:T2], cur, score, ALU.is_equal)
                sel = vts(smk[:, t - 1, NM:T2], smk[:, t - 1, NM:T2], -BIG, None, ALU.mult)

            units = [(h, t) for t in (1, 2) for h in range(4)] + [(h, 0) for h in range(4)]
            ob = {}
            st = {}
            n_u = len(units)
            for i in range(n_u + 2):
                if i < n_u:
                    h, t = units[i]
                    t0, t1 = tiles[t]
                    n = t1 - t0
                    nk = T2 if t else NM
                    bank, free = PB.take()
                    tok = mm(bank[0:n, 0:nk], qb[:, h, t0:t1], kb_[:, 0:nk], True, True, free, roped2)
                    sc, f = sc_slots.take()
                    s2, f2 = st_slots.take()
                    if t:
                        v = stt(sc[0:n, 0:nk], bank[0:n, 0:nk], BSCALE, smk[0:n, t - 1, :], ALU.mult, ALU.add,
                                tok, f, sel, free_w)
                    else:
                        v = vts(sc[0:n, 0:nk], bank[0:n, 0:nk], BSCALE, None, ALU.mult, None, tok, f, free_w)
                    PB.give(bank, v)
                    v = V(lambda e, a_=s2[0:n, 0:1], b_=sc[0:n, 0:nk]: e.tensor_reduce(a_, b_, AX.X, ALU.max,
                                                                                     negate=True), f2)
                    c = act(sc[0:n, 0:nk], sc[0:n, 0:nk], ACT.Exp, v, bias=s2[0:n, 0:1],
                            accum_out=s2[0:n, 1:2])
                    recip(s2[0:n, 1:2], s2[0:n, 1:2], c)
                    v = vts(sc[0:n, 0:nk], sc[0:n, 0:nk], s2[0:n, 1:2], None, ALU.mult)
                    st_slots.give(s2, v)
                    st[i] = (sc, v)
                if 1 <= i <= n_u:
                    h, t = units[i - 1]
                    t0, t1 = tiles[t]
                    n = t1 - t0
                    sc, v = st[i - 1]
                    bank, free = PB.take()
                    pt, f = pt_slots.take()
                    for j, (k0, k1) in enumerate(tiles if t else tiles[:1]):
                        tok = tr(bank[0:k1 - k0, 128 * j:128 * j + n], sc[0:n, k0:k1], n,
                                 [free, v])
                    sc_slots.give(sc, tok)
                    c = act(pt[0:NM, 0:n], bank[0:NM, 0:n], ACT.Copy, tok, f, free_w)
                    if t:
                        c = act(pt[:, 128:384], bank[:, 128:384], ACT.Copy)
                    PB.give(bank, c)
                    st[i - 1] = (pt, c)
                if i >= 2:
                    h, t = units[i - 2]
                    t0, t1 = tiles[t]
                    n = t1 - t0
                    pt, c = st[i - 2]
                    bank, free = PB.take()
                    kts = tiles if t else tiles[:1]
                    for j, (k0, k1) in enumerate(kts):
                        tok = mm(bank[:, 0:n], vv[0:k1 - k0, j, :], pt[0:k1 - k0, 128 * j:128 * j + n], j == 0,
                                 j == len(kts) - 1, free, c)
                    pt_slots.give(pt, tok)
                    v = vcopy(mX[:, 4 + h, t0:t1], bank[:, 0:n], tok)
                    PB.give(bank, v)
            ob_ready = V.last

            v = parts(mH[:, :, :], mL[:, :, :], mX[:, :, :], ob_ready, oa_ready, P.last, V.last, G.last)
            y_ready = {}
            free_y = [P.last, V.last]
            for pr in range(4):
                sg = {}
                for z in range(2):
                    ch = S_.take(KT, 256)
                    for i in range(2):
                        bank, free = PB.take()
                        tok = group(bank[:, 0:T2], 0, T2, ch, 128 * i, 0, KT, n_, True, True, [free, ch.ready])
                        s_, tf = tmp.take()
                        c = act(s_, bank[:, 0:T2], ACT.Sigmoid, tok, tf, free=True,
                                bias=C("b_gate", 16 * layer + 8 * z + 2 * pr + i, 1))
                        PB.give(bank, c)
                        sg[z, i] = (s_, c)
                    ch.done(tok)
                ch = S_.take(KT, 256)
                for i in range(2):
                    for z in range(2):
                        s_, c = sg[z, i]
                        bank, free = PB.take()
                        for k in range(4):
                            kk_ = 4 * z + k
                            w_ = slice(128 * i, 128 * i + 128)
                            tok = mm3(bank[:, 0:T2], ch.h[:, kk_, w_], ch.l[:, kk_, w_], mH[:, kk_, :],
                                      mL[:, kk_, :], k == 0, k == 3, [free, ch.ready, v] if k == 0 else None)
                        c = vtt(s_, s_, bank[:, 0:T2], ALU.mult, c, tok)
                        PB.give(bank, c)
                    g = 2 * pr + i
                    s0, s1_ = sg[0, i][0], sg[1, i][0]
                    c = vtt(s0, s0, s1_, ALU.add)
                    y_ready[g] = parts(yH[:, g, :], yL[:, g, :], s0, c, free_y)
                    tmp.give(s0, y_ready[g])
                    tmp.give(s1_, c)
                ch.done(tok)
            h_rdy = {}

            def addh(key, ps, tk):
                h_rdy[key] = vtt(hX[:, key, :], hX[:, key, :], ps, ALU.add, tk, free=True)
                return h_rdy[key]

            for c in range(4):
                product([2 * c, 2 * c + 1], (yH, yL), 0, T2, [y_ready[g] for g in range(8)], addh)
            n_ready = rms_norm("norm_ffn", layer, h_rdy)
            h_ready = {}
            free_ff = [P.last, V.last, A.last]

            def pair2(j, ba, ta, bb, tb_):
                s_, tf = tmp.take()
                cw = lambda i: C("conv_ffn", (layer * 22 + j) * 3 + i, 1)
                vts(s_, ba[:, 0:T2], cw(2), None, ALU.mult, None, ta, tf)
                stt(s_[:, 1:T2], ba[:, 0:T2 - 1], cw(1), s_[:, 1:T2], ALU.mult, ALU.add)
                v = stt(s_[:, 2:T2], ba[:, 0:T2 - 2], cw(0), s_[:, 2:T2], ALU.mult, ALU.add)
                PB.give(ba, v)
                c = act(s_, s_, ACT.Silu, v, free=True)
                v = vtt(s_, s_, bb[:, 0:T2], ALU.mult, c, tb_)
                PB.give(bb, v)
                h_ready[j] = parts(hH[:, j, :], hL[:, j, :], s_, v, free_ff)
                tmp.give(s_, h_ready[j])

            ffn_in(n_ready, 0, T2, pair2)
            ffn_out(h_ready, 0, T2, addh)

        n_out = 0
        for k in range(KT):
            n_out += 16
            last = dma(Y, a["out"][:, k, :], hX[:, k, NM:T2], s_out, n_out, h_rdy[k])
        Y.ops.append((None, [last], Token(None, 0), 0))

        number([P, V, A, G, Y])
        block = ctx.enter_context(nc.Block())

        @block.sync
        def _(eng):
            Y.emit(eng)

        @block.gpsimd
        def _(eng):
            G.emit(eng)

        @block.scalar
        def _(eng):
            A.emit(eng)

        @block.tensor
        def _(eng):
            P.emit(eng)

        @block.vector
        def _(eng):
            V.emit(eng)


def _pack(inp):
    pk = np.zeros((128, NPACK), np.float32)

    def put(name, v):
        v = np.asarray(v)
        v = v.reshape(v.shape[0], -1)
        pk[0:v.shape[0], AT[name]:AT[name] + v.shape[1]] = v

    i, j = np.arange(128)[:, None], np.arange(128)[None, :]
    put("ident", np.eye(128))
    put("ones", np.ones((128, 128)))
    put("mean", np.full((128, 128), 1 / 1024))
    put("iota", np.broadcast_to(j, (128, 128)))
    put("slot", i)
    put("mean64", np.where(i // 64 == j // 64, 1 / 64, 0))
    put("upper", i <= j)
    q = np.arange(256).reshape(2, 128).T[:, :, None]
    k = np.arange(256)[None, None, :]
    put("swa", np.where((k // 64 <= q // 64) & (k // 64 >= q // 64 - 2), 0, -BIG))
    put("causal", np.where(k <= q, 0, -BIG))
    put("valid", np.where(k < (q // 64 + 1) * 64, 0, -BIG))
    rot = np.zeros((128, 128))
    for h in range(2):
        for d in range(8):
            rot[64 * h + d + 8, 64 * h + d] = -1
            rot[64 * h + d, 64 * h + d + 8] = 1
    put("rot1", rot)
    rot = np.zeros((128, 128))
    for d in range(64):
        rot[d + 64, d] = -1
        rot[d, d + 64] = 1
    put("rota", rot)
    rot = np.zeros((128, 128))
    for h in range(2):
        for d in range(32):
            rot[64 * h + d + 32, 64 * h + d] = -1
            rot[64 * h + d, 64 * h + d + 32] = 1
    put("roti", rot)
    for nm, dim in (("a", 128), ("i", 64)):
        inv = (1.0 / (np.float32(10000.0) ** (np.arange(0, dim, 2, dtype=np.float32) / np.float32(dim)))).astype(
            np.float32)
        ang = (np.arange(T2, dtype=np.float32)[None, :] * inv[:, None]).astype(np.float32).astype(np.float64)
        ang = np.concatenate([ang] * (256 // dim))
        put("cos" + nm, np.cos(ang))
        put("sin" + nm, np.sin(ang))
    put("um", np.where(j > i, BIG, 0))
    put("umt", np.where(j < i, -BIG, 0))
    lm = np.zeros((128, 7, 128))
    for l in range(7):
        b = 1 << l
        lm[:, l] = (i // (2 * b) == j // (2 * b)) & (i // b % 2 == 1) & (j // b % 2 == 0)
    put("lm", lm)
    put("lmt", lm.transpose(2, 1, 0))
    put("colsel", np.broadcast_to(np.arange(15) == 7, (128, 15)))
    f = np.zeros((128, 1), np.float32)
    for h in range(2):
        for d in range(16):
            f[64 * h + d] = INV1[d % 8]
    put("inv1", f)
    put("eps5", np.full((128, 1), 1e-5))
    put("eps6", np.full((128, 1), 1e-6))

    def feat(x):
        x = np.asarray(x)
        return np.moveaxis(x.reshape(x.shape[:-1] + (-1, 128)), -1, 0)

    for nm in ("ln_attn_g", "ln_attn_b", "ln_ffn_g", "ln_ffn_b"):
        put(nm, feat(inp[nm]))
    put("norm_mix", feat(inp["norm_mix_2"]))
    put("norm_ffn", feat(inp["norm_ffn_2"]))

    def over(x):
        return np.broadcast_to(np.asarray(x).reshape(1, -1), (128, np.asarray(x).size))

    put("sinks", over(inp["attn_sinks"]))
    put("b_forget", over(inp["b_forget"]))
    put("b_router", over(inp["b_router"]))
    put("a_log", over(inp["a_log_2"]))
    put("dt_bias", over(inp["dt_bias_2"]))
    put("conv_a", np.asarray(inp["conv_a_2"]).reshape(2, 4, 12, 128).transpose(3, 0, 2, 1))
    put("conv_ffn", np.asarray(inp["conv_ffn_2"]).reshape(2, 3, 22, 128).transpose(3, 0, 2, 1))
    put("a_out_norm", feat(inp["a_out_norm_2"]))
    put("q_norm", feat(inp["q_norm_2"]))
    put("k_norm", feat(inp["k_norm_2"]))
    kx = np.asarray(inp["kidx_norm_2"]).T
    put("kidx", np.concatenate([kx, kx]))
    put("b_gate", feat(inp["b_gate_2"]))
    return pk


def _arrays(inp):
    c = np.ascontiguousarray
    f = lambda n: np.asarray(inp[n])

    def tokens(x):
        return c(x.reshape(x.shape[0], 8, 128).transpose(2, 1, 0))

    def down(w):
        lead = w.shape[:-2]
        w = w.reshape(lead + (2, 11, 128, 8, 128))
        n = len(lead)
        return c(w.transpose(tuple(range(n)) + (n + 3, n, n + 2, n + 1, n + 4)))

    w = f("w_in_swa")[0]
    kd = [w[:, 768 + 64 * h:832 + 64 * h] for h in range(3) for _ in range(2)]
    w_swa = np.concatenate([w[:, 0:768]] + kd + [w[:, 1152:1408], w[:, 960:1152]], axis=1)
    w2 = f("w_in_2")
    w_in_2 = np.concatenate([w2[:, :, 0:2048], w2[:, :, 2696:2824], w2[:, :, 2048:2056], w2[:, :, 3400:3408],
                             np.zeros((2, 1024, 112), np.float32), w2[:, :, 2056:2568], w2[:, :, 2824:3336],
                             w2[:, :, 2568:2696], w2[:, :, 3336:3400], w2[:, :, 3336:3400]], axis=2)

    def up(w):
        lead = w.shape[:-2]
        n = len(lead)
        w = w.reshape(lead + (2, 4, 128, 2, 11, 256))
        w = w.transpose(tuple(range(n)) + (n + 4, n, n + 2, n + 1, n + 3, n + 5))
        return c(w.reshape(lead + (11, 2, 128, 4, 512)))

    return {
        "pack": _pack(inp),
        "pos": c(np.broadcast_to(f("positions").reshape(1, S), (128, S))),
        "xT": tokens(f("x")[0]),
        "metaT": tokens(f("meta_tokens_2")),
        "memT": tokens(f("mem")[0]),
        "w_mem_kv": c(f("w_mem_kv")),
        "w_swa": c(w_swa),
        "w_fox": c(f("w_in_fox")[0][:, 0:2560]),
        "w_forget": c(f("w_in_fox")[0][:, 2560:].reshape(8, 128, 12).transpose(1, 0, 2)),
        "w_out": c(f("w_out")),
        "w_ffn_in": up(f("w_ffn_in")[0]),
        "w_ffn_out": down(f("w_ffn_out")[0]),
        "w_router": c(f("w_router")[0].reshape(8, 128, 8).transpose(1, 0, 2)),
        "w_exp_in": up(f("w_exp_in")[0]),
        "w_exp_out": c(f("w_exp_out")[0]),
        "w_in_2": c(w_in_2),
        "w_branch": np.concatenate([f("w_branch_a_2"), f("w_branch_b_2")], axis=1),
        "w_gate": c(f("w_gate_2")),
        "w_out_2": c(f("w_out_2")),
        "w_up": up(f("w_up_2")),
        "w_down": down(f("w_down_2")),
    }


def kernel(**inputs):
    import concourse.bacc as bacc
    from concourse.bass_utils import run_bass_kernel_spmd

    nc = bacc.Bacc("TRN2", target_bir_lowering=False, num_devices=1)
    arrays = _arrays(inputs)
    a = {}
    for name, x in arrays.items():
        a[name] = nc.dram_tensor(name, x.shape, mybir.dt.from_np(x.dtype), kind="ExternalInput").ap()
    a["out"] = nc.dram_tensor("out", (128, 8, S), F32, kind="ExternalOutput").ap()
    build(nc, a)
    r = run_bass_kernel_spmd(nc, [arrays], core_ids=[0])
    out = r.results[0]["out"]
    return np.ascontiguousarray(out.transpose(2, 1, 0).reshape(1, S, D))
```

```python
from contextlib import ExitStack

import numpy as np
import concourse.bass as bass
from concourse import mybir

F32 = mybir.dt.float32
F32R = mybir.dt.float32r
I32 = mybir.dt.int32
ALU = mybir.AluOpType
ACT = mybir.ActivationFunctionType
AX = mybir.AxisListType

D = 1024
KT = 8
S = 256
NM = 16
T2 = S + NM
FF = 2816
FT = FF // 128
NE = 8
DEPTH = 2
ALPHA = float((2.0 * DEPTH) ** 0.25)
SCALE = 0.125
BSCALE = float(128 ** -0.5)
BIG = 1e30
INV1 = [float.fromhex(x) for x in (
    '0x1.0000000000000p+0', '0x1.8d275e0000000p-3', '0x1.3411900000000p-5', '0x1.ddee9c0000000p-8',
    '0x1.72ba440000000p-10', '0x1.1f91f00000000p-12', '0x1.be21880000000p-15', '0x1.5a0f4e0000000p-17')]
TWO_PI_1 = 6.28125
TWO_PI_2 = float(np.float32(int((2 * np.pi - TWO_PI_1) * 2 ** 20) / 2 ** 20))
TWO_PI_3 = float(np.float32(2 * np.pi - TWO_PI_1 - TWO_PI_2))
MAGIC = 12582912.0

FIELDS = [
    ("ident", 128), ("ones", 128), ("mean", 128), ("iota", 128), ("slot", 1), ("mean64", 128), ("upper", 128),
    ("swa", 512), ("causal", 512), ("valid", 512), ("rot1", 128), ("rota", 128), ("roti", 128),
    ("cosa", T2), ("sina", T2), ("cosi", T2), ("sini", T2), ("um", 128), ("umt", 128),
    ("lm", 896), ("lmt", 896), ("colsel", 15), ("inv1", 1), ("eps5", 1), ("eps6", 1),
    ("ln_attn_g", 16), ("ln_attn_b", 16), ("ln_ffn_g", 16), ("ln_ffn_b", 16),
    ("norm_mix", 16), ("norm_ffn", 16), ("sinks", 12), ("b_forget", 12), ("b_router", 8),
    ("a_log", 8), ("dt_bias", 8), ("conv_a", 96), ("conv_ffn", 132), ("a_out_norm", 2),
    ("q_norm", 2), ("k_norm", 2), ("kidx", 2), ("b_gate", 32),
]
AT = {}
_n = 0
for _name, _w in FIELDS:
    AT[_name] = _n
    _n += _w
NPACK = _n

class Token:

    def __init__(self, sem, value=None):
        self.sem, self.value, self.used = sem, value, value is not None


class Queue:

    def __init__(self, sem, serial):
        self.sem, self.serial, self.ops, self.last = sem, serial, [], None

    def __call__(self, fn, *after, free=False):
        token = Token(self.sem)
        waits = flat(after)
        if self.serial and not free and self.last is not None:
            waits.append(self.last)
        self.ops.append((fn, waits, token, 1))
        self.last = token
        return token

    def branch(self, flag, after):
        b = Branch(flag, flat(after), Token(self.sem))
        self.ops.append(b)
        return b

    def emit(self, eng, ops=None, seen=None):
        ops, seen = (self.ops, {}) if ops is None else (ops, seen)

        def wait(tokens):
            need = {}
            for w in tokens:
                if w.value > need.get(w.sem, 0):
                    need[w.sem] = w.value
            for sem, value in need.items():
                if seen.get(sem, 0) < value:
                    eng.wait_ge(sem, value)
                    seen[sem] = value

        for op in ops:
            if isinstance(op, Branch):
                wait(op.waits)
                flag = eng.value_load(op.flag, min_val=0, max_val=1)
                entered = dict(seen)
                for guard, body, end in ((lambda: eng.If(flag > 0), op.taken, op.n_taken),
                                         (lambda: eng.Else(), op.other, op.n_other)):
                    with guard():
                        self.emit(eng, body, dict(entered))
                        if end < op.join.value:
                            eng.wait_ge(self.sem, end)
                            eng.sem_inc(self.sem, op.join.value - end)
                seen.clear()
                seen.update(entered)
                continue
            fn, waits, token, by = op
            wait(waits)
            if fn is None:
                continue
            ins = fn(eng)
            if token.used:
                ins.then_inc(token.sem, by)


class Branch:
    def __init__(self, flag, waits, join):
        self.flag, self.waits, self.join = flag, waits, join
        self.taken, self.other = [], []


def flat(xs):
    out = []
    for x in xs:
        if x is None:
            continue
        if isinstance(x, (list, tuple)):
            out += flat(x)
        else:
            out.append(x)
    return out


def number(queues):
    def mark(ops):
        for op in ops:
            if isinstance(op, Branch):
                for w in op.waits:
                    w.used = True
                for body in (op.taken, op.other):
                    mark(body)
                    [x for x in body if x[0] is not None][-1][2].used = True
            else:
                for w in op[1]:
                    w.used = True

    def count(ops, n):
        for op in ops:
            if isinstance(op, Branch):
                op.n_taken, op.n_other = count(op.taken, n), count(op.other, n)
                n = op.join.value = max(op.n_taken, op.n_other)
            elif op[3] == 1 and op[2].used and op[2].value is None:
                n += 1
                op[2].value = n
        return n

    for q in queues:
        mark(q.ops)
    for q in queues:
        count(q.ops, 0)


class Slots:

    def __init__(self, views):
        self.rows = [[v, []] for v in views]

    def take(self):
        row = self.rows.pop(0)
        return row[0], row[1]

    def give(self, view, *tokens):
        self.rows.append([view, flat(tokens)])

    def all_free(self, n):
        assert len(self.rows) == n
        for row in self.rows:
            row[1] = []


def build(nc, a):
    ctx = ExitStack()
    with ctx:
        def sb(name, shape, dt=F32):
            return ctx.enter_context(nc.sbuf_tensor(name, shape, dt))

        def sem(name):
            return ctx.enter_context(nc.semaphore(name))

        pk = sb("pk", [128, NPACK])
        NR = 5
        NH = 3
        CH = 2048
        wH = [sb(f"wH{i}", [128, CH], F32R) for i in range(NH)]
        hX = sb("hX", [128, KT, T2])
        rX = sb("rX", [128, KT * T2])
        sq = sb("sq", [128, KT * T2])
        mX = sb("mX", [128, KT, T2])
        TM = sb("TM", [128, 8, T2])
        sm = sb("sm", [128, 512])
        sb_flag = sb("flag", [128, 1], I32)
        sb_small = sb("small_w", [128, 96])
        base = (nc.sbuf_base + 31) // 32 * 32

        def at(name, shape, dt, off):
            return nc.alloc_sbuf_tensor_at(name, shape, dt, offset=base + 4 * (off + NR * CH + 2 * KT * T2))

        ring = [at(f"ring{i}", [128, CH], F32, -2 * KT * T2 - CH * (i + 1)) for i in range(NR)]
        ringL = [at(f"ringL{i}", [128, CH], F32R, -2 * KT * T2 - CH * (i + 1)) for i in range(NR)]
        nH = at("nH", [128, KT, T2], F32R, -2 * KT * T2)
        nL = at("nL", [128, KT, T2], F32R, -KT * T2)
        NW2 = 7696
        W1 = at("W1", [128, FT * T2], F32, 0)
        W2 = at("W2", [128, NW2], F32, FT * T2)
        kv1 = at("kv1", [128, 1024], F32, FT * T2 + NW2)
        mH = at("mH", [128, KT, T2], F32R, FT * T2 + NW2 - 2 * KT * T2)
        mL = at("mL", [128, KT, T2], F32R, FT * T2 + NW2 - KT * T2)
        yH = at("yH", [128, KT, T2], F32R, 0)
        yL = at("yL", [128, KT, T2], F32R, KT * T2)
        hH = at("hH", [128, FT, T2], F32R, 0)
        hL = at("hL", [128, FT, T2], F32R, FT * T2)
        gts = at("gts", [128, NE, S], F32, 2 * FT * T2)
        xgH = at("xgH", [128, KT, 128], F32R, 0)
        xgL = at("xgL", [128, KT, 128], F32R, 1024)
        hgH = at("hgH", [128, FT, 128], F32R, 2048)
        hgL = at("hgL", [128, FT, 128], F32R, 2048 + FT * 128)
        Pg = at("Pg", [128, 2, 2, 128], F32, 2048 + 2 * FT * 128)
        Pt = at("Pt", [128, 2, 256], F32, 2560 + 2 * FT * 128)
        banks = [ctx.enter_context(nc.psum_tensor(f"pb{i}", [128, 512], F32)) for i in range(8)]

        P = Queue(sem("s_pe"), False)
        V = Queue(sem("s_dve"), True)
        A = Queue(sem("s_act"), True)
        G = Queue(sem("s_pool"), True)
        Y = Queue(sem("s_sp"), False)
        PB = Slots(banks)
        ring_sems = [sem(f"s_ring{i}") for i in range(NR)]
        s_raw = sem("s_raw")
        s_used = sem("s_used")
        s_in = sem("s_in")
        s_mem = sem("s_mem")
        s_out = sem("s_out")

        def C(name, i=0, w=None, p=128):
            o = AT[name] + i
            return pk[0:p, o:o + (w if w is not None else dict(FIELDS)[name])]

        def dma(queue, out, src, s, total, *after):
            token = Token(s, total)
            queue.ops.append((lambda e: e.dma_start(out, src), flat(after), token, 16))
            return token

        plan = []

        def cols(w, c0, c1):
            plan.append((w.rearrange("(k p) n -> p k n", p=128)[:, :, c0:c1], w.shape[0] // 128, c1 - c0, True))

        def laid(w, split=True):
            plan.append((w, w.shape[1], w.shape[2], split))

        def plan_down(w):
            for g in range(KT):
                for z in range(2):
                    laid(w[g, z])

        def plan_up(w):
            for u in range(FT // 2):
                for z in range(2):
                    laid(w[u, z])

        for layer in range(2):
            for c in range(2):
                cols(a["w_mem_kv"][layer], 256 * c, 256 * c + 256)
        for layer in range(2):
            if layer == 0:
                for c in range(0, 1280, 256):
                    cols(a["w_swa"], c, c + 256)
                cols(a["w_swa"], 1280, 1408)
                cols(a["w_swa"], 1408, 1600)
            else:
                for c in range(0, 2560, 256):
                    cols(a["w_fox"], c, c + 256)
                laid(a["w_forget"], False)
            for c in range(4):
                cols(a["w_out"][layer], 256 * c, 256 * c + 256)
            if layer == 0:
                plan_up(a["w_ffn_in"])
                plan_down(a["w_ffn_out"])
            else:
                laid(a["w_router"], False)
                moe_at = len(plan)
                for e_ in range(NE):
                    plan_up(a["w_exp_in"][e_])
                    w = a["w_exp_out"][e_].rearrange("(k p) n -> p k n", p=128)
                    for c in range(FT // 2):
                        plan.append((w[:, 2 * c:2 * c + 2, :], 2, 1024, True))
                moe_end = len(plan)
        for layer in range(2):
            for c in (8, 0, 1, 2, 3, 4, 5, 13, 9, 10, 11, 12, 6, 7):
                cols(a["w_in_2"][layer], 256 * c, 256 * c + 256)
            for c in range(8):
                cols(a["w_gate"][layer], 256 * c, 256 * c + 256)
            for c in range(4):
                cols(a["w_branch"][layer], 256 * c, 256 * c + 256)
            for c in range(4):
                cols(a["w_out_2"][layer], 256 * c, 256 * c + 256)
            plan_up(a["w_up"][layer])
            plan_down(a["w_down"][layer])

        def queue_stream(first, end):
            for c in range(first, end):
                src, kt, n, _ = plan[c]
                i = c % NR
                dst = ring[i][:, 0:kt * n].rearrange("p (k n) -> p k n", k=kt)
                dma(Y, dst, src, ring_sems[i], 16 * (c // NR + 1), Token(s_used, c - NR + 1) if c >= NR else None)

        class Stream:

            def __init__(self):
                self.c = self.ahead = 0
                self.limit = moe_at

            def split(self):
                c = self.ahead
                self.ahead += 1
                _, kt, n, parts = plan[c]
                low = ringL[c % NR][:, 0:kt * n]
                raw = ring[c % NR][:, 0:kt * n]
                landed = Token(ring_sems[c % NR], 16 * (c // NR + 1))
                if parts:
                    h = wH[c % NH][:, 0:kt * n]
                    t = act(h, raw, ACT.Copy, landed, Token(s_used, c - NH + 1) if c >= NH else None, free=True)
                    fn = lambda e: e.tensor_tensor(low, raw, h.bitcast(F32), ALU.subtract)
                else:
                    t = P.last
                    fn = lambda e: e.tensor_copy(small_w[:, 0:kt * n], raw)
                token = Token(s_raw, c + 1)
                V.ops.append((fn, flat([t, landed]), token, 1))
                V.last = token

            def take(self, kt, n):
                c = self.c
                self.c += 1
                assert plan[c][1:3] == (kt, n), (c, plan[c][1:3], kt, n)
                while self.ahead <= min(c + NH - 1, self.limit - 1):
                    self.split()
                v = lambda b: b[:, 0:kt * n].rearrange("p (k n) -> p k n", k=kt)
                if not plan[c][3]:
                    return Chunk(c, v(small_w), None)
                return Chunk(c, v(wH[c % NH]), v(ringL[c % NR]))

        class Chunk:
            def __init__(self, c, h, l):
                self.c, self.h, self.l = c, h, l
                self.ready = Token(s_raw, c + 1)

            def done(self, token):
                token.sem, token.value, token.used = s_used, self.c + 1, True

        small_w = sb_small
        def mm(out, lhsT, rhs, start, stop, *after, **kw):
            return P(lambda e: e.matmul(out, lhsT, rhs, start=start, stop=stop, **kw), *after)

        def tr(out, in_, n, *after):
            return P(lambda e: e.transpose(out, in_, C("ident", 0, n, n)), *after)

        def vtt(out, x, y, op, *after, q=None, free=False):
            return (q or V)(lambda e: e.tensor_tensor(out, x, y, op), *after, free=free)

        def vts(out, x, s1, s2, o1, o2=None, *after, free=False, q=None):
            if o2 is None:
                return (q or V)(lambda e: e.tensor_scalar(out, x, s1, None, o1), *after, free=free)
            return (q or V)(lambda e: e.tensor_scalar(out, x, s1, s2, o1, o2), *after, free=free)

        def stt(out, x, s, y, o1, o2, *after, free=False):
            return V(lambda e: e.scalar_tensor_tensor(out=out, in0=x, scalar=s, in1=y, op0=o1, op1=o2),
                     *after, free=free)

        def act(out, x, f, *after, free=False, **kw):
            return A(lambda e: e.activation(out, x, f, **kw), *after, free=free)

        def vcopy(out, x, *after, free=False):
            return V(lambda e: e.tensor_copy(out, x), *after, free=free)

        def recip(out, x, *after):
            return V(lambda e: e.reciprocal(out, x), *after)

        M_, A_, B_ = (0, NM), (NM, NM + 128), (NM + 128, T2)

        def mm3(out, lh, ll, rh, rl, start, stop, *after, **kw):
            mm(out, lh, rh, start, False, *after, **kw)
            mm(out, lh, rl, False, False, **kw)
            return mm(out, ll, rh, False, stop, **kw)

        def group(out, t0, t1, ch, c0, k0, kt, x, first, last, after, kw={}):
            for k in range(kt):
                tok = mm3(out, ch.h[:, k, c0:c0 + 128], ch.l[:, k, c0:c0 + 128], x[0][:, k0 + k, t0:t1],
                          x[1][:, k0 + k, t0:t1], first and k == 0, last and k == kt - 1,
                          after if k == 0 else None, **kw)
            return tok

        def product_steps(keys, x, t0, t1, after, evac):
            ch = S_.take(KT, 128 * len(keys))
            for i, key in enumerate(keys):
                bank, free = PB.take()
                for k in range(KT):
                    c_ = slice(128 * i, 128 * i + 128)
                    tok = mm3(bank[:, 0:t1 - t0], ch.h[:, k, c_], ch.l[:, k, c_], x[0][:, k, t0:t1],
                              x[1][:, k, t0:t1], k == 0, k == KT - 1, [free, ch.ready, after] if k == 0 else None)
                    if k == 3:
                        yield
                if i == len(keys) - 1:
                    ch.done(tok)
                yield
                PB.give(bank, evac(key, bank[:, 0:t1 - t0], tok))

        def product(*args):
            for _ in product_steps(*args):
                pass

        def weave(strands):
            while strands:
                strands = [x for x in strands if next(x, 0) is None]

        def rows(n, x, tiles, after, evac):
            ch = S_.take(KT, n)
            for i, (t0, t1) in enumerate(tiles):
                bank, free = PB.take()
                for k in range(KT):
                    tok = mm3(bank[:, 0:n], x[0][:, k, t0:t0 + 128], x[1][:, k, t0:t0 + 128], ch.h[:, k, :],
                              ch.l[:, k, :], k == 0, k == KT - 1, [free, ch.ready, after] if k == 0 else None)
                PB.give(bank, evac(i, bank[0:t1 - t0, 0:n], tok))
            ch.done(tok)

        def few_rows(n, x, tiles, after, evac):
            ch = S_.take(KT, n)
            for i, (t0, t1) in enumerate(tiles):
                bank, free = PB.take()
                for k in range(KT):
                    tok = mm(bank[:, 0:n], x[:, k, t0:t1], ch.h[:, k, :], k == 0, k == KT - 1,
                             [free, ch.ready, after] if k == 0 else None)
                PB.give(bank, evac(i, bank[0:t1 - t0, 0:n], tok))
            ch.done(tok)

        def parts(h, l, x, *after):
            c = act(h, x, ACT.Copy, *after, free=True)
            return [c, vtt(l, x, h.bitcast(F32), ALU.subtract, c, *after, free=True)]

        S_ = Stream()

        in_tot = 0

        def load_in(out, src):
            nonlocal in_tot
            in_tot += 16
            return dma(Y, out, src, s_in, in_tot)

        sq_mem = sq[:, 0:KT * S].rearrange("p (k t) -> p k t", k=KT)
        mem_in = dma(Y, sq_mem, a["memT"], s_mem, 16)
        queue_stream(0, 2)
        load_in(pk[:, :], a["pack"])
        pos_i = TM[:, 0, 0:S].bitcast(I32)
        load_in(pos_i, a["pos"])
        load_in(hX[:, :, NM:T2], a["xT"])
        inputs = load_in(hX[:, :, 0:NM], a["metaT"])
        queue_stream(2, len(plan))

        r3 = rX[:, :].rearrange("p (k t) -> p k t", k=KT)
        q3 = sq[:, :].rearrange("p (k t) -> p k t", k=KT)

        def layer_norm(g, b, li, r_ready, split=True):
            act(sm[:, 504:505], C("eps5"), ACT.Sqrt)
            bank, free = PB.take()
            mu = bank[:, 0:S]
            for k in range(KT):
                t = mm(mu, C("mean"), r3[:, k, NM:T2], k == 0, k == KT - 1, free if k == 0 else None,
                       r_ready[k])
            bank2, free2 = PB.take()
            var = bank2[:, 0:S]
            for k in range(KT):
                d = vtt(r3[:, k, NM:T2], r3[:, k, NM:T2], mu, ALU.subtract, t, free=k > 0)
                s = act(q3[:, k, NM:T2], r3[:, k, NM:T2], ACT.Square, d, free=k > 0)
                t2 = mm(var, C("mean"), q3[:, k, NM:T2], k == 0, k == KT - 1, free2 if k == 0 else None, s)
            PB.give(bank, d)
            sd, tf = tmp.take()
            s = act(sd[:, 0:S], var, ACT.Sqrt, t2, tf, bias=C("eps5"))
            PB.give(bank2, s)
            rs = recip(sd[:, 0:S], sd[:, 0:S], s)
            readers = [P.last, V.last]
            out_ready = []
            for k in range(KT):
                v = vtt(r3[:, k, NM:T2], r3[:, k, NM:T2], sd[:, 0:S], ALU.mult, rs, free=k > 0)
                i = li * 8 + k
                aff = dict(scale=C(g, i, 1), bias=C(b, i, 1))
                c = act(hX[:, k, NM:T2], r3[:, k, NM:T2], ACT.Identity, v, readers, free=k > 0, **aff)
                if split:
                    h = nH[:, k, NM:T2]
                    c = act(h, r3[:, k, NM:T2], ACT.Identity, v, readers, free=True, **aff)
                    c = [c, vtt(nL[:, k, NM:T2], hX[:, k, NM:T2], h.bitcast(F32), ALU.subtract, c, free=True)]
                out_ready.append(c)
            tmp.give(sd, v)
            return out_ready

        def rms_norm(g, li, h_ready):
            h = hX
            act(sm[:, 504:505], C("eps6"), ACT.Sqrt)
            bank, free = PB.take()
            ms = bank[:, 0:T2]
            for k in range(KT):
                s = act(q3[:, k, :], h[:, k, :], ACT.Square, h_ready[k], P.last if k == 0 else None, free=k > 0)
                t = mm(ms, C("mean"), q3[:, k, :], k == 0, k == KT - 1, free if k == 0 else None, s)
            sd, tf = tmp.take()
            s = act(sd, ms, ACT.Sqrt, t, tf, bias=C("eps6"))
            PB.give(bank, s)
            rs = recip(sd, sd, s)
            ready = []
            readers = P.last
            for k in range(KT):
                v = stt(r3[:, k, :], h[:, k, :], C(g, li * 8 + k, 1), sd, ALU.mult, ALU.mult, rs, free=k > 0)
                c = act(nH[:, k, :], r3[:, k, :], ACT.Copy, v, readers, free=True)
                ready.append(vtt(nL[:, k, :], r3[:, k, :], nH[:, k, :].bitcast(F32), ALU.subtract, c, v,
                                 free=True))
            tmp.give(sd, ready[-1])
            return ready

        sc_slots = Slots([rX[:, 512 * i:512 * i + 512] for i in range(4)])
        pt_slots = Slots([sq[:, 512 * i:512 * i + 512] for i in range(4)])
        st_slots = Slots([sm[:, 8 * i:8 * i + 8] for i in range(6)])

        def attend(heads, ready):
            n = len(heads)
            st = {}
            for i in range(n + 3):
                if i < n:
                    h = heads[i]
                    bank, free = PB.take()
                    for t in range(2):
                        tok = mm(bank[:, 256 * t:256 * t + 256], h["q"][:, 128 * t:128 * t + 128], h["k"],
                                 t == 0, t == 1, [free, ready] if t == 0 else None, skip_group_check=True)
                    sc, f = sc_slots.take()
                    s2, f2 = st_slots.take()
                    v = h["add"](sc, bank, [tok, f])
                    PB.give(bank, v)
                    nm, den = s2[:, 0:2], s2[:, 2:4]
                    sc3 = sc.rearrange("p (t k) -> p t k", t=2)
                    v = V(lambda e, nm=nm, sc3=sc3: e.tensor_reduce(nm, sc3, AX.X, ALU.max, negate=True), f2)
                    if h.get("sink") is not None:
                        v = vts(nm, nm, h["sink_neg"], None, ALU.min)
                    for t in range(2):
                        c = act(sc[:, 256 * t:256 * t + 256], sc[:, 256 * t:256 * t + 256], ACT.Exp, v, free=True,
                                bias=nm[:, t:t + 1], accum_out=den[:, t:t + 1])
                    if h.get("sink") is not None:
                        c = act(s2[:, 4:6], nm, ACT.Exp, free=True, bias=h["sink"])
                    st[i] = (sc, s2, c)
                if 1 <= i <= n:
                    h = heads[i - 1]
                    sc, s2, c = st[i - 1]
                    den = s2[:, 2:4]
                    if h.get("sink") is not None:
                        vtt(den, den, s2[:, 4:6], ALU.add, c, free=True)
                        recip(den, den)
                    else:
                        V(lambda e, den=den: e.reciprocal(den, den), c, free=True)
                    for t in range(2):
                        v = vts(sc[:, 256 * t:256 * t + 256], sc[:, 256 * t:256 * t + 256], den[:, t:t + 1],
                                None, ALU.mult, free=t > 0)
                    st_slots.give(s2, v)
                    st[i - 1] = (sc, v)
                if 2 <= i <= n + 1:
                    sc, v = st[i - 2]
                    bank, free = PB.take()
                    for kt in range(2):
                        for t in range(2):
                            tok = tr(bank[:, 256 * kt + 128 * t:256 * kt + 128 * t + 128],
                                     sc[:, 256 * t + 128 * kt:256 * t + 128 * kt + 128], 128,
                                     [free, v] if kt + t == 0 else None)
                    sc_slots.give(sc, tok)
                    pt, f = pt_slots.take()
                    c = act(pt, bank[:, :], ACT.Copy, tok, f, free=True)
                    PB.give(bank, c)
                    st[i - 2] = (pt, c)
                if i >= 3:
                    j = i - 3
                    h = heads[j]
                    pt, c = st[j]
                    if j % 2 == 0:
                        obank, ofree = PB.take()
                    p0 = 64 * (j % 2)
                    for kt in range(2):
                        tok = mm(obank[p0:p0 + 64, 0:S], h["v"][kt], pt[:, 256 * kt:256 * kt + 256], kt == 0,
                                 kt == 1, [c, ofree] if kt == 0 else None)
                    pt_slots.give(pt, tok)
                    if j % 2 == 1:
                        v = vcopy(mX[:, h["tile"], NM:T2], obank[:, 0:S], tok, free=True)
                        PB.give(obank, v)
            return V.last

        n_ = (nH, nL)
        m_ = (mH, mL)
        hp = (hH, hL)

        def ffn_in(x_ready, t0, t1, on_pair):
            n = t1 - t0
            pairs = []
            for u in range(FT // 2):
                bk = [PB.take() for _ in range(4)]
                for z in range(2):
                    ch = S_.take(4, 512)
                    for x in pairs:
                        next(x, None)
                    pairs = []
                    toks = []
                    for i, (bank, free) in enumerate(bk):
                        toks.append(group(bank[:, 0:n], t0, t1, ch, 128 * i, 4 * z, 4, n_, z == 0, z == 1,
                                          [free, ch.ready, x_ready]))
                    ch.done(toks[-1])
                pairs = [on_pair(2 * u + g, bk[g][0], toks[g], bk[2 + g][0], toks[2 + g]) for g in range(2)]
                for _ in range(2):
                    for x in pairs:
                        next(x)
            for x in pairs:
                next(x, None)

        def ffn_out(h_ready, t0, t1, evac):
            n = t1 - t0
            for g in range(KT):
                bank, free = PB.take()
                for z in range(2):
                    ch = S_.take(FT // 2, 128)
                    tok = group(bank[:, 0:n], t0, t1, ch, 0, 11 * z, 11, hp, z == 0, z == 1,
                                [free, ch.ready, [h_ready[k] for k in range(11 * z, 11 * z + 11)]])
                    ch.done(tok)
                PB.give(bank, evac(g, bank[:, 0:n], tok))

        v = [parts(mH[:, k:k + 4, 0:S], mL[:, k:k + 4, 0:S], sq_mem[:, k:k + 4, :], mem_in) for k in (0, 4)]
        kv1_k = kv1[:, 0:512].rearrange("p (k t) -> p k t", k=2)
        kv1_v = kv1[:, 512:1024].rearrange("p (t n) -> p t n", t=2)
        kv0_k = W1[:, 5984 - 1024:5984 - 512].rearrange("p (k t) -> p k t", k=2)
        kv0_v = W1[:, 5984 - 512:5984].rearrange("p (t n) -> p t n", t=2)
        mem_ready = v
        for kd_, vd_ in ((kv0_k, kv0_v), (kv1_k, kv1_v)):
            product([0, 1], m_, 0, S, mem_ready,
                    lambda key, ps, tk: act(kd_[:, key, :], ps, ACT.Copy, tk, free=True))
            rows(256, m_, [(0, 128), (128, 256)], None, lambda i, ps, tk: vcopy(vd_[:, i, :], ps, tk, free=True))
        for q in (P, V, A, G):
            q.ops.append((None, [inputs], Token(None, 0), 0))
        x_ready = [parts(nH[:, k, NM:T2], nL[:, k, NM:T2], hX[:, k, NM:T2]) for k in range(KT)]

        cos1, sin1 = TM[:, 6, 0:S], TM[:, 7, 0:S]
        posf, ang, kk, r1 = TM[:, 1, 0:S], TM[:, 2, 0:S], TM[:, 3, 0:S], TM[:, 4, 0:S]
        vcopy(posf, pos_i)
        vts(ang, posf, C("inv1"), None, ALU.mult)
        vts(kk, ang, float(1 / (2 * np.pi)), MAGIC, ALU.mult, ALU.add)
        vts(kk, kk, MAGIC, None, ALU.subtract)
        stt(r1, kk, -TWO_PI_1, ang, ALU.mult, ALU.add)
        stt(r1, kk, -TWO_PI_2, r1, ALU.mult, ALU.add)
        stt(r1, kk, -TWO_PI_3, r1, ALU.mult, ALU.add)
        t = vts(r1, r1, 3.1415925, -3.1415925, ALU.min, ALU.max)
        act(sin1, r1, ACT.Sin, t)
        t = act(kk, r1, ACT.Sin, scale=0.5)
        vtt(kk, kk, kk, ALU.mult, t)
        rope1 = vts(cos1, kk, -2.0, 1.0, ALU.mult, ALU.add)
        rope1 = [rope1, A.last]

        tmp = Slots([TM[:, i, :] for i in range(4)])
        for i in range(4):
            v_, _ = tmp.take()
            tmp.give(v_, V.last, A.last)
        tmp2 = Slots([TM[:, i, :] for i in range(4, 6)])
        v_, _ = tmp2.take()
        tmp2.give(v_, V.last, A.last)
        for layer in range(2):
            o = 0
            lim = FT * T2 - (1024 if layer == 0 else 0)

            def area(n):
                nonlocal o
                if o < FT * T2 and o + n > lim:
                    o = FT * T2
                r = W1[:, o:o + n] if o < FT * T2 else W2[:, o - FT * T2:o - FT * T2 + n]
                o += n
                assert o <= FT * T2 + NW2
                return r

            qn = area(8 * S).rearrange("p (k t) -> p k t", k=8)
            kn = area((3 if layer == 0 else 6) * S).rearrange("p (k t) -> p k t", t=S)
            vn = area(2 * (192 if layer == 0 else 768)).rearrange("p (t n) -> p t n", t=2)
            km, vm = (kv0_k, kv0_v) if layer == 0 else (kv1_k, kv1_v)
            free_w = P.last

            def plain(dst):
                return lambda key, ps, tk: act(dst[:, key, :], ps, ACT.Copy, tk, free_w, free=True)

            if layer == 0:
                def roped(key, ps, tk):
                    dst = qn[:, key, :] if key < 8 else kn[:, key - 8, :]
                    raw, tf = tmp.take()
                    c = act(raw[:, 0:S], ps, ACT.Copy, tk, tf)
                    bank, free = PB.take()
                    m = mm(bank[:, 0:S], C("rot1"), raw[:, 0:S], True, True, c, free)
                    t2, tf2 = tmp2.take()
                    v = vtt(t2[:, 0:S], bank[:, 0:S], sin1, ALU.mult, m, tf2, rope1)
                    PB.give(bank, v)
                    vtt(dst, raw[:, 0:S], cos1, ALU.mult, c, free_w)
                    v = vtt(dst, dst, t2[:, 0:S], ALU.add)
                    tmp.give(raw, v)
                    tmp2.give(t2, v)
                    return c

                for c in range(3):
                    product([2 * c, 2 * c + 1], n_, NM, T2, x_ready if c == 0 else None, roped)
                product([8, 9], n_, NM, T2, None, roped)
                product([10, 6], n_, NM, T2, None,
                        lambda key, ps, tk: roped(key, ps, tk) if key == 10 else plain(qn)(key, ps, tk))
                product([7], n_, NM, T2, None, plain(qn))
                rows(192, n_, [A_, B_], None, lambda i, ps, tk: vcopy(vn[:, i, :], ps, tk, free_w))
                vts(sm[:, 64:76], C("sinks"), -1.0, None, ALU.mult)
                mask = C("swa")

                def add(sc, bank, after):
                    return stt(sc, bank[:, :], SCALE, mask, ALU.mult, ALU.add, after)

                heads = [dict(q=qn[64 * (i % 2):64 * (i % 2) + 64, i // 2, :],
                              k=kn[64 * (i % 2):64 * (i % 2) + 64, i // 4, :],
                              v=[vn[:, t, 64 * (i // 4):64 * (i // 4) + 64] for t in range(2)], add=add,
                              sink=C("sinks", i, 1), sink_neg=sm[:, 64 + i:65 + i], tile=i // 2)
                         for i in range(12)]
            else:
                cq = area(24).rearrange("p (t n) -> p t n", t=2)
                R = area(12 * S).rearrange("p (h t) -> p h t", t=S)
                ck = area(2 * S)
                dests = [(qn, i) for i in range(6)] + [(kn, i) for i in range(6)]

                def to(key, ps, tk):
                    d, i = dests[key]
                    return act(d[:, i, :], ps, ACT.Copy, tk, free_w, free=True)

                for c in range(6):
                    product([2 * c, 2 * c + 1], n_, NM, T2, x_ready if c == 0 else None, to)
                for c in range(3):
                    rows(256, n_, [A_, B_], None,
                         lambda i, ps, tk: vcopy(vn[:, i, 256 * c:256 * c + 256], ps, tk, free_w))
                product([6, 7], n_, NM, T2, None, plain(qn))
                lf = sm[:, 128:152].rearrange("p (t n) -> p t n", t=2)
                lg = sm[:, 152:176].rearrange("p (t n) -> p t n", t=2)
                ls = sm[:, 176:200].rearrange("p (t n) -> p t n", t=2)
                few_rows(12, hX, [A_, B_], None,
                         lambda i, ps, tk: vtt(lf[:, i, :], ps, C("b_forget"), ALU.add, tk))
                c = act(lg, lf, ACT.Abs, V.last)
                c = act(lg, lg, ACT.Exp, scale=-1.0)
                c = act(lg, lg, ACT.Ln, bias=1.0)
                lft = stt(ls, lf, 0.0, lg, ALU.min, ALU.subtract, c)
                bank, free = PB.take()
                mm(bank[:, 0:12], C("upper"), ls[:, 0, :], True, False, free, lft, skip_group_check=True)
                mm(bank[:, 16:28], C("upper"), ls[:, 1, :], False, False, skip_group_check=True)
                tok = mm(bank[:, 16:28], C("ones"), ls[:, 0, :], False, True, skip_group_check=True)
                v = vcopy(cq[:, 0, :], bank[:, 0:12], tok)
                v = vcopy(cq[:, 1, :], bank[:, 16:28], tok)
                PB.give(bank, v)
                bank, free = PB.take()
                for t in range(2):
                    tok = tr(bank[0:12, 128 * t:128 * t + 128], cq[:, t, :], 128, v, free)
                v = vcopy(ck[0:12, 0:S], bank[0:12, 0:S], tok)
                PB.give(bank, v)
                for h in range(12):
                    bank, free = PB.take()
                    tok = mm(bank[:, 0:S], C("ident", h, 1, 12).to_broadcast([12, 128]), ck[0:12, 0:S], True,
                             True, v, free)
                    c = act(R[:, h, :], bank[:, 0:S], ACT.Copy, tok, free=True)
                    PB.give(bank, c)
                tb = [tmp.take() for _ in range(2)]
                bias_buf = [x[0] for x in tb]
                bias_free = [x[1] for x in tb]

                def adder(h):
                    def add(sc, bank, after):
                        for t in range(2):
                            stt(bias_buf[t][:, 0:S], R[:, h, :], cq[:, t, h:h + 1], C("causal", 256 * t, 256),
                                ALU.subtract, ALU.subtract, c, bias_free, free=t > 0)
                        for t in range(2):
                            v = stt(sc[:, 256 * t:256 * t + 256], bank[:, 256 * t:256 * t + 256], SCALE,
                                    bias_buf[t][:, 0:S], ALU.mult, ALU.subtract, after, free=t > 0)
                        return v
                    return add

                heads = [dict(q=qn[64 * (i % 2):64 * (i % 2) + 64, i // 2, :],
                              k=kn[64 * (i % 2):64 * (i % 2) + 64, i // 2, :],
                              v=[vn[:, t, 64 * i:64 * i + 64] for t in range(2)], add=adder(i), tile=i // 2)
                         for i in range(12)]

            def add_mem(sc, bank, after):
                return vts(sc, bank[:, :], SCALE, None, ALU.mult, None, after)

            heads += [dict(q=qn[64 * (i % 2):64 * (i % 2) + 64, 6 + i // 2, :],
                           k=km[64 * (i % 2):64 * (i % 2) + 64, i // 2, :],
                           v=[vm[:, t, 64 * i:64 * i + 64] for t in range(2)], add=add_mem, tile=6 + i // 2)
                      for i in range(4)]
            mixed = attend(heads, [V.last, A.last])
            if layer == 1:
                for b in bias_buf:
                    tmp.give(b, V.last)

            r_ready = {}

            def res(key, ps, tk):
                r_ready[key] = stt(r3[:, key, NM:T2], hX[:, key, NM:T2], ALPHA, ps, ALU.mult, ALU.add, tk,
                                   P.last, A.last, free=True)
                return r_ready[key]

            v = parts(mH[:, :, NM:T2], mL[:, :, NM:T2], mX[:, :, NM:T2], mixed, P.last)
            for c in range(4):
                product([2 * c, 2 * c + 1], m_, NM, T2, v, res)
            x_ready = layer_norm("ln_attn_g", "ln_attn_b", layer, r_ready)

            if layer == 0:
                h_ready = {}
                free_ff = [P.last, V.last, A.last]

                def pair(j, ba, ta, bb, tb_):
                    s_, tf = tmp.take()
                    c = act(s_[:, 0:S], ba[:, 0:S], ACT.Silu, ta, tf, free=True)
                    PB.give(ba, c)
                    yield
                    v = vtt(s_[:, 0:S], s_[:, 0:S], bb[:, 0:S], ALU.mult, c, tb_, free=True)
                    PB.give(bb, v)
                    yield
                    h_ready[j] = parts(hH[:, j, NM:T2], hL[:, j, NM:T2], s_[:, 0:S], v, free_ff)
                    tmp.give(s_, h_ready[j])

                ffn_in(x_ready, NM, T2, pair)

                def down(g, ps, tk):
                    r_ready[g] = stt(r3[:, g, NM:T2], hX[:, g, NM:T2], ALPHA, ps, ALU.mult, ALU.add, tk,
                                     free=True)
                    return r_ready[g]

                ffn_out(h_ready, NM, T2, down)
                x_ready = layer_norm("ln_ffn_g", "ln_ffn_b", layer, r_ready)
            else:
                lo = sm[:, 200:216].rearrange("p (t n) -> p t n", t=2)
                few_rows(8, hX, [A_, B_], x_ready,
                         lambda i, ps, tk: vtt(lo[:, i, :], ps, C("b_router"), ALU.add, tk))
                gt_ = sm[:, 216:232].rearrange("p (t n) -> p t n", t=2)
                eq = sm[:, 232:248].rearrange("p (t n) -> p t n", t=2)
                cu = sm[:, 248:264].rearrange("p (t n) -> p t n", t=2)
                cv = sm[:, 264:280].rearrange("p (t n) -> p t n", t=2)
                ex = sm[:, 280:296].rearrange("p (t n) -> p t n", t=2)
                mx = sm[:, 296:312].rearrange("p (t n) -> p t n", t=2)
                s1 = sm[:, 312:314]
                for t in range(2):
                    V(lambda e, t=t: e.max(mx[:, t, :], lo[:, t, :]))
                    vts(gt_[:, t, :], lo[:, t, :], mx[:, t, 1:2], None, ALU.is_gt)
                    vts(eq[:, t, :], lo[:, t, :], mx[:, t, 1:2], None, ALU.is_equal)
                    v = vts(ex[:, t, :], lo[:, t, :], mx[:, t, 0:1], None, ALU.subtract)
                c = act(ex, ex, ACT.Exp, v)
                src, dst = eq, cu
                for sft in (1, 2, 4):
                    vcopy(dst[:, :, 0:sft], src[:, :, 0:sft])
                    vtt(dst[:, :, sft:8], src[:, :, sft:8], src[:, :, 0:8 - sft], ALU.add)
                    src, dst = dst, (cv if dst is cu else cu)
                V(lambda e: e.tensor_reduce(s1, gt_, AX.X, ALU.add))
                for t in range(2):
                    vts(src[:, t, :], src[:, t, :], s1[:, t:t + 1], 2.0, ALU.add, ALU.is_le)
                vtt(eq, eq, src, ALU.mult)
                vtt(eq, eq, gt_, ALU.add)
                vtt(ex, ex, eq, ALU.mult, c)
                V(lambda e: e.tensor_reduce(s1, ex, AX.X, ALU.add))
                recip(s1, s1)
                for t in range(2):
                    v = vts(ex[:, t, :], ex[:, t, :], s1[:, t:t + 1], None, ALU.mult)
                bank, free = PB.take()
                mm(bank[:, 0:8], C("upper"), eq[:, 0, :], True, False, v, free, skip_group_check=True)
                mm(bank[:, 8:16], C("upper"), eq[:, 1, :], False, False, skip_group_check=True)
                mm(bank[:, 8:16], C("ones"), eq[:, 0, :], False, False, skip_group_check=True)
                mm(bank[:, 16:24], C("ones"), eq[:, 0, :], False, False, skip_group_check=True)
                tok = mm(bank[:, 16:24], C("ones"), eq[:, 1, :], False, True, skip_group_check=True)
                pos = sm[:, 200:216].rearrange("p (t n) -> p t n", t=2)
                vtt(pos, bank[:, 0:16].rearrange("p (t n) -> p t n", t=2), eq, ALU.mult, tok)
                vts(pos, pos, -1.0, None, ALU.add)
                counts = bank[:, 16:24]
                V(lambda e: e.tensor_reduce(s1[:, 0:1], counts, AX.X, ALU.max))
                flag = sb_flag
                flag_ready = vts(flag[:, :], s1[:, 0:1], 128.5, None, ALU.is_gt)
                PB.give(bank, flag_ready)
                for k in range(KT):
                    r_ready[k] = vts(r3[:, k, NM:T2], hX[:, k, NM:T2], ALPHA, None, ALU.mult, None, x_ready[k],
                                     free=True)
                pools = [(PB, 8), (tmp, 4), (tmp2, 2)]

                def meet(tokens):
                    for q in (P, V, A):
                        q.ops.append((None, list(tokens), Token(None, 0), 0))
                    for pool, n in pools:
                        pool.all_free(n)

                meet([P.last, V.last, A.last, flag_ready])
                top = {q: (q.ops, q.branch(flag[0:1, 0:1], [flag_ready])) for q in (P, V, A)}

                for q, (_, b) in top.items():
                    q.ops, q.last = b.taken, None
                bank, free = PB.take()
                for t in range(2):
                    tok = tr(bank[0:8, 128 * t:128 * t + 128], ex[:, t, :], 128)
                gT = sq[0:8, 0:S]
                v = vcopy(gT, bank[0:8, 0:S], tok)
                PB.give(bank, v)
                for h in range(NE):
                    bank, free = PB.take()
                    tok = mm(bank[:, 0:S], C("ident", h, 1, 8).to_broadcast([8, 128]), gT, True, True, v, free)
                    gt_ready = act(gts[:, h, :], bank[:, 0:S], ACT.Copy, tok, free=True)
                    PB.give(bank, gt_ready)
                S_.limit = moe_end
                for e_ in range(NE):
                    h_ready = {}
                    free_ff = [P.last]

                    def pair(j, ba, ta, bb, tb_):
                        s_, tf = tmp.take()
                        c = act(s_[:, 0:S], ba[:, 0:S], ACT.Silu, ta, tf, free=True)
                        PB.give(ba, c)
                        yield
                        v = vtt(s_[:, 0:S], s_[:, 0:S], bb[:, 0:S], ALU.mult, c, tb_, free=True)
                        PB.give(bb, v)
                        yield
                        v = vtt(s_[:, 0:S], s_[:, 0:S], gts[:, e_, :], ALU.mult, gt_ready)
                        h_ready[j] = parts(hH[:, j, NM:T2], hL[:, j, NM:T2], s_[:, 0:S], v, free_ff)
                        tmp.give(s_, h_ready[j])

                    ffn_in([], NM, T2, pair)
                    bk = [PB.take() for _ in range(4)]
                    for c in range(FT // 2):
                        ch = S_.take(2, 1024)
                        for g in range(KT):
                            bank, free = bk[g // 2]
                            tok = group(bank[:, 256 * (g % 2):256 * (g % 2) + 256], NM, T2, ch, 128 * g, 2 * c, 2,
                                        hp, c == 0 and g % 2 == 0, c == FT // 2 - 1,
                                        [free, ch.ready, h_ready[2 * c], h_ready[2 * c + 1]],
                                        dict(skip_group_check=True))
                        ch.done(tok)
                    for g in range(KT):
                        v = vtt(r3[:, g, NM:T2], r3[:, g, NM:T2],
                                bk[g // 2][0][:, 256 * (g % 2):256 * (g % 2) + 256], ALU.add, tok)
                        if g % 2:
                            PB.give(bk[g // 2][0], v)
                dense_end = [P.last, V.last, A.last]
                meet([])
                for q, (ops, b) in top.items():
                    q.ops, q.last = b.other, None
                S_.c = S_.ahead = moe_at

                xt3 = sq[:, 0:2048].rearrange("p (t n) -> p t n", t=2)
                for t, (t0, t1) in enumerate([A_, B_]):
                    for half in range(2):
                        bank, free = PB.take()
                        for i in range(4):
                            tok = tr(bank[:, 128 * i:128 * i + 128], hX[:, 4 * half + i, t0:t1], 128, free)
                        xt_ready = act(xt3[:, t, 512 * half:512 * half + 512], bank[:, :], ACT.Copy, tok)
                        PB.give(bank, xt_ready)
                ym = mX[:, :, :].rearrange("p k t -> p (k t)")
                gs = sm[:, 312:320]
                st = {}

                def gather(e_):
                    Pe = Pg[:, e_ % 2, :, :]
                    for t in range(2):
                        v = vts(Pe[:, t, :], C("iota"), pos[:, t, e_:e_ + 1], None, ALU.is_equal, None,
                                st.get(("gathered", e_ - 2)))
                    yield
                    bks = [PB.take() for _ in range(2)]
                    for g in range(KT):
                        bank, free = bks[g // 4]
                        for t in range(2):
                            tok = mm(bank[:, 128 * (g % 4):128 * (g % 4) + 128], xt3[:, t, 128 * g:128 * g + 128],
                                     Pe[:, t, :], g % 4 == 0 and t == 0, t == 1, v, free, xt_ready,
                                     skip_group_check=True)
                        if g % 4 == 3:
                            x = bank[:, :].rearrange("p (k n) -> p k n", k=4)
                            w = [slice(g - 3, g + 1)]
                            r = parts(xgH[:, g - 3:g + 1, :], xgL[:, g - 3:g + 1, :], x, tok, st.get("in_done"))
                            PB.give(bank, r)
                            st["xg", g // 4] = r
                            yield
                    bank, free = PB.take()
                    for t in range(2):
                        tok = tr(bank[:, 128 * t:128 * t + 128], Pe[:, t, :], 128, free)
                    for t in range(2):
                        tok = mm(bank[:, 256:257], Pe[:, t, :], ex[:, t, e_:e_ + 1], t == 0, t == 1,
                                 skip_group_check=True)
                    st["gathered", e_] = tok
                    st["pt", e_] = act(Pt[:, e_ % 2, :], bank[:, 0:256], ACT.Copy, tok, st.get("spread_done"),
                                       free=True)
                    c = act(gs[:, e_ % 2:e_ % 2 + 1], bank[:, 256:257], ACT.Copy, free=True)
                    st["gs", e_] = c
                    PB.give(bank, c)

                def up_unit(u):
                    bank, free = PB.take()
                    for z in range(2):
                        ch = S_.take(4, 512)
                        for k in range(4):
                            kk_ = 4 * z + k
                            lh, ll = xgH[:, kk_, :], xgL[:, kk_, :]
                            w = [free, ch.ready, st["xg", z]] if k == 0 else None
                            mm(bank[:, :], lh, ch.h[:, k, :], kk_ == 0, False, w)
                            mm(bank[:, :], lh, ch.l[:, k, :], False, False)
                            tok = mm(bank[:, :], ll, ch.h[:, k, :], False, kk_ == KT - 1)
                        ch.done(tok)
                    s_, tf = tmp.take()
                    c = act(s_[:, 0:256], bank[:, 0:256], ACT.Silu, tok, tf, free=True)
                    v = vtt(s_[:, 0:256], s_[:, 0:256], bank[:, 256:512], ALU.mult, c, free=True)
                    PB.give(bank, v)
                    st["s", u] = (s_, v)
                    return tok

                def turn(u):
                    s_, v = st["s", u]
                    bank, free = PB.take()
                    for i in range(2):
                        tok = tr(bank[:, 128 * i:128 * i + 128], s_[:, 128 * i:128 * i + 128], 128, free, v)
                    tmp.give(s_, tok)
                    x = bank[:, 0:256].rearrange("p (k n) -> p k n", k=2)
                    st["h", u] = parts(hgH[:, 2 * u:2 * u + 2, :], hgL[:, 2 * u:2 * u + 2, :], x, tok,
                                       st.get("down_done"))
                    PB.give(bank, st["h", u])

                def down_all(e_):
                    bks = [PB.take() for _ in range(2)]
                    ahead = gather(e_ + 1) if e_ + 1 < NE else iter(())
                    for c in range(FT // 2):
                        ch = S_.take(2, 1024)
                        if c == 0:
                            next(ahead, None)
                        for k in range(2):
                            kk_ = 2 * c + k
                            for p_, (lh, ws) in enumerate(((hgH, (ch.h, ch.l)), (hgL, (ch.h,)))):
                                for w in ws:
                                    for half in range(2):
                                        bank, free = bks[half]
                                        tok = mm(bank[:, :], lh[:, kk_, :], w[:, k, 512 * half:512 * half + 512],
                                                 kk_ == 0 and p_ == 0 and w is ch.h,
                                                 kk_ == FT - 1 and p_ == 1, [free, ch.ready, st["h", c]])
                        ch.done(tok)
                        if c == 0:
                            turn(FT // 2 - 1)
                        else:
                            next(ahead, None)
                    st["down_done"] = tok
                    for half in range(2):
                        v = act(ym[:, 512 * half:512 * half + 512], bks[half][0][:, :], ACT.Copy, tok,
                                st["gs", e_], st.get("spread_done"), free=True,
                                scale=gs[:, e_ % 2:e_ % 2 + 1])
                        PB.give(bks[half][0], v)
                        st["y", half] = v

                def spread_all(e_):
                    for g in range(KT):
                        bank, free = PB.take()
                        tok = mm(bank[:, 0:S], ym[:, 128 * g:128 * g + 128], Pt[:, e_ % 2, :], True, True,
                                 free, st["y", g // 4], st["pt", e_])
                        v = vtt(r3[:, g, NM:T2], r3[:, g, NM:T2], bank[:, 0:S], ALU.add, tok, free=g > 0)
                        PB.give(bank, v)
                    st["spread_done"] = tok

                for _ in gather(0):
                    pass
                for e_ in range(NE):
                    for u in range(FT // 2):
                        st["in_done"] = up_unit(u)
                        if u >= 1:
                            turn(u - 1)
                        if u == 1 and e_ > 0:
                            spread_all(e_ - 1)
                    down_all(e_)
                spread_all(NE - 1)

                meet([])
                for q, (ops, b) in top.items():
                    q.ops, q.last = ops, b.join
                meet([b.join for _, b in top.values()] + [Token(s_raw, moe_end), Token(s_used, moe_end)])
                S_.limit = len(plan)
                r_ready = [[]] * KT
                x_ready = layer_norm("ln_ffn_g", "ln_ffn_b", layer, r_ready, split=False)

        h_rdy = [list(flat([x_ready[k], inputs])) for k in range(KT)]
        tiles = [M_, A_, B_]
        for layer in range(2):
            n_ready = rms_norm("norm_mix", layer, h_rdy)
            free_w = [P.last, V.last, A.last]
            o = 0

            def area(n):
                nonlocal o
                if o < FT * T2 and o + n > FT * T2:
                    o = FT * T2
                r = W1[:, o:o + n] if o < FT * T2 else W2[:, o - FT * T2:o - FT * T2 + n]
                o += n
                return r

            qkv = area(12 * T2).rearrange("p (k t) -> p k t", t=T2)
            zz = area(4 * T2).rearrange("p (k t) -> p k t", t=T2)
            qb = area(4 * T2).rearrange("p (k t) -> p k t", t=T2)
            kik = area(2 * T2).rearrange("p (k t) -> p k t", t=T2)
            kb_, ik = kik[:, 0, :], kik[:, 1, :]
            iq = mX[:, 4:8, :]
            oA = mX[:, 0:4, :]
            vv = TM[:, 6:8, :].rearrange("p a t -> p (a t)")[:, 0:384].rearrange("p (t n) -> p t n", t=3)
            w_extra = area(512)
            score, work = area(S), area(S)
            smk = area(2 * T2).rearrange("p (a n) -> p a n", a=2)
            sc2 = Slots([area(T2) for _ in range(3)])
            pt2 = Slots([area(384) for _ in range(2)])
            gate = W2[:, NW2 - 16 * T2:NW2].rearrange("p (k t) -> p k t", t=T2)
            assert o <= FT * T2 + NW2 - 16 * T2
            four = lambda x: x.rearrange("p (h n) -> p h n", h=4)
            set_a = [four(rX[:, 512 * i:512 * i + 512]) for i in range(4)] + \
                [four(sq[:, 512 * i:512 * i + 512]) for i in range(4)] + [four(kv1[:, 0:512])]
            set_b = [four(W2[:, NW2 - 512 * (i + 1):NW2 - 512 * i]) for i in range(8)] + [four(w_extra)]
            St = four(kv1[:, 512:1024])
            done = {}

            def until(key):
                while key not in done:
                    yield

            def conv(key, ps, tk):
                dst = qkv[:, key, :]
                cw = lambda i: C("conv_a", (layer * 12 + key) * 4 + i, 1)
                v = act(dst, ps, ACT.Copy, tk, free_w, free=True, scale=cw(3))
                for i in (2, 1, 0):
                    d = 3 - i
                    v = stt(dst[:, d:T2], ps[:, 0:T2 - d], cw(i), dst[:, d:T2], ALU.mult, ALU.add, v, free=True)
                last = v
                for x, v in silus:
                    act(x, x, ACT.Silu, v, free=True)
                silus[:] = [(dst, last)]
                return last

            silus = []
            sml = sm[:, 320:368].rearrange("p (t n) -> p t n", t=3)
            V(lambda e: e.memset(sml[:, 0, :], 0.0))

            def bv(i, ps, tk):
                vcopy(sml[0:ps.shape[0], i, :], ps[:, 128:144], tk, free_w)
                return vcopy(vv[0:ps.shape[0], i, :], ps[:, 0:128], tk, free_w)

            rows(256, n_, tiles, n_ready, bv)
            sml_ready = V.last

            def raw(dst):
                return lambda key, ps, tk: act(dst[:, key, :], ps, ACT.Copy, tk, free_w, free=True)

            def projections():
                for c in range(6):
                    yield from product_steps([2 * c, 2 * c + 1], n_, 0, T2, None, conv)
                    if c in (3, 5):
                        yield
                        for x, v in silus:
                            act(x, x, ACT.Silu, v, free=True)
                        silus.clear()
                        done["conv", c] = A.last
                yield from product_steps([0, 1], n_, 0, T2, None, raw(kik))
                for c in range(2):
                    yield from product_steps([2 * c, 2 * c + 1], n_, 0, T2, None, raw(qb))
                for c in range(2):
                    yield from product_steps([2 * c, 2 * c + 1], n_, 0, T2, None, raw(iq))
                done["attention"] = A.last
                for c in range(2):
                    yield from product_steps([2 * c, 2 * c + 1], n_, 0, T2, None, raw(zz))
                done["z"] = act(zz, zz, ACT.Silu)
                yield from until(("o", 2))
                free_g = [P.last, V.last, A.last, G.last]

                def biased(key, ps, tk):
                    return vts(gate[:, key, :], ps, C("b_gate", 16 * layer + key, 1), None, ALU.add, None, tk,
                               free_g, free=True)

                for c in range(8):
                    yield from product_steps([2 * c, 2 * c + 1], n_, 0, T2, None, biased)
                v = V.last
                for z in range(2):
                    done["gate"] = act(gate[:, 8 * z:8 * z + 8, :], gate[:, 8 * z:8 * z + 8, :], ACT.Sigmoid, v,
                                       free=True)

            gb = sm[:, 368:380].rearrange("p (t n) -> p t n", t=3)
            be = sm[:, 380:392].rearrange("p (t n) -> p t n", t=3)
            sa = sm[:, 392:404].rearrange("p (t n) -> p t n", t=3)
            gc = sm[:, 404:416].rearrange("p (t n) -> p t n", t=3)
            ge = sm[:, 416:428].rearrange("p (t n) -> p t n", t=3)
            gl = sm[:, 428:440].rearrange("p (t n) -> p t n", t=3)
            gk = sm[:, 440:452].rearrange("p (t n) -> p t n", t=3)
            ea = sm[:, 452:456]
            per_tile = lambda x: x.unsqueeze(1).to_broadcast([128, 3, 4])

            def col_stats(src, n, scale, eps, after):
                bank, free = PB.take()
                for i in range(n):
                    s_, tf = tmp.take()
                    c = act(s_, src(i), ACT.Square, tf, after, free=True)
                    m = mm(bank[0:n, 0:T2], C("colsel", 7 - i, n), s_, i == 0, i == n - 1, c,
                           free if i == 0 else None)
                    tmp.give(s_, m)
                    if i % 2:
                        yield
                rt, rf = tmp2.take()
                c = act(rt[0:n, :], bank[0:n, 0:T2], ACT.Sqrt, m, rf, scale=scale, bias=eps[0:n, :])
                PB.give(bank, c)
                yield
                v = recip(rt[0:n, :], rt[0:n, :], c)
                yield
                return rt, v

            def spread(rt, n, i, after):
                bank, free = PB.take()
                m = mm(bank[:, 0:T2], C("ident", i, 1, n).to_broadcast([n, 128]), rt[0:n, :], True, True, after,
                       free)
                return bank, m

            def scalars():
                c = act(ea, C("a_log", 4 * layer, 4), ACT.Exp)
                v = vtt(gb, sml[:, :, 0:4], per_tile(C("dt_bias", 4 * layer, 4)), ALU.add)
                act(be, sml[:, :, 4:8], ACT.Exp, sml_ready, scale=-1.0, free=True)
                act(sa, gb, ACT.Abs, v, free=True)
                act(sa, sa, ACT.Exp, scale=-1.0)
                c = act(sa, sa, ACT.Ln, bias=1.0)
                yield
                vts(be, be, 1.0, None, ALU.add, None, c)
                recip(be, be)
                stt(gb, gb, 0.0, sa, ALU.max, ALU.add, c, free=True)
                v = stt(gb, gb, -1.0, per_tile(ea), ALU.mult, ALU.mult)
                yield
                bank, free = PB.take()
                b3 = bank[:, 0:96].rearrange("p (t n) -> p t n", t=3)
                for i, t in enumerate((1, 2, 0)):
                    n = tiles[t][1] - tiles[t][0]
                    mm(b3[:, t, 16:20], C("ones", 0, 128, n), gb[0:n, t, :], i == 0, False, v, free,
                       skip_group_check=True)
                    tok = mm(b3[:, t, 0:4], C("upper", 0, 128, n), gb[0:n, t, :], False, i == 2,
                             skip_group_check=True)
                yield
                v = vcopy(gc, b3[:, :, 0:4], tok)
                v = vtt(gk, b3[:, :, 16:20], gc, ALU.subtract)
                c = act(gl, b3[:, :, 16:20], ACT.Exp, v)
                PB.give(bank, v, c)
                act(gk, gk, ACT.Exp, free=True)
                c = act(ge, gc, ACT.Exp, free=True)
                done["scalars"] = [c, vtt(ge, ge, be, ALU.mult, c)]
                yield

            def normed():
                yield from until(("conv", 3))
                rt, v = yield from col_stats(lambda i: qkv[:, i, :], 8, 1.0, C("eps6"), done["conv", 3])
                for i in range(8):
                    bank, m = spread(rt, 8, i, v)
                    s = BSCALE if i < 4 else 1.0
                    v2 = stt(qkv[:, i, :], qkv[:, i, :], s, bank[:, 0:T2], ALU.mult, ALU.mult, m, free=True)
                    PB.give(bank, v2)
                    if i % 2:
                        yield
                tmp2.give(rt, P.last)
                done["qk"] = v2

            def inverse(t, names):
                t0, t1 = tiles[t]
                n = t1 - t0
                Gd, EG, Mm, DT, MT, X, XT, Yb, CT = names
                start = [P.last, G.last]
                for h in range(4):
                    v = vts(Gd[0:n, h, 0:n], C("upper", 0, n, n), gb[0:n, t, h:h + 1], None, ALU.mult, None,
                            start, free=h > 0)
                yield
                bank, free = PB.take()
                g3 = four(bank[:, :])
                for h in range(4):
                    tok = mm(g3[:, h, 0:n], C("ones", 0, 128, n), Gd[0:n, h, 0:n], h == 0, h == 3, v, free,
                             skip_group_check=True)
                bank2, free = PB.take()
                k3 = four(bank2[:, :])
                for h in range(4):
                    tk = mm(k3[0:n, h, 0:n], qkv[:, 4 + h, t0:t1], qkv[:, 4 + h, t0:t1], h == 0, h == 3, free,
                            done["qk"], skip_group_check=True)
                yield
                for h in range(4):
                    stt(Mm[0:n, h, 0:n], g3[0:n, h, 0:n], gc[0:n, t, h:h + 1], C("um", 0, n, n), ALU.subtract,
                        ALU.add, tok, free=h > 0)
                    v = stt(DT[0:n, h, 0:n], g3[0:n, h, 0:n], gc[0:n, t, h:h + 1], C("umt", 0, n, n),
                            ALU.subtract, ALU.add, free=True)
                act(Mm[0:n, :, 0:n], Mm[0:n, :, 0:n], ACT.Exp, v, start, free=True, scale=-1.0)
                c1 = act(EG[:, :, 0:n], g3[:, :, 0:n], ACT.Exp, v, start, free=True)
                PB.give(bank, c1)
                c = act(DT[0:n, :, 0:n], DT[0:n, :, 0:n], ACT.Exp, free=True)
                yield
                for h in range(4):
                    v = stt(Mm[0:n, h, 0:n], k3[0:n, h, 0:n], be[0:n, t, h:h + 1], Mm[0:n, h, 0:n], ALU.mult,
                            ALU.mult, tk, c, free=h > 0)
                PB.give(bank2, v)
                yield
                bank, free = PB.take()
                m3 = four(bank[:, :])
                for h in range(4):
                    tok = tr(m3[0:n, h, 0:n], Mm[0:n, h, 0:n], n, v, free)
                yield
                c = act(MT[0:n, :, 0:n], m3[0:n, :, 0:n], ACT.Copy, tok)
                PB.give(bank, c)
                lb = lambda nm, l: C(nm, 128 * l, n, n).unsqueeze(1).to_broadcast([n, 4, n])
                ib = C("ident", 0, n, n).unsqueeze(1).to_broadcast([n, 4, n])
                vtt(X[0:n, :, 0:n], Mm[0:n, :, 0:n], lb("lm", 0), ALU.mult)
                vtt(X[0:n, :, 0:n], ib, X[0:n, :, 0:n], ALU.subtract)
                vtt(XT[0:n, :, 0:n], MT[0:n, :, 0:n], lb("lmt", 0), ALU.mult, c)
                x_tok = vtt(XT[0:n, :, 0:n], ib, XT[0:n, :, 0:n], ALU.subtract)
                yield
                levels = 7 if n == 128 else 4
                ct_read = start
                for l in range(1, levels):
                    gct = vtt(CT[0:n, :, 0:n], MT[0:n, :, 0:n], lb("lmt", l), ALU.mult, c, ct_read, q=G)
                    bank, free = PB.take()
                    b3 = four(bank[:, :])
                    for h in range(4):
                        tok = mm(b3[0:n, h, 0:n], CT[0:n, h, 0:n], X[0:n, h, 0:n], h == 0, h == 3, gct, x_tok,
                                 free, skip_group_check=True)
                    ct_read = tok
                    yield
                    cy = act(Yb[0:n, :, 0:n], b3[0:n, :, 0:n], ACT.Copy, tok)
                    PB.give(bank, cy)
                    yield
                    bank2, free2 = PB.take()
                    b4 = four(bank2[:, :])
                    for h in range(4):
                        tok2 = mm(b4[0:n, h, 0:n], Yb[0:n, h, 0:n], XT[0:n, h, 0:n], h == 0, h == 3, cy, free2,
                                  skip_group_check=True)
                    if l < levels - 1:
                        bank, free = PB.take()
                        b5 = four(bank[:, :])
                        for h in range(4):
                            tok = mm(b5[0:n, h, 0:n], XT[0:n, h, 0:n], Yb[0:n, h, 0:n], h == 0, h == 3, cy,
                                     free, skip_group_check=True)
                        yield
                        v = vtt(X[0:n, :, 0:n], X[0:n, :, 0:n], b5[0:n, :, 0:n], ALU.subtract, tok)
                        PB.give(bank, v)
                        tok2 = [tok2, tok]
                    else:
                        yield
                    x_tok = vtt(XT[0:n, :, 0:n], XT[0:n, :, 0:n], b4[0:n, :, 0:n], ALU.subtract, tok2)
                    PB.give(bank2, x_tok)
                    yield
                done["inverse", t] = [x_tok, c1]

            def values(t, names):
                t0, t1 = tiles[t]
                n = t1 - t0
                wT, qe, kd, QK, u, _, XT, kb, vb = names
                yield from until(("conv", 5))
                read = P.last
                for which in (8, 4):
                    bank, free = PB.take()
                    b3 = four(bank[:, :])
                    for h in range(4):
                        tok = tr(b3[0:n, h, :], qkv[:, which + h, t0:t1], 128, free, done["conv", 5])
                    yield
                    for h in range(4):
                        if which == 8:
                            v = vts(vb[0:n, h, :], b3[0:n, h, :], be[0:n, t, h:h + 1], None, ALU.mult, None, tok,
                                    read, free=h > 0)
                        else:
                            vts(kb[0:n, h, :], b3[0:n, h, :], ge[0:n, t, h:h + 1], None, ALU.mult, None, tok,
                                read, free=True)
                            v = vts(kd[0:n, h, :], b3[0:n, h, :], gk[0:n, t, h:h + 1], None, ALU.mult, None,
                                    free=True)
                    PB.give(bank, v)
                v = vtt(qe[:, :, 0:n], qkv[:, 0:4, t0:t1], qe[:, :, 0:n], ALU.mult, done["inverse", t], free=True)
                yield
                bank, free = PB.take()
                q3_ = four(bank[:, :])
                for h in range(4):
                    tok = mm(q3_[0:n, h, 0:n], qkv[:, 4 + h, t0:t1], qkv[:, h, t0:t1], h == 0, h == 3, free,
                             skip_group_check=True)
                yield
                v2 = vtt(QK[0:n, :, 0:n], q3_[0:n, :, 0:n], QK[0:n, :, 0:n], ALU.mult, tok)
                PB.give(bank, v2)
                bank, free = PB.take()
                u3 = four(bank[:, :])
                for h in range(4):
                    tok = mm(u3[0:n, h, :], XT[0:n, h, 0:n], vb[0:n, h, :], h == 0, h == 3, v, free,
                             skip_group_check=True)
                c = act(u[0:n, :, :], u3[0:n, :, :], ACT.Copy, tok)
                PB.give(bank, c)
                if t > 0:
                    bank, free = PB.take()
                    w3 = four(bank[:, :])
                    for h in range(4):
                        tok = mm(w3[:, h, 0:n], kb[0:n, h, :], XT[0:n, h, 0:n], h == 0, h == 3, free,
                                 skip_group_check=True)
                    c = act(wT[:, :, 0:n], w3[:, :, 0:n], ACT.Copy, tok)
                    PB.give(bank, c)
                done["values", t] = [v2, c]
                yield

            def advance(t, names):
                t0, t1 = tiles[t]
                n = t1 - t0
                wT, qe, kd, QK, u, _, XT, kb, vb = names
                v = done["values", t]
                if t > 0:
                    bank, free = PB.take()
                    s3 = four(bank[:, :])
                    for h in range(4):
                        tok = mm(s3[0:n, h, :], wT[:, h, 0:n], St[:, h, :], h == 0, h == 3, free, v,
                                 done["state", t - 1], skip_group_check=True)
                    yield
                    v = vtt(u[0:n, :, :], u[0:n, :, :], s3[0:n, :, :], ALU.subtract, tok)
                    PB.give(bank, v)
                    yield
                bank, free = PB.take()
                o3 = four(bank[:, :])
                for h in range(4):
                    if t > 0:
                        mm(o3[:, h, 0:n], St[:, h, :], qe[:, h, 0:n], h == 0, False, free, v,
                           skip_group_check=True)
                    tok_o = mm(o3[:, h, 0:n], u[0:n, h, :], QK[0:n, h, 0:n], t == 0 and h == 0, h == 3, free, v,
                               skip_group_check=True)
                if t < 2:
                    bank2, free = PB.take()
                    d3 = four(bank2[:, :])
                    for h in range(4):
                        tok = mm(d3[:, h, :], kd[0:n, h, :], u[0:n, h, :], h == 0, h == 3, free,
                                 skip_group_check=True)
                    yield
                    for h in range(4):
                        if t == 0:
                            v = vcopy(St[:, h, :], d3[:, h, :], tok, free=h > 0)
                        else:
                            v = stt(St[:, h, :], St[:, h, :], gl[:, t, h:h + 1], d3[:, h, :], ALU.mult,
                                    ALU.add, tok, free=h > 0)
                    PB.give(bank2, v)
                    done["state", t] = v
                done["o", t] = vcopy(oA[:, :, t0:t1], o3[:, :, 0:n], tok_o)
                PB.give(bank, done["o", t])
                yield

            def delta_a():
                yield from scalars()
                yield from normed()
                for t in (0, 1):
                    yield from inverse(t, set_a)
                    yield from values(t, set_a)
                    yield from advance(t, set_a)

            def delta_b():
                yield from until("qk")
                yield from inverse(2, set_b)
                yield from values(2, set_b)
                yield from until(("o", 1))
                yield from advance(2, set_b)
                rt, v = yield from col_stats(lambda i: oA[:, i, :], 4, 1.0 / 128, C("eps6"), V.last)
                for i in range(4):
                    bank, m = spread(rt, 4, i, v)
                    v2 = stt(oA[:, i, :], oA[:, i, :], C("a_out_norm", layer, 1), bank[:, 0:T2], ALU.mult,
                             ALU.mult, m, free=True)
                    PB.give(bank, v2)
                tmp2.give(rt, P.last)
                done["oa"] = vtt(oA, oA, zz, ALU.mult, done["z"])

            def rope2(src, rot, cos, sin, after):
                bank, free = PB.take()
                m = mm(bank[:, 0:T2], C(rot), src, True, True, after, free)
                yield
                t2, tf = tmp.take()
                v = vtt(t2, bank[:, 0:T2], C(sin), ALU.mult, m, tf, free=True)
                PB.give(bank, v)
                vtt(src, src, C(cos), ALU.mult, m, free=True)
                v = vtt(src, src, t2, ALU.add)
                tmp.give(t2, v)
                return v

            def attention():
                yield from until("attention")
                raws = done["attention"]
                s_, tf = tmp.take()
                c = act(s_, ik, ACT.Square, tf, raws)
                bank, free = PB.take()
                m = mm(bank[:, 0:T2], C("mean64"), s_, True, True, c, free)
                c = act(s_, bank[:, 0:T2], ACT.Sqrt, m, bias=C("eps6"))
                PB.give(bank, c)
                yield
                recip(s_, s_, c)
                v = stt(ik, ik, C("kidx", layer, 1), s_, ALU.mult, ALU.mult)
                tmp.give(s_, v)
                yield
                roped_i = [(yield from rope2(ik, "roti", "cosi", "sini", v))]
                for i in range(4):
                    roped_i.append((yield from rope2(iq[:, i, :], "roti", "cosi", "sini", raws)))
                IS = float(8 ** -0.5 * 64 ** -0.5)
                iwt = sm[:, 456:472].rearrange("p (t n) -> p t n", t=2)
                vts(iwt, sml[:, 1:3, 8:16], IS, None, ALU.mult)
                for t in (1, 2):
                    t0, t1 = tiles[t]
                    for q_ in range(2):
                        bks = [PB.take() for _ in range(2)]
                        toks = []
                        for h in range(4 * q_, 4 * q_ + 4):
                            p0 = 64 * (h % 2)
                            bank, free = bks[h % 2]
                            cc = 256 * ((h // 2) % 2)
                            toks.append(mm(bank[:, cc:cc + 256], iq[p0:p0 + 64, h // 2, t0:t1],
                                           ik[p0:p0 + 64, NM:T2], (h // 2) % 2 == 0, (h // 2) % 2 == 1, free,
                                           roped_i, skip_group_check=True))
                        yield
                        for h in range(4 * q_, 4 * q_ + 4):
                            cc = 256 * ((h // 2) % 2)
                            src = bks[h % 2][0][:, cc:cc + 256]
                            s_, tf = tmp.take()
                            c = act(s_[:, 0:S], src, ACT.Relu, toks, tf, free=True)
                            w_ = iwt[:, t - 1, h:h + 1]
                            if h == 0:
                                v = vts(score, s_[:, 0:S], w_, None, ALU.mult, None, c, free_w)
                            else:
                                v = stt(score, s_[:, 0:S], w_, score, ALU.mult, ALU.add, c)
                            tmp.give(s_, v)
                        for bank, _ in bks:
                            PB.give(bank, c)
                        yield
                    vtt(score, score, C("valid", 256 * (t - 1), 256), ALU.add)
                    cur = score
                    mx8 = sm[:, 472:480]
                    keep = smk[:, t - 1, NM:T2]
                    for r in range(8):
                        nxt = work if r % 2 else keep
                        V(lambda e, cur=cur: e.max(mx8, cur))
                        V(lambda e, cur=cur, nxt=nxt: e.match_replace(nxt, mx8, cur, -3e38))
                        cur = nxt
                        yield
                    V(lambda e, t=t: e.memset(smk[:, t - 1, 0:NM], 0.0))
                    vtt(keep, cur, score, ALU.is_equal)
                    sel = vts(keep, keep, -BIG, None, ALU.mult)
                    if t == 1:
                        rt, v = yield from col_stats(lambda i: qb[:, i, :] if i < 4 else kb_, 5, 1.0 / 128,
                                                     C("eps6"), raws)
                        for i in range(5):
                            dst = qb[:, i, :] if i < 4 else kb_
                            bank, m = spread(rt, 5, i, v)
                            v2 = stt(dst, dst, C("q_norm" if i < 4 else "k_norm", layer, 1), bank[:, 0:T2],
                                     ALU.mult, ALU.mult, m, free=True)
                            PB.give(bank, v2)
                        tmp2.give(rt, P.last)
                        yield
                        for i in range(4):
                            yield from rope2(qb[:, i, :], "rota", "cosa", "sina", v2)
                        roped2 = yield from rope2(kb_, "rota", "cosa", "sina", v2)

                units = [(h, t) for t in (1, 2) for h in range(4)] + [(h, 0) for h in range(4)]
                st = {}
                n_u = len(units)
                for i in range(n_u + 2):
                    if i < n_u:
                        h, t = units[i]
                        t0, t1 = tiles[t]
                        n = t1 - t0
                        nk = T2 if t else NM
                        bank, free = PB.take()
                        tok = mm(bank[0:n, 0:nk], qb[:, h, t0:t1], kb_[:, 0:nk], True, True, free, roped2)
                        sc, f = sc2.take()
                        s2, f2 = st_slots.take()
                        if t:
                            v = stt(sc[0:n, 0:nk], bank[0:n, 0:nk], BSCALE, smk[0:n, t - 1, :], ALU.mult,
                                    ALU.add, tok, f, sel, free_w)
                        else:
                            v = vts(sc[0:n, 0:nk], bank[0:n, 0:nk], BSCALE, None, ALU.mult, None, tok, f, free_w)
                        PB.give(bank, v)
                        v = V(lambda e, a_=s2[0:n, 0:1], b_=sc[0:n, 0:nk]: e.tensor_reduce(
                            a_, b_, AX.X, ALU.max, negate=True), f2)
                        c = act(sc[0:n, 0:nk], sc[0:n, 0:nk], ACT.Exp, v, free=True, bias=s2[0:n, 0:1],
                                accum_out=s2[0:n, 1:2])
                        yield
                        recip(s2[0:n, 1:2], s2[0:n, 1:2], c)
                        v = vts(sc[0:n, 0:nk], sc[0:n, 0:nk], s2[0:n, 1:2], None, ALU.mult)
                        st_slots.give(s2, v)
                        st[i] = (sc, v)
                    if 1 <= i <= n_u:
                        h, t = units[i - 1]
                        t0, t1 = tiles[t]
                        n = t1 - t0
                        sc, v = st[i - 1]
                        bank, free = PB.take()
                        pt, f = pt2.take()
                        for j, (k0, k1) in enumerate(tiles if t else tiles[:1]):
                            tok = tr(bank[0:k1 - k0, 128 * j:128 * j + n], sc[0:n, k0:k1], n,
                                     [free, v])
                        sc2.give(sc, tok)
                        c = act(pt[0:NM, 0:n], bank[0:NM, 0:n], ACT.Copy, tok, f, free_w, free=True)
                        if t:
                            c = act(pt[:, 128:384], bank[:, 128:384], ACT.Copy, tok, free=True)
                        PB.give(bank, c)
                        st[i - 1] = (pt, c)
                    if i >= 2:
                        h, t = units[i - 2]
                        t0, t1 = tiles[t]
                        n = t1 - t0
                        pt, c = st[i - 2]
                        bank, free = PB.take()
                        kts = tiles if t else tiles[:1]
                        for j, (k0, k1) in enumerate(kts):
                            tok = mm(bank[:, 0:n], vv[0:k1 - k0, j, :], pt[0:k1 - k0, 128 * j:128 * j + n],
                                     j == 0, j == len(kts) - 1, free, c)
                        pt2.give(pt, tok)
                        v = vcopy(mX[:, 4 + h, t0:t1], bank[:, 0:n], tok, free=True)
                        PB.give(bank, v)
                done["ob"] = V.last

            weave([projections(), delta_a(), delta_b(), attention()])

            m2 = (nH, nL)
            cut = {}
            for z, ready in ((1, done["ob"]), (0, done["oa"])):
                k4 = slice(4 * z, 4 * z + 4)
                cut[z] = parts(nH[:, k4, :], nL[:, k4, :], mX[:, k4, :], ready, P.last, V.last, G.last)
            y_ready = {}
            free_y = [P.last, V.last]
            sums = []

            def split_sums():
                for g, c in sums:
                    y_ready[g] = parts(yH[:, g, :], yL[:, g, :], gate[:, g, :], c, free_y)
                sums.clear()

            for pr in range(4):
                ch = S_.take(KT, 256)
                split_sums()
                for i in range(2):
                    g = 2 * pr + i
                    for z in (1, 0):
                        s_ = gate[:, 8 * z + g, :]
                        bank, free = PB.take()
                        for k in range(4):
                            kk_ = 4 * z + k
                            w_ = slice(128 * i, 128 * i + 128)
                            tok = mm3(bank[:, 0:T2], ch.h[:, kk_, w_], ch.l[:, kk_, w_], m2[0][:, kk_, :],
                                      m2[1][:, kk_, :], k == 0, k == 3, [free, ch.ready, cut[z]] if k == 0 else None)
                        c = vtt(s_, s_, bank[:, 0:T2], ALU.mult, done["gate"], tok, free=True)
                        PB.give(bank, c)
                    s0 = gate[:, g, :]
                    sums.append((g, vtt(s0, s0, gate[:, 8 + g, :], ALU.add, c, q=G, free=True)))
                ch.done(tok)
            split_sums()
            h_rdy = {}

            def addh(key, ps, tk):
                h_rdy[key] = vtt(hX[:, key, :], hX[:, key, :], ps, ALU.add, tk, free=True)
                return h_rdy[key]

            for c in range(4):
                product([2 * c, 2 * c + 1], (yH, yL), 0, T2, [y_ready[g] for g in range(8)], addh)
            n_ready = rms_norm("norm_ffn", layer, h_rdy)
            h_ready = {}
            free_ff = [P.last, V.last, A.last]

            def pair2(j, ba, ta, bb, tb_):
                s_, tf = tmp.take()
                cw = lambda i: C("conv_ffn", (layer * 22 + j) * 3 + i, 1)
                vts(s_, ba[:, 0:T2], cw(2), None, ALU.mult, None, ta, tf)
                stt(s_[:, 1:T2], ba[:, 0:T2 - 1], cw(1), s_[:, 1:T2], ALU.mult, ALU.add)
                v = stt(s_[:, 2:T2], ba[:, 0:T2 - 2], cw(0), s_[:, 2:T2], ALU.mult, ALU.add)
                PB.give(ba, v)
                c = act(s_, s_, ACT.Silu, v, free=True)
                yield
                v = vtt(s_, s_, bb[:, 0:T2], ALU.mult, c, tb_, free=True)
                PB.give(bb, v)
                yield
                h_ready[j] = parts(hH[:, j, :], hL[:, j, :], s_, v, free_ff)
                tmp.give(s_, h_ready[j])

            ffn_in(n_ready, 0, T2, pair2)
            ffn_out(h_ready, 0, T2, addh)

        n_out = 0
        for k in range(KT):
            n_out += 16
            last = dma(Y, a["out"][:, k, :], hX[:, k, NM:T2], s_out, n_out, h_rdy[k])
        Y.ops.append((None, [last], Token(None, 0), 0))

        number([P, V, A, G, Y])
        block = ctx.enter_context(nc.Block())

        @block.sync
        def _(eng):
            Y.emit(eng)

        @block.gpsimd
        def _(eng):
            G.emit(eng)

        @block.scalar
        def _(eng):
            A.emit(eng)

        @block.tensor
        def _(eng):
            P.emit(eng)

        @block.vector
        def _(eng):
            V.emit(eng)


def _pack(inp):
    pk = np.zeros((128, NPACK), np.float32)

    def put(name, v):
        v = np.asarray(v)
        v = v.reshape(v.shape[0], -1)
        pk[0:v.shape[0], AT[name]:AT[name] + v.shape[1]] = v

    i, j = np.arange(128)[:, None], np.arange(128)[None, :]
    put("ident", np.eye(128))
    put("ones", np.ones((128, 128)))
    put("mean", np.full((128, 128), 1 / 1024))
    put("iota", np.broadcast_to(j, (128, 128)))
    put("slot", i)
    put("mean64", np.where(i // 64 == j // 64, 1 / 64, 0))
    put("upper", i <= j)
    q = np.arange(256).reshape(2, 128).T[:, :, None]
    k = np.arange(256)[None, None, :]
    put("swa", np.where((k // 64 <= q // 64) & (k // 64 >= q // 64 - 2), 0, -BIG))
    put("causal", np.where(k <= q, 0, -BIG))
    put("valid", np.where(k < (q // 64 + 1) * 64, 0, -BIG))
    rot = np.zeros((128, 128))
    for h in range(2):
        for d in range(8):
            rot[64 * h + d + 8, 64 * h + d] = -1
            rot[64 * h + d, 64 * h + d + 8] = 1
    put("rot1", rot)
    rot = np.zeros((128, 128))
    for d in range(64):
        rot[d + 64, d] = -1
        rot[d, d + 64] = 1
    put("rota", rot)
    rot = np.zeros((128, 128))
    for h in range(2):
        for d in range(32):
            rot[64 * h + d + 32, 64 * h + d] = -1
            rot[64 * h + d, 64 * h + d + 32] = 1
    put("roti", rot)
    for nm, dim in (("a", 128), ("i", 64)):
        inv = (1.0 / (np.float32(10000.0) ** (np.arange(0, dim, 2, dtype=np.float32) / np.float32(dim)))).astype(
            np.float32)
        ang = (np.arange(T2, dtype=np.float32)[None, :] * inv[:, None]).astype(np.float32).astype(np.float64)
        ang = np.concatenate([ang] * (256 // dim))
        put("cos" + nm, np.cos(ang))
        put("sin" + nm, np.sin(ang))
    put("um", np.where(j > i, BIG, 0))
    put("umt", np.where(j < i, -BIG, 0))
    lm = np.zeros((128, 7, 128))
    for l in range(7):
        b = 1 << l
        lm[:, l] = (i // (2 * b) == j // (2 * b)) & (i // b % 2 == 1) & (j // b % 2 == 0)
    put("lm", lm)
    put("lmt", lm.transpose(2, 1, 0))
    put("colsel", np.broadcast_to(np.arange(15) == 7, (128, 15)))
    f = np.zeros((128, 1), np.float32)
    for h in range(2):
        for d in range(16):
            f[64 * h + d] = INV1[d % 8]
    put("inv1", f)
    put("eps5", np.full((128, 1), 1e-5))
    put("eps6", np.full((128, 1), 1e-6))

    def feat(x):
        x = np.asarray(x)
        return np.moveaxis(x.reshape(x.shape[:-1] + (-1, 128)), -1, 0)

    for nm in ("ln_attn_g", "ln_attn_b", "ln_ffn_g", "ln_ffn_b"):
        put(nm, feat(inp[nm]))
    put("norm_mix", feat(inp["norm_mix_2"]))
    put("norm_ffn", feat(inp["norm_ffn_2"]))

    def over(x):
        return np.broadcast_to(np.asarray(x).reshape(1, -1), (128, np.asarray(x).size))

    put("sinks", over(inp["attn_sinks"]))
    put("b_forget", over(inp["b_forget"]))
    put("b_router", over(inp["b_router"]))
    put("a_log", over(inp["a_log_2"]))
    put("dt_bias", over(inp["dt_bias_2"]))
    put("conv_a", np.asarray(inp["conv_a_2"]).reshape(2, 4, 12, 128).transpose(3, 0, 2, 1))
    put("conv_ffn", np.asarray(inp["conv_ffn_2"]).reshape(2, 3, 22, 128).transpose(3, 0, 2, 1))
    put("a_out_norm", feat(inp["a_out_norm_2"]))
    put("q_norm", feat(inp["q_norm_2"]))
    put("k_norm", feat(inp["k_norm_2"]))
    kx = np.asarray(inp["kidx_norm_2"]).T
    put("kidx", np.concatenate([kx, kx]))
    put("b_gate", feat(inp["b_gate_2"]))
    return pk


def _arrays(inp):
    c = np.ascontiguousarray
    f = lambda n: np.asarray(inp[n])

    def tokens(x):
        return c(x.reshape(x.shape[0], 8, 128).transpose(2, 1, 0))

    def down(w):
        lead = w.shape[:-2]
        w = w.reshape(lead + (2, 11, 128, 8, 128))
        n = len(lead)
        return c(w.transpose(tuple(range(n)) + (n + 3, n, n + 2, n + 1, n + 4)))

    w = f("w_in_swa")[0]
    kd = [w[:, 768 + 64 * h:832 + 64 * h] for h in range(3) for _ in range(2)]
    w_swa = np.concatenate([w[:, 0:768]] + kd + [w[:, 1152:1408], w[:, 960:1152]], axis=1)
    w2 = f("w_in_2")
    w_in_2 = np.concatenate([w2[:, :, 0:2048], w2[:, :, 2696:2824], w2[:, :, 2048:2056], w2[:, :, 3400:3408],
                             np.zeros((2, 1024, 112), np.float32), w2[:, :, 2056:2568], w2[:, :, 2824:3336],
                             w2[:, :, 2568:2696], w2[:, :, 3336:3400], w2[:, :, 3336:3400]], axis=2)

    def up(w):
        lead = w.shape[:-2]
        n = len(lead)
        w = w.reshape(lead + (2, 4, 128, 2, 11, 256))
        w = w.transpose(tuple(range(n)) + (n + 4, n, n + 2, n + 1, n + 3, n + 5))
        return c(w.reshape(lead + (11, 2, 128, 4, 512)))

    return {
        "pack": _pack(inp),
        "pos": c(np.broadcast_to(f("positions").reshape(1, S), (128, S))),
        "xT": tokens(f("x")[0]),
        "metaT": tokens(f("meta_tokens_2")),
        "memT": tokens(f("mem")[0]),
        "w_mem_kv": c(f("w_mem_kv")),
        "w_swa": c(w_swa),
        "w_fox": c(f("w_in_fox")[0][:, 0:2560]),
        "w_forget": c(f("w_in_fox")[0][:, 2560:].reshape(8, 128, 12).transpose(1, 0, 2)),
        "w_out": c(f("w_out")),
        "w_ffn_in": up(f("w_ffn_in")[0]),
        "w_ffn_out": down(f("w_ffn_out")[0]),
        "w_router": c(f("w_router")[0].reshape(8, 128, 8).transpose(1, 0, 2)),
        "w_exp_in": up(f("w_exp_in")[0]),
        "w_exp_out": c(f("w_exp_out")[0]),
        "w_in_2": c(w_in_2),
        "w_branch": np.concatenate([f("w_branch_a_2"), f("w_branch_b_2")], axis=1),
        "w_gate": c(f("w_gate_2")),
        "w_out_2": c(f("w_out_2")),
        "w_up": up(f("w_up_2")),
        "w_down": down(f("w_down_2")),
    }


def kernel(**inputs):
    import concourse.bacc as bacc
    from concourse.bass_utils import run_bass_kernel_spmd

    nc = bacc.Bacc("TRN2", target_bir_lowering=False, num_devices=1)
    arrays = _arrays(inputs)
    a = {}
    for name, x in arrays.items():
        a[name] = nc.dram_tensor(name, x.shape, mybir.dt.from_np(x.dtype), kind="ExternalInput").ap()
    a["out"] = nc.dram_tensor("out", (128, 8, S), F32, kind="ExternalOutput").ap()
    build(nc, a)
    r = run_bass_kernel_spmd(nc, [arrays], core_ids=[0])
    out = r.results[0]["out"]
    return np.ascontiguousarray(out.transpose(2, 1, 0).reshape(1, S, D))
```
